# Optimizing a Trainium2 kernel written in Bass

```python
import math
import jax, jax.numpy as jnp
from jax import lax
import numpy as np

D_MODEL = 1024
BATCH = 1
SEQ = 256
DEPTH = 1

HEAD_DIM = 64
SWA_Q_HEADS = 8
SWA_KV_HEADS = 2
SWA_GROUP = SWA_Q_HEADS // SWA_KV_HEADS
WINDOW = 128
FOX_HEADS = 4
MLA_HEADS = 4
MLA_Q_RANK = 256
MLA_KV_RANK = 128
MLA_NOPE_DIM = 64
MLA_ROPE_DIM = 32
MLA_V_DIM = 64
ROPE_THETA = 10000.0
REL_BUCKETS = 32
REL_MAX_DIST = 128
D_FF = 2816
CONV_WIDTH = 3
Q_BLOCK = 128
EPS = 1e-6
NEG_INF = -1e30

SWA_WIDTH = SWA_Q_HEADS * HEAD_DIM
FOX_WIDTH = FOX_HEADS * HEAD_DIM
MLA_WIDTH = MLA_HEADS * MLA_V_DIM
MIX_WIDTH = SWA_WIDTH + FOX_WIDTH + MLA_WIDTH
SWA_COLS = (SWA_Q_HEADS + 2 * SWA_KV_HEADS) * HEAD_DIM
FOX_COLS = 3 * FOX_HEADS * HEAD_DIM + FOX_HEADS
MLA_COLS = MLA_Q_RANK + MLA_KV_RANK + MLA_ROPE_DIM
IN_COLS = SWA_COLS + FOX_COLS + MLA_COLS
MLA_QK_DIM = MLA_NOPE_DIM + MLA_ROPE_DIM


def rmsnorm(x, g):
    xf = x.astype(jnp.float32)
    y = xf * lax.rsqrt(jnp.mean(xf * xf, axis=-1, keepdims=True) + EPS) * g.astype(jnp.float32)
    return y.astype(x.dtype)

def t5_causal_bucket(dist):
    max_exact = REL_BUCKETS // 2
    d = jnp.maximum(dist, 0)
    log_ratio = jnp.log(jnp.maximum(d, 1).astype(jnp.float32) / max_exact) / math.log(REL_MAX_DIST / max_exact)
    large = max_exact + (log_ratio * (REL_BUCKETS - max_exact)).astype(jnp.int32)
    large = jnp.minimum(large, REL_BUCKETS - 1)
    return jnp.where(d < max_exact, d, large)

def apply_rope(t, cos, sin):
    t1, t2 = jnp.split(t, 2, axis=-1)
    return jnp.concatenate([t1 * cos - t2 * sin, t1 * sin + t2 * cos], axis=-1)

def swa_sink_attention(q, k, v, sinks, rel_bias):
    B, S = q.shape[0], q.shape[1]
    nb = S // WINDOW
    qb = q.reshape(B, nb, WINDOW, SWA_KV_HEADS, SWA_GROUP, HEAD_DIM)

    def band(t):
        tb = t.reshape(B, nb, WINDOW, SWA_KV_HEADS, HEAD_DIM)
        prev = jnp.pad(tb, ((0, 0), (1, 0), (0, 0), (0, 0), (0, 0)))[:, :-1]
        return jnp.concatenate([prev, tb], axis=2)

    kb, vb = band(k), band(v)
    qi = jnp.arange(WINDOW, dtype=jnp.int32)[:, None] + WINDOW
    kj = jnp.arange(2 * WINDOW, dtype=jnp.int32)[None, :]
    dist = qi - kj
    in_band = (dist >= 0) & (dist < WINDOW)
    valid_key = (jnp.arange(nb)[:, None, None] > 0) | (kj >= WINDOW)[None]
    mask = in_band[None] & valid_key
    bias = rel_bias.astype(jnp.float32)[t5_causal_bucket(dist)]
    bias = bias.transpose(2, 0, 1).reshape(SWA_KV_HEADS, SWA_GROUP, WINDOW, 2 * WINDOW)
    s = jnp.einsum('bnqhgd,bnkhd->bnhgqk', qb, kb, preferred_element_type=jnp.float32)
    s = s * (HEAD_DIM ** -0.5) + bias
    s = jnp.where(mask[None, :, None, None], s, NEG_INF)
    sink = sinks.astype(jnp.float32).reshape(1, 1, SWA_KV_HEADS, SWA_GROUP, 1, 1)
    sink = jnp.broadcast_to(sink, s.shape[:-1] + (1,))
    p = jax.nn.softmax(jnp.concatenate([s, sink], axis=-1), axis=-1)[..., :-1]
    o = jnp.einsum('bnhgqk,bnkhd->bnqhgd', p.astype(v.dtype), vb)
    return o.reshape(B, S, SWA_Q_HEADS * HEAD_DIM)

def blocked_causal_attention(q, k, v, scale, log_forget_cum=None):
    B, S, H = q.shape[0], q.shape[1], q.shape[2]
    nb = S // Q_BLOCK
    q_blocks = q.reshape(B, nb, Q_BLOCK, H, q.shape[-1]).swapaxes(0, 1)
    k_pos = jnp.arange(S, dtype=jnp.int32)
    if log_forget_cum is None:
        f_blocks, f_keys = None, None
    else:
        f_t = log_forget_cum.transpose(0, 2, 1)
        f_blocks = f_t.reshape(B, H, nb, Q_BLOCK).transpose(2, 0, 1, 3)
        f_keys = f_t

    def one_block(args):
        qb, fb, i = args
        s = jnp.einsum('bqhd,bkhd->bhqk', qb, k, preferred_element_type=jnp.float32) * scale
        if fb is not None:
            s = s + (fb[..., :, None] - f_keys[..., None, :])
        q_pos = i * Q_BLOCK + jnp.arange(Q_BLOCK, dtype=jnp.int32)
        s = jnp.where(k_pos[None, :] <= q_pos[:, None], s, NEG_INF)
        p = jax.nn.softmax(s, axis=-1)
        return jnp.einsum('bhqk,bkhd->bqhd', p.astype(v.dtype), v)

    out = lax.map(one_block, (q_blocks, f_blocks, jnp.arange(nb, dtype=jnp.int32)))
    return out.swapaxes(0, 1).reshape(B, S, H * v.shape[-1])

def causal_depthwise_conv(u, w, b):
    S = u.shape[1]
    up = jnp.pad(u, ((0, 0), (CONV_WIDTH - 1, 0), (0, 0)))
    y = b.astype(u.dtype)
    for tap in range(CONV_WIDTH):
        y = y + w[tap].astype(u.dtype) * up[:, tap:tap + S]
    return y

def first_inputs(seed: int = 0) -> dict:
    key = jax.random.key(seed)
    ks = jax.random.split(key, 20)
    L, D = DEPTH, D_MODEL
    f32 = jnp.float32

    def nrm(k, shape, scale):
        return jax.random.normal(k, shape, f32) * scale

    def gain(k, shape):
        return 1.0 + 0.05 * jax.random.normal(k, shape, f32)

    return {
        "x": jax.random.normal(ks[0], (BATCH, SEQ, D), f32),
        "attn_pre_norm": gain(ks[1], (L, D)),
        "w_in": nrm(ks[2], (L, D, IN_COLS), D ** -0.5),
        "forget_bias": 2.0 + 0.5 * jax.random.normal(ks[3], (L, FOX_HEADS), f32),
        "swa_sinks": nrm(ks[4], (L, SWA_Q_HEADS), 0.5),
        "rel_bias": nrm(ks[5], (REL_BUCKETS, SWA_Q_HEADS), 0.5),
        "q_latent_norm": gain(ks[6], (L, MLA_Q_RANK)),
        "w_uq": nrm(ks[7], (L, MLA_Q_RANK, MLA_HEADS * MLA_QK_DIM), MLA_Q_RANK ** -0.5),
        "kv_latent_norm": gain(ks[8], (L, MLA_KV_RANK)),
        "w_ukv": nrm(ks[9], (L, MLA_KV_RANK, MLA_HEADS * (MLA_NOPE_DIM + MLA_V_DIM)), MLA_KV_RANK ** -0.5),
        "group_norm": gain(ks[10], (L, MIX_WIDTH)),
        "w_out": nrm(ks[11], (L, MIX_WIDTH, D), MIX_WIDTH ** -0.5),
        "attn_post_norm": gain(ks[12], (L, D)),
        "ffn_pre_norm": gain(ks[13], (L, D)),
        "w_up": nrm(ks[14], (L, D, 2 * D_FF), D ** -0.5),
        "conv_w": nrm(ks[15], (L, CONV_WIDTH, 2 * D_FF), CONV_WIDTH ** -0.5),
        "conv_b": nrm(ks[16], (L, 2 * D_FF), 0.02),
        "w_down": nrm(ks[17], (L, D_FF, D), D_FF ** -0.5),
        "ffn_post_norm": gain(ks[18], (L, D)),
    }

def first_block(x, attn_pre_norm, w_in, forget_bias, swa_sinks, rel_bias, q_latent_norm, w_uq,
              kv_latent_norm, w_ukv, group_norm, w_out, attn_post_norm, ffn_pre_norm, w_up,
              conv_w, conv_b, w_down, ffn_post_norm):
    B, S, _ = x.shape
    pos = jnp.arange(S, dtype=jnp.float32)
    inv_freq = ROPE_THETA ** (-(jnp.arange(MLA_ROPE_DIM // 2, dtype=jnp.float32) * 2.0 / MLA_ROPE_DIM))
    ang = pos[:, None] * inv_freq[None, :]
    cos = jnp.cos(ang)[:, None, :].astype(x.dtype)
    sin = jnp.sin(ang)[:, None, :].astype(x.dtype)

    for l in range(DEPTH):
        h = rmsnorm(x, attn_pre_norm[l])
        proj = h @ w_in[l]
        a_cols, f_cols, m_cols = jnp.split(proj, [SWA_COLS, SWA_COLS + FOX_COLS], axis=-1)

        qa, ka, va = jnp.split(a_cols, [SWA_WIDTH, SWA_WIDTH + SWA_KV_HEADS * HEAD_DIM], axis=-1)
        out_a = swa_sink_attention(qa.reshape(B, S, SWA_Q_HEADS, HEAD_DIM),
                                   ka.reshape(B, S, SWA_KV_HEADS, HEAD_DIM),
                                   va.reshape(B, S, SWA_KV_HEADS, HEAD_DIM),
                                   swa_sinks[l], rel_bias)

        qf, kf, vf, f_logit = jnp.split(f_cols, [FOX_WIDTH, 2 * FOX_WIDTH, 3 * FOX_WIDTH], axis=-1)
        log_f = jax.nn.log_sigmoid(f_logit.astype(jnp.float32) + forget_bias[l].astype(jnp.float32))
        F = jnp.cumsum(log_f, axis=1)
        out_b = blocked_causal_attention(qf.reshape(B, S, FOX_HEADS, HEAD_DIM),
                                         kf.reshape(B, S, FOX_HEADS, HEAD_DIM),
                                         vf.reshape(B, S, FOX_HEADS, HEAD_DIM),
                                         HEAD_DIM ** -0.5, log_forget_cum=F)

        c_q, c_kv, k_rope = jnp.split(m_cols, [MLA_Q_RANK, MLA_Q_RANK + MLA_KV_RANK], axis=-1)
        qm = (rmsnorm(c_q, q_latent_norm[l]) @ w_uq[l]).reshape(B, S, MLA_HEADS, MLA_QK_DIM)
        q_nope, q_rope = jnp.split(qm, [MLA_NOPE_DIM], axis=-1)
        kv = (rmsnorm(c_kv, kv_latent_norm[l]) @ w_ukv[l]).reshape(B, S, MLA_HEADS, MLA_NOPE_DIM + MLA_V_DIM)
        k_nope, vm = jnp.split(kv, [MLA_NOPE_DIM], axis=-1)
        q_rope = apply_rope(q_rope, cos, sin)
        k_rope = jnp.broadcast_to(apply_rope(k_rope[:, :, None, :], cos, sin), (B, S, MLA_HEADS, MLA_ROPE_DIM))
        out_c = blocked_causal_attention(jnp.concatenate([q_nope, q_rope], axis=-1),
                                         jnp.concatenate([k_nope, k_rope], axis=-1),
                                         vm, MLA_QK_DIM ** -0.5)

        g_a, g_b, g_c = jnp.split(group_norm[l], [SWA_WIDTH, SWA_WIDTH + FOX_WIDTH])
        mixed = jnp.concatenate([rmsnorm(out_a, g_a), rmsnorm(out_b, g_b), rmsnorm(out_c, g_c)], axis=-1)
        x = x + rmsnorm(mixed @ w_out[l], attn_post_norm[l])

        h = rmsnorm(x, ffn_pre_norm[l])
        u = causal_depthwise_conv(h @ w_up[l], conv_w[l], conv_b[l])
        gate, up = jnp.split(u, 2, axis=-1)
        y = (jax.nn.gelu(gate, approximate=True) * up) @ w_down[l]
        x = x + rmsnorm(y, ffn_post_norm[l])
    return x


DEPTH_2 = 2

N_SB_HEADS = 8
N_MOBA_HEADS = 8
N_ATT_HEADS = N_SB_HEADS + N_MOBA_HEADS
ATT_W = N_ATT_HEADS * HEAD_DIM
SB_QBLOCK = 128
MOBA_BLOCK = 256
MOBA_TOPK = 3
MOBA_QBLOCK = 32
N_RET_HEADS = 4
RET_DK = D_MODEL // N_RET_HEADS
RET_DV = 2 * RET_DK
RET_QK_W = N_RET_HEADS * RET_DK
RET_V_W = N_RET_HEADS * RET_DV
RET_CHUNK = 128
D_FF_2 = -(-8 * D_MODEL // 768) * 256
NORM_EPS = 1e-6
GN_EPS = 1e-5
NEG = -1e30
N_EVEN = (DEPTH_2 + 1) // 2
N_ODD = DEPTH_2 // 2


def rms_norm(x, g):
    xf = x.astype(jnp.float32)
    y = xf * lax.rsqrt(jnp.mean(xf * xf, axis=-1, keepdims=True) + NORM_EPS)
    return (y * g.astype(jnp.float32)).astype(x.dtype)

def rotary(x, pos):
    d = x.shape[-1]
    inv = ROPE_THETA ** (-jnp.arange(0, d, 2, dtype=jnp.float32) / d)
    ang = pos.astype(jnp.float32)[:, None] * inv[None, :]
    cos, sin = jnp.cos(ang), jnp.sin(ang)
    xf = x.astype(jnp.float32)
    x1, x2 = xf[..., : d // 2], xf[..., d // 2:]
    out = jnp.concatenate([x1 * cos - x2 * sin, x2 * cos + x1 * sin], axis=-1)
    return out.astype(x.dtype)

def ada_mod(c, w, b):
    m = jax.nn.silu(c) @ w + b
    return jnp.split(m[:, None, :], 6, axis=-1)

def modulate(h, shift, scale):
    return h * (1 + scale) + shift

def stick_breaking_attention(q, k, v):
    B, H, S, D = q.shape
    nblk = S // SB_QBLOCK
    kpos = jnp.arange(S)
    scale = D ** -0.5

    def block(i):
        start = i * SB_QBLOCK
        qb = lax.dynamic_slice_in_dim(q, start, SB_QBLOCK, axis=2)
        z = jnp.einsum('bhqd,bhkd->bhqk', qb, k).astype(jnp.float32) * scale
        qpos = start + jnp.arange(SB_QBLOCK)
        strict = kpos[None, :] < qpos[:, None]
        log_1mb = jnp.where(strict, jax.nn.log_sigmoid(-z), 0.0)
        after = lax.cumsum(log_1mb, axis=3, reverse=True) - log_1mb
        a = jnp.where(strict, jnp.exp(jax.nn.log_sigmoid(z) + after), 0.0)
        return jnp.einsum('bhqk,bhkd->bhqd', a.astype(v.dtype), v)

    out = lax.map(block, jnp.arange(nblk))
    return jnp.moveaxis(out, 0, 2).reshape(B, H, S, D)

def moba_attention(q, k, v):
    B, H, S, D = q.shape
    nb = -(-S // MOBA_BLOCK)
    spad = nb * MOBA_BLOCK
    pad = ((0, 0), (0, 0), (0, spad - S), (0, 0))
    kp = jnp.pad(k, pad)
    vp = jnp.pad(v, pad)
    kb = kp.reshape(B, H, nb, MOBA_BLOCK, D)
    vb = vp.reshape(B, H, nb, MOBA_BLOCK, D)
    kmean = jnp.mean(kb.astype(jnp.float32), axis=3).astype(k.dtype)
    kk = min(MOBA_TOPK, nb)
    scale = D ** -0.5
    nqb = S // MOBA_QBLOCK
    bi = jnp.arange(B)[:, None, None, None]
    hi = jnp.arange(H)[None, :, None, None]
    blk_ids = jnp.arange(nb)
    kpos_in = jnp.arange(MOBA_BLOCK)

    def block(i):
        start = i * MOBA_QBLOCK
        qb = lax.dynamic_slice_in_dim(q, start, MOBA_QBLOCK, axis=2)
        qpos = start + jnp.arange(MOBA_QBLOCK)
        own = start // MOBA_BLOCK
        gate = jnp.einsum('bhqd,bhnd->bhqn', qb, kmean).astype(jnp.float32)
        gate = jnp.where(blk_ids < own, gate, NEG)
        _, idx = lax.top_k(gate, kk)
        sel_valid = idx < own
        ksel = kb[bi, hi, idx]
        vsel = vb[bi, hi, idx]
        s_past = jnp.einsum('bhqd,bhqnkd->bhqnk', qb, ksel).astype(jnp.float32) * scale
        s_past = jnp.where(sel_valid[..., None], s_past, NEG)
        s_past = s_past.reshape(B, H, MOBA_QBLOCK, kk * MOBA_BLOCK)
        k_own = lax.dynamic_slice_in_dim(kp, own * MOBA_BLOCK, MOBA_BLOCK, axis=2)
        v_own = lax.dynamic_slice_in_dim(vp, own * MOBA_BLOCK, MOBA_BLOCK, axis=2)
        s_own = jnp.einsum('bhqd,bhkd->bhqk', qb, k_own).astype(jnp.float32) * scale
        kpos_own = own * MOBA_BLOCK + kpos_in
        s_own = jnp.where(kpos_own[None, :] <= qpos[:, None], s_own, NEG)
        p = jax.nn.softmax(jnp.concatenate([s_past, s_own], axis=-1), axis=-1).astype(v.dtype)
        p_past = p[..., : kk * MOBA_BLOCK].reshape(B, H, MOBA_QBLOCK, kk, MOBA_BLOCK)
        p_own = p[..., kk * MOBA_BLOCK:]
        return (jnp.einsum('bhqnk,bhqnkd->bhqd', p_past, vsel)
                + jnp.einsum('bhqk,bhkd->bhqd', p_own, v_own))

    out = lax.map(block, jnp.arange(nqb))
    return jnp.moveaxis(out, 0, 2).reshape(B, H, S, D)

def retention_chunkwise(q, k, v):
    B, H, S, dk = q.shape
    dv = v.shape[-1]
    C = RET_CHUNK
    nc = S // C
    log_g = jnp.log(1.0 - 2.0 ** (-5.0 - jnp.arange(H, dtype=jnp.float32)))
    n = jnp.arange(C, dtype=jnp.float32)
    diff = n[:, None] - n[None, :]
    decay = jnp.where(diff >= 0, jnp.exp(log_g[:, None, None] * jnp.maximum(diff, 0.0)), 0.0)
    xi = jnp.exp(log_g[:, None] * (n + 1.0))
    zeta = jnp.exp(log_g[:, None] * (C - 1.0 - n))
    chunk_decay = jnp.exp(log_g * C)

    def chunks(t):
        return jnp.moveaxis(t.reshape(B, H, nc, C, t.shape[-1]), 2, 0)

    def step(state, inp):
        qi, ki, vi = inp
        inner = jnp.einsum('bhqd,bhkd->bhqk', qi, ki).astype(jnp.float32) * decay
        o = (jnp.einsum('bhqk,bhkv->bhqv', inner, vi.astype(jnp.float32))
             + jnp.einsum('bhqd,bhdv->bhqv', qi.astype(jnp.float32), state) * xi[..., None])
        state = state * chunk_decay[:, None, None] + jnp.einsum(
            'bhkd,bhkv->bhdv', ki.astype(jnp.float32) * zeta[..., None], vi.astype(jnp.float32))
        return state, o

    init = jnp.zeros((B, H, dk, dv), jnp.float32)
    _, out = lax.scan(step, init, (chunks(q), chunks(k), chunks(v)))
    return jnp.moveaxis(out, 0, 2).reshape(B, H, S, dv)

def attn_hybrid_mixer(h, w_qkv, w_o, pos):
    B, S, _ = h.shape
    qkv = (h @ w_qkv).reshape(B, S, 3, N_ATT_HEADS, HEAD_DIM).transpose(2, 0, 3, 1, 4)
    q, k, v = qkv[0], qkv[1], qkv[2]
    sb = stick_breaking_attention(q[:, :N_SB_HEADS], k[:, :N_SB_HEADS], v[:, :N_SB_HEADS])
    qm = rotary(q[:, N_SB_HEADS:], pos)
    km = rotary(k[:, N_SB_HEADS:], pos)
    mb = moba_attention(qm, km, v[:, N_SB_HEADS:])
    o = jnp.concatenate([sb, mb], axis=1).transpose(0, 2, 1, 3).reshape(B, S, ATT_W)
    return o @ w_o

def retention_mixer(h, w_in, gn_gain, w_o, pos):
    B, S, _ = h.shape
    proj = h @ w_in
    q, k, v, g = jnp.split(proj, [RET_QK_W, 2 * RET_QK_W, 2 * RET_QK_W + RET_V_W], axis=-1)

    def heads(t, d):
        return t.reshape(B, S, N_RET_HEADS, d).transpose(0, 2, 1, 3)

    q = rotary(heads(q, RET_DK), pos)
    k = rotary(heads(k, RET_DK), pos) * (RET_DK ** -0.5)
    v = heads(v, RET_DV)
    o = retention_chunkwise(q, k, v)
    mu = jnp.mean(o, axis=-1, keepdims=True)
    var = jnp.mean(jnp.square(o - mu), axis=-1, keepdims=True)
    o = (o - mu) * lax.rsqrt(var + GN_EPS)
    o = o.transpose(0, 2, 1, 3).reshape(B, S, RET_V_W) * gn_gain.astype(jnp.float32)
    return (jax.nn.silu(g) * o.astype(h.dtype)) @ w_o

def swiglu(h, w_gate_up, w_down):
    gt, up = jnp.split(h @ w_gate_up, 2, axis=-1)
    return (jax.nn.silu(gt) * up) @ w_down

def second_inputs(seed: int = 0) -> dict:
    key = jax.random.key(seed)
    ks = jax.random.split(key, 14)
    f32 = jnp.float32

    def nrm(k, shape, fan_in):
        return jax.random.normal(k, shape, f32) * (fan_in ** -0.5)

    return {
        "x": jax.random.normal(ks[0], (BATCH, SEQ, D_MODEL), f32),
        "c": jax.random.normal(ks[1], (BATCH, D_MODEL), f32),
        "ada_w": nrm(ks[2], (DEPTH_2, D_MODEL, 6 * D_MODEL), D_MODEL),
        "ada_b": 0.02 * jax.random.normal(ks[3], (DEPTH_2, 6 * D_MODEL), f32),
        "norm_gains": 1.0 + 0.05 * jax.random.normal(ks[4], (DEPTH_2, 2, D_MODEL), f32),
        "att_w_qkv": nrm(ks[5], (N_EVEN, D_MODEL, 3 * ATT_W), D_MODEL),
        "att_w_o": nrm(ks[6], (N_EVEN, ATT_W, D_MODEL), ATT_W),
        "ret_w_in": nrm(ks[7], (N_ODD, D_MODEL, 2 * RET_QK_W + 2 * RET_V_W), D_MODEL),
        "ret_gn": 1.0 + 0.05 * jax.random.normal(ks[8], (N_ODD, RET_V_W), f32),
        "ret_w_o": nrm(ks[9], (N_ODD, RET_V_W, D_MODEL), RET_V_W),
        "ffn_w_gate_up": nrm(ks[10], (DEPTH_2, D_MODEL, 2 * D_FF_2), D_MODEL),
        "ffn_w_down": nrm(ks[11], (DEPTH_2, D_FF_2, D_MODEL), D_FF_2),
        "final_norm": 1.0 + 0.05 * jax.random.normal(ks[12], (D_MODEL,), f32),
    }

def second_block(x, c, ada_w, ada_b, norm_gains, att_w_qkv, att_w_o, ret_w_in, ret_gn,
              ret_w_o, ffn_w_gate_up, ffn_w_down, final_norm):
    S = x.shape[1]
    pos = jnp.arange(S, dtype=jnp.int32)
    for layer in range(DEPTH_2):
        shift_m, scale_m, gate_m, shift_f, scale_f, gate_f = ada_mod(c, ada_w[layer], ada_b[layer])
        h = modulate(rms_norm(x, norm_gains[layer, 0]), shift_m, scale_m)
        j = layer // 2
        if layer % 2 == 0:
            y = attn_hybrid_mixer(h, att_w_qkv[j], att_w_o[j], pos)
        else:
            y = retention_mixer(h, ret_w_in[j], ret_gn[j], ret_w_o[j], pos)
        x = x + gate_m * y
        h = modulate(rms_norm(x, norm_gains[layer, 1]), shift_f, scale_f)
        x = x + gate_f * swiglu(h, ffn_w_gate_up[layer], ffn_w_down[layer])
    return rms_norm(x, final_norm)


def setup_inputs(seed=0):
    out = dict(first_inputs(seed))
    for name, value in second_inputs(seed + 1).items():
        if name != "x":
            out[name + "_2"] = value
    return out


def reference(
    x, attn_pre_norm, w_in, forget_bias, swa_sinks, rel_bias, q_latent_norm, w_uq,
    kv_latent_norm, w_ukv, group_norm, w_out, attn_post_norm, ffn_pre_norm, w_up, conv_w,
    conv_b, w_down, ffn_post_norm, c_2, ada_w_2, ada_b_2, norm_gains_2, att_w_qkv_2, att_w_o_2,
    ret_w_in_2, ret_gn_2, ret_w_o_2, ffn_w_gate_up_2, ffn_w_down_2, final_norm_2,
):
    x = first_block(
        x, attn_pre_norm, w_in, forget_bias, swa_sinks, rel_bias, q_latent_norm, w_uq,
        kv_latent_norm, w_ukv, group_norm, w_out, attn_post_norm, ffn_pre_norm, w_up, conv_w,
        conv_b, w_down, ffn_post_norm,
    )
    return second_block(
        x, c_2, ada_w_2, ada_b_2, norm_gains_2, att_w_qkv_2, att_w_o_2, ret_w_in_2, ret_gn_2,
        ret_w_o_2, ffn_w_gate_up_2, ffn_w_down_2, final_norm_2,
    )


_drawn_inputs = setup_inputs


def setup_inputs(seed=0):
    import zlib

    import numpy as np

    out = dict(_drawn_inputs(seed))
    spreads = {}
    factors = {'swa_sinks': 3.27, 'conv_b': 2.961, 'ret_gn_2': 4.108}
    for name, (base, spread) in spreads.items():
        noise = np.random.default_rng([zlib.crc32(name.encode()), seed]).standard_normal(out[name].shape)
        drawn = base * np.exp(spread * noise) if base else spread * noise
        out[name] = __import__('jax').numpy.asarray(drawn.astype(out[name].dtype))
    for name, factor in factors.items():
        out[name] = (out[name] * factor).astype(out[name].dtype)
    return out
```

```python
import math
from contextlib import ExitStack

import concourse.bass as bass
import numpy as np
from concourse import mybir

F32 = mybir.dt.float32
F32R = mybir.dt.float32r
ACT = mybir.ActivationFunctionType
ALU = mybir.AluOpType

P = 128
S = 256
D = 1024
DT = D // P
FF = 2816
FT = FF // P
HALF = FT // 2
EPS = 1e-6
GN_EPS = 1e-5
NEG = -1e30
HD = 64
RANKQ, RANKKV, ROPE = 256, 128, 32
BUCKETS, MAX_DIST, WINDOW = 32, 128, 128
BAND = 384
RET_H, RET_DV = 4, 512
THETA = 10000.0

RAW_SLOTS, SPLIT_SLOTS = 4, 2
CHUNK = 2048
UNROLL = 4

PHASES = [
    ("w_in", 9, DT, 2, 1), ("mla", 1, 1, 10, 1), ("w_out", 4, DT, 2, 1),
    ("up", 22, DT, 2, 1), ("down", 16, HALF, 1, 2),
    ("qkv", 12, DT, 2, 1), ("att_o", 4, DT, 2, 1), ("gu0", 22, DT, 2, 1), ("dn0", 16, HALF, 1, 2),
    ("ret_in", 24, DT, 2, 1), ("ret_o", 8, 2 * DT, 1, 1), ("gu1", 22, DT, 2, 1), ("dn1", 16, HALF, 1, 2),
]
MLA_UNITS = 4


class Phase:

    def __init__(self, name, n, kt, nb, per_unit, chunk0, unit0):
        self.name, self.n, self.kt, self.nb, self.per_unit = name, n, kt, nb, per_unit
        self.chunk0, self.unit0 = chunk0, unit0
        self.units = MLA_UNITS if name == "mla" else n // per_unit

    def size(self, c):
        if self.name == "w_in" and c == self.n - 1:
            return DT * P
        return self.kt * self.nb * P


def lay_out_phases():
    out, chunk, unit = {}, 0, 0
    for name, n, kt, nb, per in PHASES:
        ph = out[name] = Phase(name, n, kt, nb, per, chunk, unit)
        chunk, unit = chunk + n, unit + ph.units
    return out


PH = lay_out_phases()
ORDER = list(PH.values())
CHUNKS = sum(ph.n for ph in ORDER)


def phase_of(chunk):
    for ph in ORDER:
        if chunk < ph.chunk0 + ph.n:
            return ph, chunk - ph.chunk0


ADA_PIECES = 24
ADA_STEPS = {
    "w_in": lambda c: int(c < 8), "w_out": lambda c: 2, "down": lambda c: c % 2,
    "qkv": lambda c: 1, "att_o": lambda c: 1, "dn0": lambda c: c % 2,
}


def ada_before(name, c):
    n = 0
    for ph in ORDER:
        f = ADA_STEPS.get(ph.name, lambda c: 0)
        if ph.name == name:
            return n + sum(f(i) for i in range(c))
        n += sum(f(i) for i in range(ph.n))


COLS = {}
for _name, _n in [("pre", 8), ("qlat", 2), ("kvlat", 1), ("group", 8), ("post", 8), ("ffnpre", 8), ("conv_w", 132),
                  ("conv_b", 44), ("ffnpost", 8), ("norms2", 32), ("ada_b", 96), ("gn", 16), ("final", 8),
                  ("cond", 8), ("sinks", 8), ("fbias", 1), ("rel", 8)]:
    COLS[_name] = (sum(v[1] for v in COLS.values()), _n)
NCOLS = sum(v[1] for v in COLS.values())

TAB1 = [("mask", 384), ("cos", S), ("sin", S), ("perm", P), ("onehot", BAND)]
TAB2 = [("mask", 384), ("cos", S), ("sin", S), ("perm", P), ("tri", P), ("negones", P), ("strict", 384), ("strictneg", 384)]
TAB3 = [("cos", S), ("sin", S), ("decay", RET_H * 384)]

ARENA = 17600
ADA0 = ARENA - 2 * CHUNK
EARLY = [("y", 2048), ("sq", 2048)]
ATT1 = [("qa", 1024), ("ka", 256), ("qf", 512), ("kf", 512), ("v_a", 256), ("v_f", 512), ("qn", 512), ("kn", 512),
        ("mixed", 2048), ("s", 768), ("pT", 768), ("bias", 2048)] + [(n, k) for n, k in TAB1] + [
        ("lat", 768), ("kr", 256), ("qr", 256), ("v_m", 512), ("f", 256), ("fneg", 256)]
FFN = EARLY + [("u", 1024), ("g", 512), ("hid", 512)]
ATT2 = [("q", 2048), ("k", 2048), ("v", 2048)] + TAB2 + [("s", 768), ("pT", 768), ("e", 768), ("lm", 768), ("rot", 512)]
RET = [("q", 2048), ("k", 2048), ("v", 4096)] + TAB3 + [("inner", 768), ("on", 1024), ("rot", 512), ("o", 512)]


TAB1_AT = sum(n for _, n in ATT1[:ATT1.index(TAB1[0])])
TAB2_AT = sum(n for _, n in ATT2[:ATT2.index(TAB2[0])])
TAB3_AT = sum(n for _, n in RET[:RET.index(TAB3[0])])


class Step:

    def __init__(self, j, i=None):
        self.j, self.i = j, i

    def n(self, f):
        if self.i is None:
            return f(self.j)
        by = f(self.j + UNROLL) - f(self.j)
        return self.i * by + f(self.j) if by else f(self.j)


def steps(eng, n, lead, tail, body):
    lead = min(lead, n)
    trips = (n - lead - tail) // UNROLL
    if trips < 2:
        trips = 0
    for c in range(lead):
        body(Step(c))
    if trips:
        with eng.Fori(0, trips) as i:
            for j in range(UNROLL):
                body(Step(lead + j, i))
    for c in range(lead + trips * UNROLL, n):
        body(Step(c))


NORM_TILES = [8, 2, 1, 4, 2, 2, 8, 8, 8, 8, 8, 8, 8, 8]
PRE, QLAT, KVLAT, GROUP_A, GROUP_F, GROUP_M, POST, FFNPRE, FFNPOST, L0, L0F, L1, L1F, FINAL = range(14)
SPLITS = [PRE, QLAT, KVLAT, GROUP_A, GROUP_F, GROUP_M, FFNPRE, L0, L0F, L1, L1F]


def tiles_before(norm):
    return sum(NORM_TILES[i] for i in SPLITS if i < norm)


HEADS1, HEADS2 = 16, 8
SB_HEADS = 8


def build(nc, dram):
    ctx = ExitStack()
    with ctx:
        def sb(name, n, dt=F32, parts=P):
            return ctx.enter_context(nc.sbuf_tensor(name, [parts, n], dt))

        def sem(name):
            return ctx.enter_context(nc.semaphore(name))

        raw = [sb(f"raw{i}", CHUNK) for i in range(RAW_SLOTS)]
        w_hi = [sb(f"w_hi{i}", CHUNK, F32R) for i in range(SPLIT_SLOTS)]
        w_lo = [sb(f"w_lo{i}", CHUNK, F32R) for i in range(SPLIT_SLOTS)]
        h_hi, h_lo = sb("h_hi", DT * S, F32R), sb("h_lo", DT * S, F32R)
        hid_hi, hid_lo = sb("hid_hi", FT * S, F32R), sb("hid_lo", FT * S, F32R)
        x = sb("x", DT * S)
        cols = sb("cols", NCOLS)
        ident, ones = sb("ident", P), sb("ones", S)
        mod = sb("mod", 96)
        gscale = sb("gscale", 32)
        cond_silu = sb("cond_silu", 8)
        diag = sb("diag", 2 * P)
        stat = sb("stat", 16)
        head_stat = sb("head_stat", 2 * 16)
        gn_stat = sb("gn_stat", 2 * 32)
        ada_acc = [sb(f"ada_acc{i}", S) for i in range(2)]
        arena = sb("arena", ARENA)
        ada_raw = [arena[:, ADA0 + i * CHUNK:ADA0 + (i + 1) * CHUNK] for i in range(2)]

        def parts(table):
            at, out = 0, {}
            for name, n in table:
                out[name] = arena[:, at:at + n]
                at += n
            assert at <= ADA0, (at, ADA0)
            return out

        e0, a1, ff, a2, rt = parts(EARLY), parts(ATT1), parts(FFN), parts(ATT2), parts(RET)
        rt["g"] = arena[:, ADA0:ARENA]
        band0 = sum(n for name, n in ATT1[:8])
        band = arena[:, band0:band0 + 8 * BAND]
        rel_rows = a1["bias"][0:BUCKETS + 1, 0:8 * P]
        lat_sq, lat_y = arena[:, band0 + 2048:band0 + 2816], arena[:, band0 + 2816:band0 + 3584]
        gate_tmp = a1["mixed"][0:4, :]

        def col(name, j, n=1, rows=P):
            o = COLS[name][0]
            return cols[0:rows, o + j:o + j + n]

        psum = [ctx.enter_context(nc.psum_tensor(f"psum{i}", [P, 512], F32)) for i in range(8)]
        lin, sco, tra, att = psum[0:2], psum[2:4], psum[4:6], psum[6:8]
        ssum, rbc, ada_ps = sco[0][:, 0:2], sco[1][:, 0:S], att

        x_in, cols_in, tab1_in, tab2_in, tab3_in = (sem(n) for n in ("x_in", "cols_in", "tab1_in", "tab2_in", "tab3_in"))
        ident_in, band_out, bias_in, y_out = sem("ident_in"), sem("band_out"), sem("bias_in"), sem("y_out")
        raw_in = [sem(f"raw_in{i}") for i in range(RAW_SLOTS)]
        hi_ready, split_ready, chunk_done = sem("hi_ready"), sem("split_ready"), sem("chunk_done")
        lin_free = [sem(f"lin_free{i}") for i in range(2)]
        mla_units = sem("mla_units")
        ada_in = [sem(f"ada_in{i}") for i in range(2)]
        ada_step, ada_mul, ada_sum, ada_out, cond_ready = (sem(n) for n in (
            "ada_step", "ada_mul", "ada_sum", "ada_out", "cond_ready"))
        ones_ready, rel_ready, band_ps, band_ready = sem("ones_ready"), sem("rel_ready"), sem("band_ps"), sem("band_ready")
        sq_ready, ssum_ready, ms_ready, rsq_ready = sem("sq_ready"), sem("ssum_ready"), sem("ms_ready"), sem("rsq_ready")
        diag_ready, rbc_ready, r_used = sem("diag_ready"), sem("rbc_ready"), sem("r_used")
        hh_ready, h_tiles, x_ready = sem("hh_ready"), sem("h_tiles"), sem("x_ready")
        dve_chain, act_chain = sem("dve_chain"), sem("act_chain")
        rot_ready, rot_done, f_in, f_ln, f_ready = (sem(n) for n in (
            "rot_ready", "rot_done", "f_in", "f_ln", "f_ready"))
        scores, scores_read, exps, probs, trans, trans_out, pv, att_out, o_hi, o_tiles = (sem(n) for n in (
            "scores", "scores_read", "exps", "probs", "trans", "trans_out", "pv", "att_out", "o_hi", "o_tiles"))
        z_ready, z_ln, lm_ready, z_sum, z_masked, stick = (sem(n) for n in (
            "z_ready", "z_ln", "lm_ready", "z_sum", "z_masked", "stick"))
        conv_in, conv_tap, gelu_ready, hid_ready, hid_hh, hid_tiles = (sem(n) for n in (
            "conv_in", "conv_tap", "gelu_ready", "hid_ready", "hid_hh", "hid_tiles"))
        ret_s, ret_inner, ret_o, ret_var, ret_rsq, ret_rstd, ret_norm, ret_tr, ret_y, ret_hh, ret_tiles = (sem(n) for n in (
            "ret_s", "ret_inner", "ret_o", "ret_var", "ret_rsq", "ret_rstd", "ret_norm", "ret_tr", "ret_y", "ret_hh", "ret_tiles"))

        def units_done(eng, unit):
            for b in range(2):
                n = (unit + 1 - b) // 2
                if n > 0:
                    eng.wait_ge(lin_free[b], n)

        def unit_free(eng, ph, step, f):
            if ph.unit0 + f(step.j) >= 2:
                eng.wait_ge(lin_free[(ph.unit0 + f(step.j)) % 2], step.n(lambda c: (ph.unit0 + f(c)) // 2))

        def leave(ins, unit):
            return ins.then_inc(lin_free[unit % 2], 1)

        def v3(ap, n):
            return ap.rearrange("p (a b) -> p a b", a=n)

        def over(ap, n):
            return ap.unsqueeze(1).to_broadcast([ap.shape[0], n, ap.shape[1]])

        def mod_col(layer, which, k):
            return mod[:, 48 * layer + 8 * which + k:48 * layer + 8 * which + k + 1]

        hh, hl = h_hi[:, :], h_lo[:, :]
        no_shift = lambda k: None
        NORM = {
            PRE: (x[:, :], e0["sq"], e0["y"], lambda k: col("pre", k), no_shift, hh, hl),
            QLAT: (a1["lat"][:, 0:512], lat_sq[:, 0:512], lat_y[:, 0:512], lambda k: col("qlat", k), no_shift,
                   hid_hi[:, 0:512], hid_lo[:, 0:512]),
            KVLAT: (a1["lat"][:, 512:768], lat_sq[:, 512:768], lat_y[:, 512:768], lambda k: col("kvlat", k), no_shift,
                    hid_hi[:, 512:768], hid_lo[:, 512:768]),
            POST: (e0["y"], e0["sq"], None, lambda k: col("post", k), None, None, None),
            FFNPRE: (x[:, :], e0["sq"], e0["y"], lambda k: col("ffnpre", k), no_shift, hh, hl),
            FFNPOST: (e0["y"], e0["sq"], None, lambda k: col("ffnpost", k), None, None, None),
            FINAL: (x[:, :], e0["sq"], e0["y"], lambda k: col("final", k), None, None, None),
        }
        for i, t0, n in ((GROUP_A, 0, 4), (GROUP_F, 4, 2), (GROUP_M, 6, 2)):
            cut = slice(t0 * S, (t0 + n) * S)
            NORM[i] = (a1["mixed"][:, cut], e0["sq"][:, cut], e0["y"][:, cut], lambda k, t0=t0: col("group", t0 + k),
                       no_shift, hh[:, cut], hl[:, cut])
        for i, layer, which in ((L0, 0, 0), (L0F, 0, 3), (L1, 1, 0), (L1F, 1, 3)):
            NORM[i] = (x[:, :], e0["sq"], e0["y"],
                       lambda k, i=i: gscale[:, 8 * (L0, L0F, L1, L1F).index(i) + k:8 * (L0, L0F, L1, L1F).index(i) + k + 1],
                       lambda k, layer=layer, which=which: mod_col(layer, which, k), hh, hl)

        def half(ap, tile, h):
            return ap[HD * h:HD * h + HD, tile * S:(tile + 1) * S]

        heads1 = []
        for n in range(8):
            pair, h = n // 2, n % 2
            bias = a1["bias"][:, n * S:(n + 1) * S]
            v = v3(a1["v_a"], 2)
            heads1.append(dict(parts=[(half(a1["qa"], pair, h), half(a1["ka"], 0, h))], bias=(bias[:, P:S], bias),
                               sink=col("sinks", n), v=lambda kt, v=v, h=h: v[:, kt, HD * h:HD * h + HD], decay=None))
        mask = a1["mask"]
        for n in range(4):
            v = v3(a1["v_f"], 2)
            heads1.append(dict(parts=[(half(a1["qf"], n // 2, n % 2), half(a1["kf"], n // 2, n % 2))],
                               bias=(mask[:, 0:P], mask[:, P:384]), sink=None, decay=n,
                               v=lambda kt, v=v, n=n: v[:, kt, HD * n:HD * n + HD]))
        for n in range(4):
            v = v3(a1["v_m"], 2)
            rope = slice(ROPE * n, ROPE * n + ROPE)
            heads1.append(dict(parts=[(half(a1["qn"], n // 2, n % 2), half(a1["kn"], n // 2, n % 2)),
                                      (a1["qr"][rope, :], a1["kr"][rope, :])],
                               bias=(mask[:, 0:P], mask[:, P:384]), sink=None, decay=None,
                               v=lambda kt, v=v, n=n: v[:, kt, HD * n:HD * n + HD]))
        heads2 = []
        mask2, v2 = a2["mask"], v3(a2["v"], 2)
        for n in range(8, 16):
            heads2.append(dict(parts=[(half(a2["q"], n // 2, n % 2), half(a2["k"], n // 2, n % 2))],
                               bias=(mask2[:, 0:P], mask2[:, P:384]), sink=None, decay=None,
                               v=lambda kt, n=n: v2[:, kt, HD * n:HD * n + HD]))

        PAIRS1 = HEADS1 // 2
        PAIRS_SB = SB_HEADS // 2

        def two(ap, n):
            return ap[:, n % 2 * 384:(n % 2 + 1) * 384]

        block = ctx.enter_context(nc.Block())

        @block.sync
        def _(sp):
            sp.dma_start(cols[:, :], dram["cols"]).then_inc(cols_in, 16)
            sp.dma_start(x[:, :], dram["x"]).then_inc(x_in, 16)
            sp.dma_start(ident[:, :], dram["ident"]).then_inc(ident_in, 16)
            sp.dma_start(arena[:, TAB1_AT:TAB1_AT + dram["tab1"].shape[1]], dram["tab1"]).then_inc(tab1_in, 16)

            def load_ada(step, f):
                slot = f(step.j) % 2
                if f(step.j) >= 2:
                    sp.wait_ge(ada_mul, step.n(lambda c: f(c) - 1))
                sp.dma_start(ada_raw[slot], dram["ada"][bass.ds(step.n(lambda c: f(c) * P), P), :]).then_inc(ada_in[slot], 16)

            def phase(ph):
                pieces = ADA_STEPS.get(ph.name, lambda c: 0)

                def load(step):
                    chunk = ph.chunk0 + step.j
                    slot, n = chunk % RAW_SLOTS, ph.size(step.j)
                    if chunk >= RAW_SLOTS:
                        sp.wait_ge(split_ready, step.n(lambda c: ph.chunk0 + c - RAW_SLOTS + 1))
                    src = dram[ph.name][bass.ds(step.n(lambda c: c * P), P), 0:n]
                    sp.dma_start(raw[slot][:, 0:n], src).then_inc(raw_in[slot], 16)
                    for m in range(pieces(step.j)):
                        load_ada(step, lambda c, m=m: ada_before(ph.name, c) + m)

                steps(sp, ph.n, 4, 0, load)

            for ph in ORDER:
                if ph.name == "up":
                    sp.wait_ge(h_tiles, tiles_before(FFNPRE))
                    sp.dma_start(arena[:, TAB2_AT:TAB2_AT + dram["tab2"].shape[1]], dram["tab2"]).then_inc(tab2_in, 16)
                if ph.name == "gu0":
                    sp.wait_ge(o_tiles, 8)
                    sp.dma_start(arena[:, TAB3_AT:TAB3_AT + dram["tab3"].shape[1]], dram["tab3"]).then_inc(tab3_in, 16)
                phase(ph)
            sp.wait_ge(x_ready, 3)
            sp.dma_start(dram["out"], e0["sq"]).then_inc(y_out, 16)
            sp.wait_ge(y_out, 16)

        @block.gpsimd
        def _(pool):
            pool.wait_ge(band_ready, 8)
            pool.dma_start(dram["band"], band).then_inc(band_out, 16)
            pool.wait_ge(band_out, 16)
            skew = dram["band_skew"]
            pool.wait_ge(band_ps, 8)
            pool.dma_start(v3(a1["bias"], 8), skew).then_inc(bias_in, 16)

        @block.scalar
        def _(act):
            chain = [0]

            def link(ins):
                chain[0] += 1
                ins.then_inc(act_chain, 1)
                act.wait_ge(act_chain, chain[0])

            def hi(chunk, step=None, ph=None):
                if chunk >= CHUNKS:
                    return
                of, c = phase_of(chunk)
                n = of.size(c)
                at = (lambda f: f(chunk)) if step is None else (lambda f: step.n(lambda c: f(ph.chunk0 + c + 1)))
                act.wait_ge(raw_in[chunk % RAW_SLOTS], at(lambda k: 16 * (k // RAW_SLOTS + 1)))
                if chunk >= SPLIT_SLOTS:
                    act.wait_ge(chunk_done, at(lambda k: k - SPLIT_SLOTS + 1))
                nc.scalar.activation(w_hi[chunk % SPLIT_SLOTS][:, 0:n], raw[chunk % RAW_SLOTS][:, 0:n], ACT.Copy)\
                    .then_inc(hi_ready, 1)

            def unit_ready(ph, step, f):
                act.wait_ge(chunk_done, step.n(lambda c: ph.chunk0 + f(c) + 1))

            def square(i):
                src, sq = NORM[i][0], NORM[i][1]
                if i and i not in (GROUP_F, GROUP_M):
                    act.wait_ge(ssum_ready, i)
                nc.scalar.activation(sq, src, ACT.Square).then_inc(sq_ready, 1)

            def rsqrt(i):
                act.wait_ge(ms_ready, i + 1)
                link(nc.scalar.activation(stat[:, 2:4], stat[:, 0:2], ACT.Ln))
                nc.scalar.activation(stat[:, 4:6], stat[:, 2:4], ACT.Exp, scale=-0.5).then_inc(rsq_ready, 1)

            def round_h(i):
                _, _, tmp, gain, shift, dst, _ = NORM[i]
                act.wait_ge(r_used, i + 1)
                for k in range(NORM_TILES[i]):
                    cut = slice(k * S, (k + 1) * S)
                    if shift(k) is None:
                        ins = nc.scalar.activation(dst[:, cut], tmp[:, cut], ACT.Copy, scale=gain(k))
                    else:
                        ins = nc.scalar.activation(dst[:, cut], tmp[:, cut], ACT.Identity, scale=gain(k), bias=shift(k))
                    ins.then_inc(hh_ready, 1)

            def norm_h(i):
                square(i)
                rsqrt(i)
                round_h(i)

            act.wait_ge(cols_in, 16)
            nc.scalar.activation(cond_silu[:, :], col("cond", 0, 8), ACT.Silu).then_inc(cond_ready, 1)
            act.wait_ge(x_in, 16)
            square(PRE)
            for n in range(8):
                act.wait_ge(band_ps, n + 1)
                nc.scalar.activation(band[:, n * BAND:(n + 1) * BAND], (tra + att)[n % 4][:, 0:BAND], ACT.Copy)\
                    .then_inc(band_ready, 1)
            hi(0)
            rsqrt(PRE)
            round_h(PRE)

            ph = PH["w_in"]
            dst = {0: [(a1["lat"][:, 0:512], 0, 512, 1.0)],
                   1: [(a1["lat"][:, 512:768], 0, 256, 1.0), (a1["kr"], 256, 512, 1.0)],
                   2: [(a1["qa"][:, 0:512], 0, 512, HD ** -0.5)], 3: [(a1["qa"][:, 512:1024], 0, 512, HD ** -0.5)],
                   4: [(a1["qf"], 0, 512, HD ** -0.5)], 5: [(a1["kf"], 0, 512, 1.0)],
                   6: [(a1["ka"], 0, 256, 1.0)], 7: [(a1["v_f"], 0, 512, 1.0)]}

            def leave_w_in(c):
                act.wait_ge(chunk_done, c + 1)
                bank = lin[c % 2]
                if c == 0:
                    act.wait_ge(h_tiles, 8)
                    act.wait_ge(band_out, 16)
                if c == 6:
                    nc.scalar.activation(gate_tmp[:, 0:S], bank[0:4, S:2 * S], ACT.Identity, bias=col("fbias", 0, 1, 4))\
                        .then_inc(f_in, 1)
                if c == 8:
                    ins = nc.scalar.activation(v3(a1["v_a"], 2), v3(bank[:, :], 2)[:, :, 0:P], ACT.Copy)
                else:
                    for to, a, b, scale in dst[c]:
                        ins = nc.scalar.activation(to, bank[:, a:b], ACT.Copy, scale=scale)
                leave(ins, c)

            for c in range(ph.n):
                hi(ph.chunk0 + c + 1)
                if c:
                    leave_w_in(c - 1)
                if c == 3:
                    act.wait_ge(lin_free[0], 1)
                    act.wait_ge(lin_free[1], 1)
                    square(QLAT)
                    nc.scalar.activation(NORM[KVLAT][1], NORM[KVLAT][0], ACT.Square).then_inc(sq_ready, 1)
                if c == 4:
                    rsqrt(QLAT)
                if c == 5:
                    round_h(QLAT)
                    rsqrt(KVLAT)
                if c == 6:
                    round_h(KVLAT)
                if c == 8:
                    act.wait_ge(f_in, 1)
                    link(nc.scalar.activation(gate_tmp[:, S:2 * S], gate_tmp[:, 0:S], ACT.Abs))
                    link(nc.scalar.activation(gate_tmp[:, 2 * S:3 * S], gate_tmp[:, S:2 * S], ACT.Exp, scale=-1.0))
                    nc.scalar.activation(gate_tmp[:, 3 * S:4 * S], gate_tmp[:, 2 * S:3 * S], ACT.Ln, bias=ones[0:4, 0:1])\
                        .then_inc(f_ln, 1)
            leave_w_in(8)
            hi(PH["w_out"].chunk0)
            u0 = PH["mla"].unit0
            vm = a1["v_m"]
            qscale = (HD + ROPE) ** -0.5
            for u, todo in enumerate([[(a1["qn"], 0, 512, qscale)],
                                      [(a1["qr"], 0, 256, qscale), (a1["kn"][:, 0:256], 256, 512, 1.0)],
                                      [(a1["kn"][:, 256:512], 0, 256, 1.0), (vm[:, 0:256], 256, 512, 1.0)],
                                      [(vm[:, 256:512], 0, 256, 1.0)]]):
                if u < MLA_UNITS - 1:
                    act.wait_ge(mla_units, u + 1)
                else:
                    act.wait_ge(chunk_done, PH["mla"].chunk0 + 1)
                for to, a, b, scale in todo:
                    ins = nc.scalar.activation(to, lin[(u0 + u) % 2][:, a:b], ACT.Copy, scale=scale)
                leave(ins, u0 + u)

            def exp_head(n, base, a, sink):
                hs = head_stat[:, 16 * (n % 2):16 * (n % 2) + 16]
                s = two(a["s"], n)
                act.wait_ge(scores_read, base + n + 1)
                if sink is not None:
                    nc.scalar.activation(hs[:, 6:8], hs[:, 2:4], ACT.Exp, bias=sink)
                nc.scalar.activation(s[:, 0:P], s[:, 0:P], ACT.Exp, bias=hs[:, 2:3], accum_out=hs[:, 4:5])
                nc.scalar.activation(s[:, P:384], s[:, P:384], ACT.Exp, bias=hs[:, 3:4], accum_out=hs[:, 5:6])\
                    .then_inc(exps, 1)

            def copy_head(n, base, a):
                act.wait_ge(trans, base + n + 1)
                if n >= 2:
                    act.wait_ge(pv, base + n - 1)
                nc.scalar.activation(two(a["pT"], n), tra[n % 2][:, 0:384], ACT.Copy).then_inc(trans_out, 1)

            for n in range(HEADS1):
                exp_head(n, 0, a1, heads1[n]["sink"])
                if n:
                    copy_head(n - 1, 0, a1)
            copy_head(HEADS1 - 1, 0, a1)

            act.wait_ge(att_out, PAIRS1)
            for i in (GROUP_A, GROUP_F, GROUP_M):
                square(i)
            for i in (GROUP_A, GROUP_F, GROUP_M):
                rsqrt(i)
                round_h(i)

            def copy_units(ph):
                per = ph.per_unit

                def leave_unit(step):
                    u = (step.j + 1) // per - 1
                    act.wait_ge(chunk_done, step.n(lambda c: ph.chunk0 + c + 1))
                    w = 512 // per
                    to = e0["y"][:, bass.ds(step.n(lambda c: ((c + 1) // per - 1) * w), w)]
                    leave(nc.scalar.activation(to, lin[(ph.unit0 + u) % 2][:, 0:w], ACT.Copy), ph.unit0 + u)
                return leave_unit

            ph = PH["w_out"]
            out_unit = copy_units(ph)
            for c in range(ph.n):
                hi(ph.chunk0 + c + 1)
                if c:
                    out_unit(Step(c - 1))
            out_unit(Step(ph.n - 1))
            units_done(act, ph.unit0 + ph.units)
            square(POST)
            rsqrt(POST)
            act.wait_ge(x_ready, 1)
            norm_h(FFNPRE)

            ph = PH["up"]
            cw, cb = COLS["conv_w"][0], COLS["conv_b"][0]

            def at_col(v):
                return cols[:, bass.ds(v, 1)]

            def conv_start(step):
                j = step.j - 1
                act.wait_ge(chunk_done, step.n(lambda c: ph.chunk0 + c))
                if j >= 2:
                    act.wait_ge(hid_ready, step.n(lambda c: c - 2))
                for s in range(2):
                    ins = nc.scalar.activation(
                        ff["u"][:, 512 * (j % 2) + S * s:512 * (j % 2) + S * s + S],
                        lin[(ph.unit0 + j) % 2][:, S * s:S * s + S], ACT.Identity,
                        scale=at_col(step.n(lambda c: cw + 88 + 2 * (c - 1) + s)),
                        bias=at_col(step.n(lambda c: cb + 2 * (c - 1) + s)))
                ins.then_inc(conv_in, 1)

            def gelu(step):
                j = step.j - 2
                act.wait_ge(lin_free[(ph.unit0 + j) % 2], step.n(lambda c: (ph.unit0 + c - 2) // 2 + 1))
                nc.scalar.activation(ff["g"][:, S * (j % 2):S * (j % 2) + S],
                                     ff["u"][:, 512 * (j % 2):512 * (j % 2) + S], ACT.Gelu_apprx_tanh)\
                    .then_inc(gelu_ready, 1)

            def round_hid(step, lag, unit0=None):
                j = step.j - lag
                if unit0 is None:
                    act.wait_ge(hid_ready, step.n(lambda c: c - lag + 1))
                else:
                    act.wait_ge(lin_free[(unit0 + j) % 2], step.n(lambda c: (unit0 + c - lag) // 2 + 1))
                nc.scalar.activation(hid_hi[:, bass.ds(step.n(lambda c: (c - lag) * S), S)],
                                     ff["hid"][:, S * (j % 2):S * (j % 2) + S], ACT.Copy).then_inc(hid_hh, 1)

            def up_step(step):
                c = step.j
                if c < ph.n:
                    hi(ph.chunk0 + c + 1, step if step.i is not None else None, ph)
                if c >= 2:
                    gelu(step)
                if 1 <= c <= ph.n:
                    conv_start(step)
                if c >= 2:
                    round_hid(step, 2)

            steps(act, ph.n, 2, 1, up_step)
            up_step(Step(ph.n))
            up_step(Step(ph.n + 1))

            ph = PH["down"]
            out_unit = copy_units(ph)

            def down_step(ph, step, out_unit):
                hi(ph.chunk0 + step.j + 1, step if step.i is not None else None, ph)
                if out_unit is not None and step.j >= 2 and step.j % 2 == 0:
                    out_unit(Step(step.j - 1, step.i))

            steps(act, ph.n, 4, 1, lambda s: down_step(ph, s, out_unit))
            out_unit(Step(ph.n - 1))
            units_done(act, ph.unit0 + ph.units)
            square(FFNPOST)
            rsqrt(FFNPOST)
            act.wait_ge(x_ready, 2)

            norm_h(L0)
            ph = PH["qkv"]

            def qkv_unit(c):
                act.wait_ge(chunk_done, ph.chunk0 + c + 1)
                bank = lin[(ph.unit0 + c) % 2]
                if c == 0:
                    act.wait_ge(h_tiles, tiles_before(L0F))
                if c < 8:
                    to = a2["q" if c < 4 else "k"][:, c % 4 * 512:c % 4 * 512 + 512]
                    ins = nc.scalar.activation(to, bank[:, :], ACT.Copy, scale=HD ** -0.5 if c < 4 else 1.0)
                else:
                    to = v2[:, :, (c - 8) * S:(c - 7) * S]
                    ins = nc.scalar.activation(to, v3(bank[:, :], 2), ACT.Copy)
                leave(ins, ph.unit0 + c)

            for c in range(ph.n):
                hi(ph.chunk0 + c + 1)
                if c:
                    qkv_unit(c - 1)
            qkv_unit(ph.n - 1)

            def round_pair(j, pair):
                act.wait_ge(pv, HEADS1 + 2 * j + 2)
                nc.scalar.activation(h_hi[:, j * S:(j + 1) * S], att[pair % 2][:, 0:S], ACT.Copy).then_inc(o_hi, 1)

            for n in range(SB_HEADS + 1):
                if n < SB_HEADS:
                    e = two(a2["e"], n)
                    act.wait_ge(z_ready, n + 1)
                    if n >= 2:
                        act.wait_ge(lm_ready, n - 1)
                    link(nc.scalar.activation(e, sco[n % 2][:, 0:384], ACT.Abs))
                    link(nc.scalar.activation(e, e, ACT.Exp, scale=-1.0))
                    nc.scalar.activation(e, e, ACT.Ln, bias=ones[:, 0:1]).then_inc(z_ln, 1)
                if n:
                    act.wait_ge(z_masked, n)
                    if n >= 3:
                        act.wait_ge(pv, HEADS1 + n - 2)
                    nc.scalar.activation(two(a2["pT"], n - 1), two(a2["s"], n - 1), ACT.Exp).then_inc(stick, 1)
                if n >= 3 and n % 2:
                    round_pair((n - 3) // 2, PAIRS1 + (n - 3) // 2)
            round_pair(3, PAIRS1 + 3)
            base = HEADS1
            for n in range(HEADS2):
                exp_head(n, base, a2, None)
                if n:
                    act.wait_ge(trans, base + n)
                    act.wait_ge(pv, HEADS1 + SB_HEADS + max(n - 2, 0))
                    nc.scalar.activation(two(a2["pT"], n - 1), tra[(n - 1) % 2][:, 0:384], ACT.Copy).then_inc(trans_out, 1)
                if n >= 3 and n % 2:
                    j = PAIRS_SB + (n - 3) // 2
                    round_pair(j, PAIRS1 + j)
            n = HEADS2
            act.wait_ge(trans, base + n)
            act.wait_ge(pv, HEADS1 + SB_HEADS + n - 2)
            nc.scalar.activation(two(a2["pT"], n - 1), tra[(n - 1) % 2][:, 0:384], ACT.Copy).then_inc(trans_out, 1)
            round_pair(7, PAIRS1 + 7)

            ph = PH["att_o"]
            for c in range(ph.n):
                hi(ph.chunk0 + c + 1)

            def swiglu(ph):
                def silu(step):
                    j = step.j - 1
                    act.wait_ge(chunk_done, step.n(lambda c: ph.chunk0 + c))
                    nc.scalar.activation(ff["g"][:, S * (j % 2):S * (j % 2) + S], lin[(ph.unit0 + j) % 2][:, 0:S], ACT.Silu)\
                        .then_inc(gelu_ready, 1)

                def step_(step):
                    hi(ph.chunk0 + step.j + 1, step if step.i is not None else None, ph)
                    if step.j >= 1:
                        silu(step)
                        round_hid(step, 1, ph.unit0)

                steps(act, ph.n, 2, 1, step_)
                silu(Step(ph.n))
                round_hid(Step(ph.n), 1, ph.unit0)

            def down(ph):
                steps(act, ph.n, 0, 1, lambda s: down_step(ph, s, None))

            units_done(act, PH["att_o"].unit0 + PH["att_o"].units)
            norm_h(L0F)
            swiglu(PH["gu0"])
            down(PH["dn0"])

            units_done(act, PH["dn0"].unit0 + PH["dn0"].units)
            norm_h(L1)
            ph = PH["ret_in"]

            def ret_unit(step):
                c = step.j - 1
                bank = lin[(ph.unit0 + c) % 2]
                act.wait_ge(chunk_done, step.n(lambda c: ph.chunk0 + c))
                if c < 16:
                    to = v3(rt["v"], 2)[:, :, (c - 8) * S:(c - 7) * S]
                    ins = nc.scalar.activation(to, v3(bank[:, :], 2), ACT.Copy)
                else:
                    ins = nc.scalar.activation(rt["g"][:, (c - 16) * 512:(c - 15) * 512], bank[:, :], ACT.Silu)
                leave(ins, ph.unit0 + c)

            for c in range(ph.n):
                hi(ph.chunk0 + c + 1)
                if c > 8:
                    ret_unit(Step(c))
            ret_unit(Step(ph.n))

            for h in range(RET_H):
                gs = gn_stat[:, 32 * (h % 2):32 * (h % 2) + 32]
                act.wait_ge(ret_var, h + 1)
                link(nc.scalar.activation(gs[:, 18:20], gs[:, 16:18], ACT.Ln))
                nc.scalar.activation(gs[:, 20:22], gs[:, 18:20], ACT.Exp, scale=-0.5).then_inc(ret_rsq, 1)
                act.wait_ge(ret_rstd, h + 1)
                if h:
                    act.wait_ge(ret_tr, 2 * h)
                for q in range(2):
                    nc.scalar.activation(rt["on"][:, 512 * q:512 * q + 512], (tra + att)[2 * (h % 2) + q][:, :], ACT.Identity,
                                         scale=gs[:, 24 + q:25 + q], bias=gs[:, 28 + q:29 + q]).then_inc(ret_norm, 1)
                for m in range(2):
                    act.wait_ge(ret_y, 2 * h + m + 1)
                    t = (4 * h + 2 * m) * S
                    nc.scalar.activation(hid_hi[:, t:t + 512], rt["o"] if m == 0 else rt["rot"], ACT.Copy).then_inc(ret_hh, 1)

            ph = PH["ret_o"]
            for c in range(ph.n):
                hi(ph.chunk0 + c + 1)
            units_done(act, PH["ret_o"].unit0 + PH["ret_o"].units)
            norm_h(L1F)
            swiglu(PH["gu1"])
            down(PH["dn1"])
            units_done(act, PH["dn1"].unit0 + PH["dn1"].units)
            square(FINAL)
            rsqrt(FINAL)

        @block.tensor
        def _(pe):
            def three(out, w, hc, lc, start, stop):
                nc.tensor.matmul(out, w[0], hc, start=start, stop=False, skip_group_check=True)
                nc.tensor.matmul(out, w[0], lc, start=False, stop=False, skip_group_check=True)
                return nc.tensor.matmul(out, w[1], hc, start=False, stop=stop, skip_group_check=True)

            def weights(chunk, step, ph):
                pe.wait_ge(split_ready, step.n(lambda c: ph.chunk0 + c + 1))
                s = chunk % SPLIT_SLOTS
                return w_hi[s], w_lo[s]

            def by_feature(ph, step, first_tiles=None, rhs=None, k0=lambda c: 0):
                j = step.j
                f = lambda c: (c + ph.per_unit) // ph.per_unit - 1
                whi, wlo = weights(ph.chunk0 + j, step, ph)
                if j % ph.per_unit == 0:
                    unit_free(pe, ph, step, f)
                bank = lin[(ph.unit0 + f(j)) % 2]
                r_hi, r_lo = rhs or (h_hi, h_lo)
                width = ph.nb * P
                for b in range(ph.nb):
                    for k in range(ph.kt):
                        if first_tiles is not None and b == 0:
                            pe.wait_ge(first_tiles[0], first_tiles[1] + k + 1)
                        cut = slice(k * width + b * P, k * width + b * P + P)
                        t = slice((k0(j) + k) * S, (k0(j) + k + 1) * S)
                        ins = three(bank[:, b * S:(b + 1) * S], (whi[:, cut], wlo[:, cut]), r_hi[:, t], r_lo[:, t],
                                    start=(k == 0 and j % ph.per_unit == 0),
                                    stop=(k == ph.kt - 1 and j % ph.per_unit == ph.per_unit - 1))
                ins.then_inc(chunk_done, 1)

            def by_row(ph, step, nb=2):
                j = step.j
                whi, wlo = weights(ph.chunk0 + j, step, ph)
                unit_free(pe, ph, step, lambda c: c)
                bank = lin[(ph.unit0 + j) % 2]
                width = nb * P
                for r in range(2):
                    for k in range(ph.kt):
                        w = slice(k * width, (k + 1) * width)
                        t = slice(k * S + r * P, k * S + r * P + P)
                        out = bank[:, r * S:r * S + width]
                        nc.tensor.matmul(out, h_hi[:, t], whi[:, w], start=k == 0, stop=False, skip_group_check=True)
                        nc.tensor.matmul(out, h_hi[:, t], wlo[:, w], start=False, stop=False, skip_group_check=True)
                        ins = nc.tensor.matmul(out, h_lo[:, t], whi[:, w], start=False, stop=k == ph.kt - 1,
                                               skip_group_check=True)
                ins.then_inc(chunk_done, 1)

            def sum_squares(i):
                sq, nt = NORM[i][1], NORM_TILES[i]
                pe.wait_ge(sq_ready, i + 1)
                for r in range(2):
                    for k in range(nt):
                        ins = nc.tensor.matmul(ssum[:, r:r + 1], sq[:, k * S + r * P:k * S + r * P + P], ones[:, 0:1],
                                               start=k == 0, stop=k == nt - 1)
                ins.then_inc(ssum_ready, 1)

            def spread(i):
                if i:
                    pe.wait_ge(r_used, i)
                for r in range(2):
                    pe.wait_ge(diag_ready, 2 * i + r + 1)
                    ins = nc.tensor.matmul(rbc[:, r * P:(r + 1) * P], ones[:, 0:P], diag[:, r * P:(r + 1) * P],
                                           start=True, stop=True)
                ins.then_inc(rbc_ready, 1)

            def norm(i):
                sum_squares(i)
                spread(i)

            def modulation(step, f):
                a = f(step.j)
                pe.wait_ge(ada_mul, step.n(lambda c: f(c) + 1))
                if a >= 2:
                    pe.wait_ge(ada_out, step.n(lambda c: f(c) - 1))
                for b in range(2):
                    ins = nc.tensor.matmul(ada_ps[a % 2][:, b:b + 1],
                                           ada_acc[a % 2][:, b * P:(b + 1) * P], ones[:, 0:1], start=True, stop=True)
                ins.then_inc(ada_sum, 1)

            def modulations(ph, step):
                pieces = ADA_STEPS.get(ph.name, lambda c: 0)
                if step.j:
                    for m in range(pieces(step.j - 1)):
                        modulation(step, lambda c, m=m: ada_before(ph.name, c - 1) + m)

            def rotate(n, perm, src, width=S):
                return nc.tensor.matmul(tra[n % 2][:, 0:width], perm, src, start=True, stop=True)

            pe.wait_ge(rel_ready, 1)
            pe.wait_ge(tab1_in, 16)
            for n in range(8):
                if n >= 4:
                    pe.wait_ge(band_ready, n - 3)
                nc.tensor.matmul((tra + att)[n % 4][:, 0:BAND], rel_rows[:, n * P:(n + 1) * P],
                                 a1["onehot"][0:BUCKETS + 1, :], start=True, stop=True).then_inc(band_ps, 1)
            pe.wait_ge(ones_ready, 1)
            norm(PRE)
            ph = PH["w_in"]
            pe.wait_ge(band_ready, 8)
            for c in range(ph.n):
                modulations(ph, Step(c))
                if c < 7:
                    by_feature(ph, Step(c), (h_tiles, 0) if c == 0 else None)
                else:
                    by_row(ph, Step(c), 2 if c == 7 else 1)
                if c == 3:
                    sum_squares(QLAT)
                if c == 4:
                    spread(QLAT)
                    sum_squares(KVLAT)
                    units_done(pe, 2)
                    rotate(0, a1["perm"], a1["kr"]).then_inc(rot_ready, 1)
                if c == 5:
                    spread(KVLAT)
            modulations(ph, Step(ph.n))

            ph = PH["mla"]
            whi, wlo = weights(ph.chunk0, Step(0), ph)
            pe.wait_ge(h_tiles, tiles_before(GROUP_A))
            up, wide = 2 * 384, 384

            def latent(unit, at, out_cols, w0, tiles, width):
                for n, k in enumerate(tiles):
                    w = slice(w0 + n * width, w0 + n * width + P)
                    t = slice(k * S, (k + 1) * S)
                    ins = three(lin[(ph.unit0 + unit) % 2][:, at * S:(at + 1) * S], (whi[:, w], wlo[:, w]),
                                hid_hi[:, t], hid_lo[:, t], n == 0, n == len(tiles) - 1)
                return ins

            def latent_v(unit, at, r):
                t = slice(2 * S + r * P, 2 * S + r * P + P)
                w = slice(up + 2 * P, up + 4 * P)
                out = lin[(ph.unit0 + unit) % 2][:, at * S:(at + 1) * S]
                nc.tensor.matmul(out, hid_hi[:, t], whi[:, w], start=True, stop=False, skip_group_check=True)
                nc.tensor.matmul(out, hid_hi[:, t], wlo[:, w], start=False, stop=False, skip_group_check=True)
                return nc.tensor.matmul(out, hid_lo[:, t], whi[:, w], start=False, stop=True, skip_group_check=True)

            for u in range(MLA_UNITS):
                unit_free(pe, ph, Step(u), lambda c: c)
                if u == 0:
                    latent(u, 0, None, 0, (0, 1), wide)
                    ins = latent(u, 1, None, P, (0, 1), wide)
                elif u == 1:
                    latent(u, 0, None, 2 * P, (0, 1), wide)
                    ins = latent(u, 1, None, up, (2,), P)
                elif u == 2:
                    latent(u, 0, None, up + P, (2,), P)
                    ins = latent_v(u, 1, 0)
                else:
                    ins = latent_v(u, 0, 1)
                ins.then_inc(mla_units if u < MLA_UNITS - 1 else chunk_done, 1)
            units_done(pe, ph.unit0 + 2)
            rotate(1, a1["perm"], a1["qr"]).then_inc(rot_ready, 1)

            def score_head(n, base, head):
                out = sco[n % 2]
                if n >= 2:
                    pe.wait_ge(scores_read, base + n - 1)
                first, todo = True, []
                for q, k in head["parts"]:
                    todo.append((out[:, 0:P], q[:, 0:P], k[:, 0:P]))
                    todo.append((out[:, P:384], q[:, P:S], k))
                if head["decay"] is not None:
                    pick = ident[0:4, head["decay"]:head["decay"] + 1]
                    f, fneg = a1["f"][0:4, :], a1["fneg"][0:4, :]
                    for o, q, k in ((out[:, 0:P], slice(0, P), slice(0, P)), (out[:, P:384], slice(P, S), slice(0, S))):
                        n_k = k.stop - k.start
                        todo.append((o, f[:, q], pick.to_broadcast([4, n_k])))
                        todo.append((o, pick.to_broadcast([4, P]), fneg[:, k]))
                for m, (o, q, k) in enumerate(todo):
                    ins = nc.tensor.matmul(o, q, k, start=first, stop=m == len(todo) - 1, skip_group_check=True)
                    first = False
                ins.then_inc(scores, 1)

            def turn_head(n, base, a):
                s = two(a["s"], n)
                pe.wait_ge(probs, base + n + 1)
                if n >= 2:
                    pe.wait_ge(trans_out, base + n - 1)
                for m in range(3):
                    ins = nc.tensor.transpose(tra[n % 2][:, m * P:(m + 1) * P], s[:, m * P:(m + 1) * P], ident[:, :])
                ins.then_inc(trans, 1)

            def values(n, pT, v, pair):
                h = n % 2
                if pair >= 2 and h == 0:
                    if pair - 2 < PAIRS1:
                        pe.wait_ge(att_out, pair - 1)
                    else:
                        pe.wait_ge(o_tiles, pair - 1 - PAIRS1)
                o = att[pair % 2][HD * h:HD * h + HD, 0:S]
                nc.tensor.matmul(o, v(0), pT[:, 0:S], start=True, stop=False, skip_group_check=True)
                nc.tensor.matmul(o[:, P:S], v(1), pT[:, S:384], start=False, stop=True, skip_group_check=True)\
                    .then_inc(pv, 1)

            def softmax_heads(heads, base, a, pair0):
                score_head(0, base, heads[0])
                for n in range(len(heads) + 1):
                    if n + 1 < len(heads):
                        score_head(n + 1, base, heads[n + 1])
                    if n < len(heads):
                        turn_head(n, base, a)
                    if n:
                        pe.wait_ge(trans_out, base + n)
                        values(n - 1, two(a["pT"], n - 1), heads[n - 1]["v"], pair0 + (n - 1) // 2)

            units_done(pe, ph.unit0 + ph.units)
            pe.wait_ge(r_used, KVLAT + 1)
            pe.wait_ge(rot_done, 2)
            pe.wait_ge(f_ready, 1)
            pe.wait_ge(ada_out, ada_before("w_out", 0))
            softmax_heads(heads1, 0, a1, 0)

            pe.wait_ge(scores_read, HEADS1)
            pe.wait_ge(att_out, PAIRS1)
            for i in (GROUP_A, GROUP_F, GROUP_M):
                norm(i)
            ph = PH["w_out"]
            for c in range(ph.n):
                modulations(ph, Step(c))
                by_feature(ph, Step(c), (h_tiles, tiles_before(GROUP_A)) if c == 0 else None)
            modulations(ph, Step(ph.n))
            norm(POST)
            norm(FFNPRE)

            def up_phase(name, i):
                ph = PH[name]
                by_feature(ph, Step(0), (h_tiles, tiles_before(i)))
                steps(pe, ph.n, 1, 1, lambda s: by_feature(ph, s) if s.i is not None or s.j else None)

            def down_phase(name, base):
                ph = PH[name]

                def one(step):
                    if step.i is None and step.j < 2:
                        pe.wait_ge(hid_tiles, base + HALF * (step.j + 1))
                    modulations(ph, step)
                    by_feature(ph, step, rhs=(hid_hi, hid_lo), k0=lambda c: HALF * (c % 2))

                steps(pe, ph.n, 4, 0, one)
                modulations(ph, Step(ph.n))

            up_phase("up", FFNPRE)
            down_phase("down", 0)
            norm(FFNPOST)
            norm(L0)
            ph = PH["qkv"]
            pe.wait_ge(tab2_in, 16)
            for c in range(ph.n):
                modulations(ph, Step(c))
                if c < 8:
                    by_feature(ph, Step(c), (h_tiles, tiles_before(L0)) if c == 0 else None)
                else:
                    by_row(ph, Step(c))
                if c >= 8:
                    r = c - 8
                    units_done(pe, ph.unit0 + 8)
                    if r >= 2:
                        pe.wait_ge(rot_done, 2 + r - 1)
                    t = a2["q" if r < 2 else "k"][:, (4 + r % 2 * 2) * S:(6 + r % 2 * 2) * S]
                    rotate(r, a2["perm"], t, 512).then_inc(rot_ready, 1)
            modulations(ph, Step(ph.n))
            units_done(pe, ph.unit0 + ph.units)
            pe.wait_ge(r_used, L0 + 1)
            pe.wait_ge(ada_out, ada_before("att_o", 0))

            def stick_scores(n):
                if n >= 2:
                    pe.wait_ge(z_masked, n - 1)
                q, k = half(a2["q"], n // 2, n % 2), half(a2["k"], n // 2, n % 2)
                nc.tensor.matmul(sco[n % 2][:, 0:S], k[:, 0:P], q, start=True, stop=False, skip_group_check=True)
                nc.tensor.matmul(sco[n % 2][:, S:384], k[:, P:S], q[:, P:S], start=False, stop=False, skip_group_check=True)\
                    .then_inc(z_ready, 1)

            def stick_sums(n):
                out, lm = sco[n % 2], two(a2["lm"], n)
                pe.wait_ge(lm_ready, n + 1)
                nc.tensor.matmul(out[:, 0:S], a2["tri"], lm[:, 0:S], start=False, stop=False, skip_group_check=True)
                nc.tensor.matmul(out[:, S:384], a2["tri"], lm[:, S:384], start=False, stop=False, skip_group_check=True)
                nc.tensor.matmul(out[:, P:S], a2["negones"], lm[:, S:384], start=False, stop=True, skip_group_check=True)\
                    .then_inc(z_sum, 1)

            stick_scores(0)
            stick_scores(1)
            for n in range(SB_HEADS + 1):
                if n < SB_HEADS:
                    stick_sums(n)
                if n:
                    pe.wait_ge(stick, n)
                    values(n - 1, two(a2["pT"], n - 1), lambda kt, n=n: v2[:, kt, HD * (n - 1):HD * n], PAIRS1 + (n - 1) // 2)
                if n + 2 < SB_HEADS:
                    stick_scores(n + 2)
            pe.wait_ge(z_masked, SB_HEADS)
            pe.wait_ge(rot_done, 6)
            softmax_heads(heads2, HEADS1, a2, PAIRS1 + PAIRS_SB)

            ph = PH["att_o"]
            for c in range(ph.n):
                modulations(ph, Step(c))
                by_feature(ph, Step(c), (o_tiles, 0) if c == 0 else None)
            modulations(ph, Step(ph.n))
            pe.wait_ge(scores_read, HEADS1 + HEADS2)
            norm(L0F)
            up_phase("gu0", L0F)
            down_phase("dn0", FT)

            norm(L1)
            ph = PH["ret_in"]
            for c in range(ph.n):
                if 8 <= c < 16:
                    by_row(ph, Step(c))
                else:
                    by_feature(ph, Step(c), (h_tiles, tiles_before(L1)) if c == 0 else None)
            units_done(pe, ph.unit0 + ph.units)
            pe.wait_ge(r_used, L1 + 1)
            pe.wait_ge(ada_out, 2 * ADA_PIECES)
            rv = v3(rt["v"], 2)

            def ret_scores(h):
                out = sco[h % 2]
                if h >= 2:
                    pe.wait_ge(ret_inner, h - 1)
                for kt, (a, b) in enumerate(((0, S), (S, 384))):
                    for d in range(2):
                        t = (2 * h + d) * S
                        ins = nc.tensor.matmul(out[:, a:b], rt["k"][:, t + kt * P:t + kt * P + P], rt["q"][:, t + kt * P:t + S],
                                               start=kt == 0 and d == 0, stop=kt == 1 and d == 1, skip_group_check=True)
                ins.then_inc(ret_s, 1)

            ret_scores(0)
            for h in range(RET_H):
                if h + 1 < RET_H:
                    ret_scores(h + 1)
                inner = two(rt["inner"], h)
                pe.wait_ge(ret_inner, h + 1)
                if h >= 2:
                    pe.wait_ge(ret_norm, 2 * (h - 1))
                o = (tra + att)[2 * (h % 2):2 * (h % 2) + 2]
                v = slice(h * RET_DV, (h + 1) * RET_DV)
                nc.tensor.matmul(o[0][:, :], inner[:, 0:P], rv[:, 0, v], start=True, stop=True).then_inc(ret_o, 1)
                nc.tensor.matmul(o[1][:, :], inner[:, P:S], rv[:, 0, v], start=True, stop=False)
                nc.tensor.matmul(o[1][:, :], inner[:, S:384], rv[:, 1, v], start=False, stop=True).then_inc(ret_o, 1)
                pe.wait_ge(ret_norm, 2 * h + 2)
                for m in range(2):
                    if h:
                        pe.wait_ge(ret_y, 2 * (h - 1) + m + 1)
                    for b in range(2):
                        for q in range(2):
                            src = rt["on"][:, 512 * q + (2 * m + b) * P:512 * q + (2 * m + b + 1) * P]
                            ins = nc.tensor.transpose(lin[m][:, b * S + q * P:b * S + q * P + P], src, ident[:, :])
                    ins.then_inc(ret_tr, 1)

            ph = PH["ret_o"]
            pe.wait_ge(ret_tiles, 8)
            for c in range(ph.n):
                by_feature(ph, Step(c), rhs=(hid_hi, hid_lo))
            norm(L1F)
            up_phase("gu1", L1F)
            down_phase("dn1", 2 * FT)
            norm(FINAL)

        @block.vector
        def _(dve):
            chain = [0]

            def link(ins):
                chain[0] += 1
                ins.then_inc(dve_chain, 1)
                dve.wait_ge(dve_chain, chain[0])

            tt, stt, ts = nc.vector.tensor_tensor, nc.vector.scalar_tensor_tensor, nc.vector.tensor_scalar

            def lo(chunk, step=None, ph=None):
                if chunk >= CHUNKS:
                    return
                of, c = phase_of(chunk)
                n = of.size(c)
                at = (lambda f: f(chunk)) if step is None else (lambda f: step.n(lambda c: f(ph.chunk0 + c + 1)))
                dve.wait_ge(hi_ready, at(lambda k: k + 1))
                s = chunk % SPLIT_SLOTS
                tt(w_lo[s][:, 0:n], raw[chunk % RAW_SLOTS][:, 0:n], w_hi[s][:, 0:n].bitcast(F32), ALU.subtract)\
                    .then_inc(split_ready, 1)

            def rstd(i):
                n = NORM_TILES[i] * P
                dve.wait_ge(ssum_ready, i + 1)
                ts(stat[:, 0:2], ssum, 1.0 / n, EPS, ALU.mult, ALU.add).then_inc(ms_ready, 1)
                dve.wait_ge(rsq_ready, i + 1)
                link(tt(stat[:, 6:8], stat[:, 4:6], stat[:, 4:6], ALU.mult))
                link(tt(stat[:, 8:10], stat[:, 6:8], stat[:, 0:2], ALU.mult))
                link(ts(stat[:, 10:12], stat[:, 8:10], -0.5, 1.5, ALU.mult, ALU.add))
                link(tt(stat[:, 12:14], stat[:, 10:12], stat[:, 4:6], ALU.mult))
                if i:
                    dve.wait_ge(rbc_ready, i)
                for r in range(2):
                    ts(diag[:, r * P:(r + 1) * P], ident[:, :], stat[:, 12 + r:13 + r], None, ALU.mult).then_inc(diag_ready, 1)

            def scaled(i, dst):
                src, nt = NORM[i][0], NORM_TILES[i]
                dve.wait_ge(rbc_ready, i + 1)
                return tt(v3(dst, nt), v3(src, nt), over(rbc, nt), ALU.mult)

            def norm_h(i):
                _, _, tmp, gain, shift, hi_, lo_ = NORM[i]
                rstd(i)
                scaled(i, tmp).then_inc(r_used, 1)
                dve.wait_ge(r_used, i + 1)
                for k in range(NORM_TILES[i]):
                    cut = slice(k * S, (k + 1) * S)
                    dve.wait_ge(hh_ready, tiles_before(i) + k + 1)
                    if shift(k) is None:
                        ins = stt(lo_[:, cut], tmp[:, cut], gain(k), hi_[:, cut].bitcast(F32), ALU.mult, ALU.subtract)
                    else:
                        link(ts(tmp[:, cut], tmp[:, cut], gain(k), shift(k), ALU.mult, ALU.add))
                        ins = tt(lo_[:, cut], tmp[:, cut], hi_[:, cut].bitcast(F32), ALU.subtract)
                    ins.then_inc(h_tiles, 1)

            def norm_residual(i):
                src, gain = NORM[i][0], NORM[i][3]
                rstd(i)
                scaled(i, src).then_inc(r_used, 1)
                dve.wait_ge(r_used, i + 1)
                for k in range(DT):
                    cut = slice(k * S, (k + 1) * S)
                    ins = stt(x[:, cut], src[:, cut], gain(k), x[:, cut], ALU.mult, ALU.add)
                ins.then_inc(x_ready, 1)

            pieces_out = [0]

            def piece(step, f):
                a = f(step.j)
                acc, w = ada_acc[a % 2], v3(ada_raw[a % 2], DT)
                dve.wait_ge(ada_in[a % 2], step.n(lambda c: 16 * (f(c) // 2 + 1)))
                if a - 2 >= pieces_out[0]:
                    piece_out(step, lambda c: f(c) - 2)
                ts(acc[:, :], w[:, 0, :], cond_silu[:, 0:1], None, ALU.mult).then_inc(ada_step, 1)
                for k in range(1, DT):
                    dve.wait_ge(ada_step, step.n(lambda c: f(c) * (DT - 1) + k))
                    ins = stt(acc[:, :], w[:, k, :], cond_silu[:, k:k + 1], acc[:, :], ALU.mult, ALU.add)
                    ins.then_inc(ada_step if k < DT - 1 else ada_mul, 1)

            def piece_out(step, f):
                a = f(step.j)
                dve.wait_ge(ada_sum, step.n(lambda c: f(c) + 1))
                o = COLS["ada_b"][0]
                tt(mod[:, bass.ds(step.n(lambda c: 2 * f(c)), 2)], ada_ps[a % 2][:, 0:2],
                   cols[:, bass.ds(step.n(lambda c: o + 2 * f(c)), 2)], ALU.add).then_inc(ada_out, 1)

            def pieces(ph, step):
                for m in range(ADA_STEPS.get(ph.name, lambda c: 0)(step.j)):
                    piece(step, lambda c, m=m: ada_before(ph.name, c) + m)

            def flush_pieces(a):
                for m in (a - 2, a - 1):
                    piece_out(Step(0), lambda c, m=m: m)
                pieces_out[0] = a

            link(nc.vector.memset(ones[:, :], 1.0))
            dve.wait_ge(cols_in, 16)
            for n in range(8):
                ins = ts(rel_rows[:, n * P:(n + 1) * P], ones[0:BUCKETS + 1, 0:P], col("rel", n, 1, BUCKETS + 1), None, ALU.mult)
            ins.then_inc(rel_ready, 1)
            nc.vector.memset(diag[:, 0:1], 0.0).then_inc(ones_ready, 1)
            dve.wait_ge(ident_in, 16)
            dve.wait_ge(cond_ready, 1)
            dve.wait_ge(ones_ready, 1)
            dve.wait_ge(x_in, 16)
            norm_h(PRE)
            lo(0)
            ph = PH["w_in"]

            def rotary(n, tile, cos, sin, nt):
                dve.wait_ge(rot_ready, n + 1)
                rot = tra[ROT_BANK[n]][:, 0:nt * S]
                link(tt(v3(tile, nt), v3(tile, nt), over(cos, nt), ALU.mult))
                tmp = ROT_TMP[n]
                link(tt(v3(tmp, nt), v3(rot, nt), over(sin, nt), ALU.mult))
                tt(tile, tile, tmp, ALU.add).then_inc(rot_done, 1)

            ROT_BANK = [0, 1, 0, 1, 0, 1]
            ROT_TMP = [a1["pT"][:, 0:S]] * 2 + [a2["rot"]] * 4
            for c in range(ph.n):
                lo(ph.chunk0 + c + 1)
                if c == 4:
                    rstd(QLAT)
                if c == 5:
                    _, _, tmp, gain, _, hi_, lo_ = NORM[QLAT]
                    scaled(QLAT, tmp).then_inc(r_used, 1)
                    dve.wait_ge(r_used, QLAT + 1)
                    for k in range(2):
                        cut = slice(k * S, (k + 1) * S)
                        dve.wait_ge(hh_ready, tiles_before(QLAT) + k + 1)
                        stt(lo_[:, cut], tmp[:, cut], gain(k), hi_[:, cut].bitcast(F32), ALU.mult, ALU.subtract)\
                            .then_inc(h_tiles, 1)
                    rstd(KVLAT)
                if c == 6:
                    _, _, tmp, gain, _, hi_, lo_ = NORM[KVLAT]
                    scaled(KVLAT, tmp).then_inc(r_used, 1)
                    dve.wait_ge(r_used, KVLAT + 1)
                    dve.wait_ge(hh_ready, tiles_before(KVLAT) + 1)
                    stt(lo_, tmp, gain(0), hi_.bitcast(F32), ALU.mult, ALU.subtract).then_inc(h_tiles, 1)
                    rotary(0, a1["kr"], a1["cos"], a1["sin"], 1)
                pieces(ph, Step(c))
            dve.wait_ge(f_ln, 1)
            link(stt(gate_tmp[:, 4 * S:5 * S], gate_tmp[:, 0:S], 0.0, gate_tmp[:, 3 * S:4 * S], ALU.min, ALU.subtract))
            link(nc.vector.tensor_tensor_scan(a1["f"][0:4, :], ones[0:4, :], gate_tmp[:, 4 * S:5 * S], 0.0, ALU.mult, ALU.add))
            ts(a1["fneg"][0:4, :], a1["f"][0:4, :], -1.0, None, ALU.mult).then_inc(f_ready, 1)
            flush_pieces(ada_before("w_out", 0))
            lo(PH["w_out"].chunk0)
            rotary(1, a1["qr"], a1["cos"], a1["sin"], 1)

            def score_head(n, base, head, a):
                hs = head_stat[:, 16 * (n % 2):16 * (n % 2) + 16]
                s, out = two(a["s"], n), sco[n % 2]
                dve.wait_ge(scores, base + n + 1)
                if n >= 2:
                    dve.wait_ge(trans, base + n - 1)
                first = NEG * 3 if head["sink"] is None else head["sink"]
                nc.vector.tensor_tensor_reduce(s[:, 0:P], out[:, 0:P], head["bias"][0], 1.0, first, ALU.add, ALU.max, hs[:, 0:1])
                link(nc.vector.tensor_tensor_reduce(s[:, P:384], out[:, P:384], head["bias"][1], 1.0, first, ALU.add, ALU.max,
                                                    hs[:, 1:2]))
                ts(hs[:, 2:4], hs[:, 0:2], -1.0, None, ALU.mult).then_inc(scores_read, 1)

            def weigh_head(n, base, head, a):
                hs = head_stat[:, 16 * (n % 2):16 * (n % 2) + 16]
                s = two(a["s"], n)
                dve.wait_ge(exps, base + n + 1)
                total = hs[:, 4:6]
                if head["sink"] is not None:
                    link(tt(hs[:, 8:10], hs[:, 4:6], hs[:, 6:8], ALU.add))
                    total = hs[:, 8:10]
                link(nc.vector.reciprocal(hs[:, 10:12], total))
                ts(s[:, 0:P], s[:, 0:P], hs[:, 10:11], None, ALU.mult)
                ts(s[:, P:384], s[:, P:384], hs[:, 11:12], None, ALU.mult).then_inc(probs, 1)

            def softmax_heads(heads, base, a, pair_out):
                score_head(0, base, heads[0], a)
                for n in range(len(heads)):
                    if n + 1 < len(heads):
                        score_head(n + 1, base, heads[n + 1], a)
                    weigh_head(n, base, heads[n], a)
                    if n >= 3 and n % 2:
                        pair_out((n - 3) // 2)
                pair_out(len(heads) // 2 - 1)

            def pair_to_mixed(j):
                dve.wait_ge(pv, 2 * j + 2)
                nc.vector.tensor_copy(a1["mixed"][:, j * S:(j + 1) * S], att[j % 2][:, 0:S]).then_inc(att_out, 1)

            dve.wait_ge(bias_in, 16)
            softmax_heads(heads1, 0, a1, pair_to_mixed)
            for i in (GROUP_A, GROUP_F, GROUP_M):
                norm_h(i)
            ph = PH["w_out"]
            for c in range(ph.n):
                lo(ph.chunk0 + c + 1)
                pieces(ph, Step(c))
            flush_pieces(ada_before("down", 0))
            norm_residual(POST)
            dve.wait_ge(x_ready, 1)
            norm_h(FFNPRE)

            ph = PH["up"]
            cw = COLS["conv_w"][0]

            def taps(step):
                j = step.j - 1
                bank = lin[(ph.unit0 + j) % 2]
                dve.wait_ge(conv_in, step.n(lambda c: c))
                for back in (1, 2):
                    for s in range(2):
                        u = ff["u"][:, 512 * (j % 2) + S * s:512 * (j % 2) + S * s + S]
                        w = cols[:, bass.ds(step.n(lambda c: cw + 44 * (2 - back) + 2 * (c - 1) + s), 1)]
                        if back == 2:
                            dve.wait_ge(conv_tap, step.n(lambda c: 2 * (c - 1) + s + 1))
                        ins = stt(u[:, back:S], bank[:, S * s:S * s + S - back], w, u[:, back:S], ALU.mult, ALU.add)
                        if back == 1:
                            ins.then_inc(conv_tap, 1)
                ins.then_inc(lin_free[(ph.unit0 + j) % 2], 1)

            def product(step, lag, base, up):
                j = step.j - lag
                dve.wait_ge(gelu_ready, step.n(lambda c: base + c - lag + 1))
                return tt(ff["hid"][:, S * (j % 2):S * (j % 2) + S], up, ff["g"][:, S * (j % 2):S * (j % 2) + S], ALU.mult)

            def rest(step, lag, base):
                j = step.j - lag
                dve.wait_ge(hid_hh, step.n(lambda c: base + c - lag + 1))
                cut = bass.ds(step.n(lambda c: (c - lag) * S), S)
                tt(hid_lo[:, cut], ff["hid"][:, S * (j % 2):S * (j % 2) + S], hid_hi[:, cut].bitcast(F32), ALU.subtract)\
                    .then_inc(hid_tiles, 1)

            def u_up(step, lag):
                j = step.j - lag
                return ff["u"][:, 512 * (j % 2) + S:512 * (j % 2) + 2 * S]

            def up_step(step):
                c = step.j
                if c < ph.n:
                    lo(ph.chunk0 + c + 1, step if step.i is not None else None, ph)
                if c >= 2:
                    product(step, 2, 0, u_up(step, 2)).then_inc(hid_ready, 1)
                if 1 <= c <= ph.n:
                    taps(step)
                if c >= 2:
                    rest(step, 2, 0)

            steps(dve, ph.n, 2, 1, up_step)
            up_step(Step(ph.n))
            up_step(Step(ph.n + 1))

            ph = PH["down"]

            def down_step(ph, step, out):
                lo(ph.chunk0 + step.j + 1, step if step.i is not None else None, ph)
                if out is not None and step.j >= 2 and step.j % 2 == 0:
                    out(Step(step.j - 1, step.i))
                pieces(ph, step)

            steps(dve, ph.n, 4, 1, lambda s: down_step(ph, s, None))
            flush_pieces(ADA_PIECES)
            norm_residual(FFNPOST)

            def gains(layer):
                for w, which in ((0, 1), (1, 4)):
                    i = 2 * layer + w
                    ins = stt(gscale[:, 8 * i:8 * i + 8], mod[:, 48 * layer + 8 * which:48 * layer + 8 * which + 8], 1.0,
                              col("norms2", 8 * i, 8), ALU.add, ALU.mult)
                    link(ins)

            def residual_units(ph, layer, which):
                w = 2 // ph.per_unit if ph.nb == 2 else 1

                def out(step):
                    u = (step.j + 1) // ph.per_unit - 1
                    dve.wait_ge(chunk_done, step.n(lambda c: ph.chunk0 + c + 1))
                    for b in range(w):
                        k = lambda c, b=b: ((c + 1) // ph.per_unit - 1) * w + b
                        xk = x[:, bass.ds(step.n(lambda c: k(c) * S), S)]
                        gate = mod[:, bass.ds(step.n(lambda c: 48 * layer + 8 * which + k(c)), 1)]
                        ins = stt(xk, lin[(ph.unit0 + u) % 2][:, b * S:(b + 1) * S], gate, xk, ALU.mult, ALU.add)
                    leave(ins, ph.unit0 + u)
                return out

            dve.wait_ge(ada_out, ADA_PIECES)
            dve.wait_ge(x_ready, 2)
            gains(0)
            norm_h(L0)
            ph = PH["qkv"]
            dve.wait_ge(tab2_in, 16)
            for c in range(ph.n):
                lo(ph.chunk0 + c + 1)
                if c >= 9:
                    r = c - 9
                    rotary(2 + r, a2["q" if r < 2 else "k"][:, (4 + r % 2 * 2) * S:(6 + r % 2 * 2) * S], a2["cos"], a2["sin"], 2)
                pieces(ph, Step(c))
            rotary(5, a2["k"][:, 6 * S:8 * S], a2["cos"], a2["sin"], 2)
            flush_pieces(ada_before("att_o", 0))

            def pair_to_split(j):
                dve.wait_ge(o_hi, j + 1)
                tt(h_lo[:, j * S:(j + 1) * S], att[(PAIRS1 + j) % 2][:, 0:S], h_hi[:, j * S:(j + 1) * S].bitcast(F32), ALU.subtract)\
                    .then_inc(o_tiles, 1)

            for n in range(SB_HEADS + 1):
                if n < SB_HEADS:
                    lm, z = two(a2["lm"], n), sco[n % 2][:, 0:384]
                    dve.wait_ge(z_ln, n + 1)
                    if n >= 2:
                        dve.wait_ge(z_sum, n - 1)
                    link(stt(lm, z, 0.0, two(a2["e"], n), ALU.max, ALU.add))
                    tt(lm, lm, a2["strict"], ALU.mult).then_inc(lm_ready, 1)
                if n:
                    dve.wait_ge(z_sum, n)
                    if n >= 3:
                        dve.wait_ge(stick, n - 2)
                    tt(two(a2["s"], n - 1), sco[(n - 1) % 2][:, 0:384], a2["strictneg"], ALU.add).then_inc(z_masked, 1)
                if n >= 3 and n % 2:
                    pair_to_split((n - 3) // 2)
            pair_to_split(3)
            softmax_heads(heads2, HEADS1, a2, lambda j: pair_to_split(PAIRS_SB + j))

            ph = PH["att_o"]
            out = residual_units(ph, 0, 2)
            for c in range(ph.n):
                lo(ph.chunk0 + c + 1)
                if c:
                    out(Step(c - 1))
                pieces(ph, Step(c))
            out(Step(ph.n - 1))
            flush_pieces(ada_before("dn0", 0))
            units_done(dve, ph.unit0 + ph.units)
            norm_h(L0F)

            def swiglu(ph, base):
                def one(step):
                    c = step.j
                    if c < ph.n:
                        lo(ph.chunk0 + c + 1, step if step.i is not None else None, ph)
                    if c >= 1:
                        bank = (ph.unit0 + c - 1) % 2
                        product(step, 1, base, lin[bank][:, S:2 * S]).then_inc(lin_free[bank], 1)
                        rest(step, 1, base)

                steps(dve, ph.n, 2, 1, one)
                one(Step(ph.n))

            def down(ph, layer):
                out = residual_units(ph, layer, 5)
                steps(dve, ph.n, 4, 1, lambda s: down_step(ph, s, out))
                out(Step(ph.n - 1))

            swiglu(PH["gu0"], FT)
            down(PH["dn0"], 0)
            flush_pieces(2 * ADA_PIECES)
            units_done(dve, PH["dn0"].unit0 + PH["dn0"].units)
            dve.wait_ge(ada_out, 2 * ADA_PIECES)
            gains(1)
            norm_h(L1)
            ph = PH["ret_in"]
            dve.wait_ge(tab3_in, 16)

            def ret_rotary(c):
                bank = v3(lin[(ph.unit0 + c) % 2][:, :], 2)
                to = v3(rt["q" if c < 4 else "k"][:, c % 4 * 512:c % 4 * 512 + 512], 2)
                rot = v3(rt["rot"], 2)
                dve.wait_ge(chunk_done, ph.chunk0 + c + 1)
                link(tt(to, bank, over(rt["cos"], 2), ALU.mult))
                leave(tt(rot, bank, over(rt["sin"], 2), ALU.mult), ph.unit0 + c)
                dve.wait_ge(lin_free[(ph.unit0 + c) % 2], (ph.unit0 + c) // 2 + 1)
                tt(to[:, 0, :], to[:, 0, :], rot[:, 1, :], ALU.subtract)
                link(tt(to[:, 1, :], to[:, 1, :], rot[:, 0, :], ALU.add))

            for c in range(ph.n):
                lo(ph.chunk0 + c + 1)
                if 1 <= c <= 8:
                    ret_rotary(c - 1)

            def ret_decay(h):
                dve.wait_ge(ret_s, h + 1)
                if h >= 2:
                    dve.wait_ge(ret_o, 2 * (h - 1))
                tt(two(rt["inner"], h), sco[h % 2][:, 0:384], rt["decay"][:, h * 384:(h + 1) * 384], ALU.mult)\
                    .then_inc(ret_inner, 1)

            ret_decay(0)
            for h in range(RET_H):
                if h + 1 < RET_H:
                    ret_decay(h + 1)
                gs = gn_stat[:, 32 * (h % 2):32 * (h % 2) + 32]
                o = (tra + att)[2 * (h % 2):2 * (h % 2) + 2]
                dve.wait_ge(ret_o, 2 * h + 2)
                for q in range(2):
                    link(nc.vector.bn_stats(gs[:, 6 * q:6 * q + 6], o[q][:, :]))
                    link(nc.vector.bn_aggr(gs[:, 12 + 2 * q:14 + 2 * q], gs[:, 6 * q:6 * q + 6]))
                mv = v3(gs[:, 12:16], 2)
                ts(gs[:, 16:18], mv[:, :, 1], GN_EPS, None, ALU.add).then_inc(ret_var, 1)
                dve.wait_ge(ret_rsq, h + 1)
                link(tt(gs[:, 22:24], gs[:, 20:22], gs[:, 20:22], ALU.mult))
                link(tt(gs[:, 22:24], gs[:, 22:24], gs[:, 16:18], ALU.mult))
                link(ts(gs[:, 22:24], gs[:, 22:24], -0.5, 1.5, ALU.mult, ALU.add))
                link(tt(gs[:, 24:26], gs[:, 22:24], gs[:, 20:22], ALU.mult))
                stt(gs[:, 28:30], mv[:, :, 0], -1.0, gs[:, 24:26], ALU.mult, ALU.mult).then_inc(ret_rstd, 1)
                for m in range(2):
                    dve.wait_ge(ret_tr, 2 * h + m + 1)
                    to = rt["o"] if m == 0 else rt["rot"]
                    for b in range(2):
                        t = 4 * h + 2 * m + b
                        ins = stt(to[:, b * S:(b + 1) * S], lin[m][:, b * S:(b + 1) * S], col("gn", t), rt["g"][:, t * S:(t + 1) * S],
                                  ALU.mult, ALU.mult)
                    ins.then_inc(ret_y, 1)
                    t = (4 * h + 2 * m) * S
                    dve.wait_ge(ret_hh, 2 * h + m + 1)
                    tt(hid_lo[:, t:t + 512], to, hid_hi[:, t:t + 512].bitcast(F32), ALU.subtract).then_inc(ret_tiles, 1)

            ph = PH["ret_o"]
            out = residual_units(ph, 1, 2)
            for c in range(ph.n):
                lo(ph.chunk0 + c + 1)
                if c:
                    out(Step(c - 1))
            out(Step(ph.n - 1))
            units_done(dve, ph.unit0 + ph.units)
            norm_h(L1F)
            swiglu(PH["gu1"], 2 * FT)
            down(PH["dn1"], 1)
            units_done(dve, PH["dn1"].unit0 + PH["dn1"].units)
            rstd(FINAL)
            scaled(FINAL, e0["y"]).then_inc(r_used, 1)
            dve.wait_ge(r_used, FINAL + 1)
            for k in range(DT):
                cut = slice(k * S, (k + 1) * S)
                ins = ts(e0["sq"][:, cut], e0["y"][:, cut], col("final", k), None, ALU.mult)
            ins.then_inc(x_ready, 1)


def tables():
    f32 = np.float32
    key, query = np.arange(P)[:, None], np.arange(P)[None, :]
    zero, full = np.zeros((P, P), f32), np.ones((P, P), f32)
    causal = np.where(query <= key, 0.0, NEG).astype(f32)
    mask = np.concatenate([causal, zero, causal], 1)
    earlier = (key < query).astype(f32)
    strict = np.concatenate([earlier, full, earlier], 1)
    strict_neg = np.where(strict > 0, 0.0, NEG).astype(f32)

    def rope(dim, repeat):
        inv = (f32(THETA) ** (-(np.arange(dim // 2, dtype=f32) * f32(2.0) / f32(dim)))).astype(f32)
        ang = np.arange(S, dtype=f32)[None, :] * inv[:, None]
        c, s = np.cos(ang.astype(np.float64)).astype(f32), np.sin(ang.astype(np.float64)).astype(f32)
        return np.tile(c, (repeat, 1)), np.tile(s, (repeat, 1))

    def swap(dim):
        m = np.zeros((P, P), f32)
        for o in range(P):
            half = dim // 2
            if o % dim < half:
                m[o + half, o] = -1.0
            else:
                m[o - half, o] = 1.0
        return m

    dist = 255 - np.arange(BAND)
    exact = BUCKETS // 2
    near = np.maximum(dist, 1).astype(f32) / f32(exact)
    ratio = np.log(near).astype(f32) / f32(math.log(MAX_DIST / exact))
    large = np.minimum(exact + (ratio * f32(BUCKETS - exact)).astype(np.int32), BUCKETS - 1)
    bucket = np.where(dist < exact, np.maximum(dist, 0), large)
    inside = (dist >= 0) & (dist < WINDOW)
    onehot = np.zeros((P, BAND), f32)
    onehot[:BUCKETS] = (np.arange(BUCKETS)[:, None] == bucket[None, :]) & inside[None, :]
    onehot[BUCKETS] = np.where(inside, 0.0, NEG)
    decay = []
    pos = np.arange(S)
    for h in range(RET_H):
        diff = pos[None, :] - pos[:, None]
        full_decay = np.where(diff >= 0, np.exp(math.log(1.0 - 2.0 ** (-5 - h)) * np.maximum(diff, 0)), 0.0)
        full_decay = (full_decay / 16.0).astype(f32)
        decay += [full_decay[:P, :], full_decay[P:, P:]]
    c1, s1 = rope(ROPE, 8)
    c2, s2 = rope(HD, 4)
    c3, s3 = rope(256, 1)
    return {
        "ident": np.eye(P, dtype=f32),
        "tab1": np.concatenate([mask, c1, s1, swap(ROPE), onehot], 1),
        "tab2": np.concatenate([mask, c2, s2, swap(HD), -(key >= query).astype(f32), -full, strict, strict_neg], 1),
        "tab3": np.concatenate([c3, s3] + decay, 1),
    }


def lay_out(i):
    f32 = np.float32

    def chunks(w, width):
        k, n = w.shape
        a = w.reshape(k // P, P, n // width, width).transpose(2, 1, 0, 3)
        return np.ascontiguousarray(a).reshape(n // width * P, k // P * width)

    def pad(a, n):
        return np.concatenate([a, np.zeros(a.shape[:-1] + (n - a.shape[-1],), f32)], -1)

    def columns(v):
        return np.ascontiguousarray(v.reshape(-1, P).T)

    arrays = tables()
    arrays["x"] = np.ascontiguousarray(i["x"][0].T.reshape(DT, P, S).transpose(1, 0, 2)).reshape(P, DT * S)
    order = np.concatenate([np.r_[j * HD:(j + 1) * HD, (4 + j) * HD:(5 + j) * HD] for j in range(4)])
    heads = np.array([n // 2 + 4 * (n % 2) for n in range(8)])
    w = i["w_in"][0]
    a, f, m = w[:, :768], w[:, 768:1540], w[:, 1540:]
    w_in = np.concatenate([m[:, :384], np.tile(m[:, 384:416], (1, 4)), a[:, order], f[:, :512], a[:, 512:640],
                           pad(f[:, 768:772], P), f[:, 512:768], pad(a[:, 640:768], 2 * P)], 1)
    last = chunks(w_in[:, -256:-128], P)
    arrays["w_in"] = np.concatenate([chunks(w_in[:, :-256], 256), pad(last, CHUNK)], 0)
    uq = i["w_uq"][0].reshape(256, 4, 96)
    uq = np.concatenate([uq[:, :, :64].reshape(256, 256), uq[:, :, 64:].reshape(256, 128)], 1)
    ukv = i["w_ukv"][0].reshape(128, 4, 2, 64).transpose(0, 2, 1, 3).reshape(128, 512)
    arrays["mla"] = np.concatenate([chunks(uq, 384), ukv], 1)
    mixed = np.concatenate([order, np.arange(512, 1024)])
    arrays["w_out"] = chunks(i["w_out"][0][mixed], 256)

    def paired(w):
        k, n = w.shape
        return w.reshape(k, 2, FT, P).transpose(0, 2, 1, 3).reshape(k, n)

    def halves(w):
        a = w.reshape(2, HALF, P, DT, P).transpose(3, 0, 2, 1, 4)
        return np.ascontiguousarray(a).reshape(2 * DT * P, HALF * P)

    arrays["up"] = chunks(paired(i["w_up"][0]), 256)
    arrays["down"] = halves(i["w_down"][0])
    arrays["qkv"] = chunks(i["att_w_qkv_2"][0], 256)
    arrays["att_o"] = chunks(i["att_w_o_2"][0], 256)
    arrays["ret_in"] = chunks(i["ret_w_in_2"][0], 256)
    arrays["ret_o"] = chunks(i["ret_w_o_2"][0], P)
    for n in range(2):
        arrays[f"gu{n}"] = chunks(paired(i["ffn_w_gate_up_2"][n]), 256)
        arrays[f"dn{n}"] = halves(i["ffn_w_down_2"][n])
    arrays["ada"] = np.concatenate([chunks(i["ada_w_2"][n], 256) for n in range(2)], 0)

    def conv(v):
        return columns(paired(v[None, :])[0])

    def rows(v):
        return np.concatenate([v, np.zeros((P - v.shape[0], v.shape[1]), f32)], 0)

    rel = np.concatenate([i["rel_bias"][:, heads], np.ones((1, 8), f32)], 0)
    vectors = {
        "pre": columns(i["attn_pre_norm"][0]), "qlat": columns(i["q_latent_norm"][0]),
        "kvlat": columns(i["kv_latent_norm"][0]), "group": columns(i["group_norm"][0][mixed]),
        "post": columns(i["attn_post_norm"][0]), "ffnpre": columns(i["ffn_pre_norm"][0]),
        "conv_w": np.concatenate([conv(i["conv_w"][0, t]) for t in range(3)], 1), "conv_b": conv(i["conv_b"][0]),
        "ffnpost": columns(i["ffn_post_norm"][0]), "norms2": columns(i["norm_gains_2"]),
        "ada_b": columns(i["ada_b_2"]), "gn": columns(i["ret_gn_2"][0]), "final": columns(i["final_norm_2"]),
        "cond": columns(i["c_2"][0]), "sinks": np.tile(i["swa_sinks"][0][heads], (P, 1)),
        "fbias": rows(i["forget_bias"][0][:, None]), "rel": rows(rel),
    }
    arrays["cols"] = np.concatenate([vectors[n].astype(f32) for n in COLS], 1)
    return {n: np.ascontiguousarray(a) for n, a in arrays.items()}


def program(nc, arrays):
    dram = {n: nc.dram_tensor(f"in_{n}", a.shape, F32, kind="ExternalInput").ap() for n, a in arrays.items()}
    dram["out"] = nc.dram_tensor("out_0", (P, DT * S), F32, kind="ExternalOutput").ap()
    band = nc.dram_tensor("band", (P, 8 * BAND), F32, kind="Internal")
    dram["band"] = band.ap()
    dram["band_skew"] = bass.AP(band, P - 1, [[8 * BAND - 1, P], [BAND, 8], [1, S]])
    build(nc, dram)


def kernel(**inputs):
    import concourse.bacc as bacc
    from concourse.bass_utils import run_bass_kernel_spmd

    arrays = lay_out({n: np.asarray(a) for n, a in inputs.items()})
    nc = bacc.Bacc("TRN2", target_bir_lowering=False, num_devices=1)
    program(nc, arrays)
    result = run_bass_kernel_spmd(nc, [{f"in_{n}": a for n, a in arrays.items()}], core_ids=[0]).results[0]["out_0"]
    return np.ascontiguousarray(result.reshape(P, DT, S).transpose(2, 1, 0)).reshape(1, S, D)
```

```python
import math
from contextlib import ExitStack

import concourse.bass as bass
import numpy as np
from concourse import mybir

F32 = mybir.dt.float32
F32R = mybir.dt.float32r
ACT = mybir.ActivationFunctionType
ALU = mybir.AluOpType

P = 128
S = 256
D = 1024
DT = D // P
FF = 2816
FT = FF // P
HALF = FT // 2
EPS = 1e-6
GN_EPS = 1e-5
NEG = -1e30
HD = 64
RANKQ, RANKKV, ROPE = 256, 128, 32
BUCKETS, MAX_DIST, WINDOW = 32, 128, 128
BAND = 384
RET_H, RET_DV = 4, 512
THETA = 10000.0

RAW_SLOTS, SPLIT_SLOTS = 4, 2
CHUNK = 2048
UNROLL = 4

PHASES = [
    ("w_in", 9, DT, 2, 1), ("mla", 1, 1, 10, 1), ("w_out", 4, DT, 2, 1),
    ("up", 22, DT, 2, 1), ("down", 16, HALF, 1, 2),
    ("qkv", 12, DT, 2, 1), ("att_o", 4, DT, 2, 1), ("gu0", 22, DT, 2, 1), ("dn0", 16, HALF, 1, 2),
    ("ret_in", 24, DT, 2, 1), ("ret_o", 8, 2 * DT, 1, 1), ("gu1", 22, DT, 2, 1), ("dn1", 16, HALF, 1, 2),
]
MLA_UNITS = 4
ROW_CHUNKS = {"w_in": (7, 8), "qkv": range(8, 12), "ret_in": range(8, 16)}


class Phase:

    def __init__(self, name, n, kt, nb, per_unit, chunk0, unit0):
        self.name, self.n, self.kt, self.nb, self.per_unit = name, n, kt, nb, per_unit
        self.chunk0, self.unit0 = chunk0, unit0
        self.units = MLA_UNITS if name == "mla" else n // per_unit

    def size(self, c):
        if self.name == "w_in" and c == self.n - 1:
            return DT * P
        return self.kt * self.nb * P

    def row(self, c):
        return c in ROW_CHUNKS.get(self.name, ())

    def halves(self, c):
        n = self.size(c)
        if self.name == "mla":
            at = 2 * 3 * P
        else:
            at = n // 2 if n // P % 2 == 0 else (n // P + 1) // 2 * P
        return (0, at), (at, n)


def lay_out_phases():
    out, chunk, unit = {}, 0, 0
    for name, n, kt, nb, per in PHASES:
        ph = out[name] = Phase(name, n, kt, nb, per, chunk, unit)
        chunk, unit = chunk + n, unit + ph.units
    return out


PH = lay_out_phases()
ORDER = list(PH.values())
CHUNKS = sum(ph.n for ph in ORDER)


def phase_of(chunk):
    for ph in ORDER:
        if chunk < ph.chunk0 + ph.n:
            return ph, chunk - ph.chunk0


ADA_PIECES = 24
ADA_STEPS = [("w_in", 9, lambda c: int(c < 8) * (c % 2)), ("att1", 16, lambda c: int(c % 4 == 3)), ("down", 16, lambda c: c % 2),
             ("qkv", 12, lambda c: c % 2), ("att2", 16, lambda c: int(c % 4 == 3)), ("att_o", 4, lambda c: int(c < 3)),
             ("gu0", 22, lambda c: c % 2), ("dn0", 16, lambda c: c % 2)]
ADA_AT = {name: f for name, _, f in ADA_STEPS}


def ada_before(name, c):
    n = 0
    for at, steps_, f in ADA_STEPS:
        if at == name:
            return n + sum(f(i) for i in range(c))
        n += sum(f(i) for i in range(steps_))


def ada_here(name, c):
    return ADA_AT[name](c) if name in ADA_AT else 0


COLS = {}
for _name, _n in [("pre", 8), ("qlat", 2), ("kvlat", 1), ("group", 8), ("post", 8), ("ffnpre", 8), ("conv_w", 132),
                  ("conv_b", 44), ("ffnpost", 8), ("norms2", 32), ("ada_b", 96), ("gn", 16), ("final", 8),
                  ("sinks", 8), ("fbias", 1), ("rel", 8)]:
    COLS[_name] = (sum(v[1] for v in COLS.values()), _n)
NCOLS = sum(v[1] for v in COLS.values())

TAB1 = [("mask", 384), ("cos", S), ("sin", S), ("perm", P)]
TAB2 = [("mask", 384), ("cos", S), ("sin", S), ("perm", P), ("tri", P), ("strict", 384), ("strictneg", 384)]
TAB3 = [("cos", S), ("sin", S), ("decay", RET_H * 384)]

ARENA = 17152
ADA0 = ARENA - 2 * CHUNK
EARLY = [("y", 2048), ("sq", 2048)]
ATT1 = [("qa", 1024), ("qf", 512), ("qn", 512), ("ka", 256), ("kf", 512), ("v_a", 256), ("v_f", 512), ("kn", 512), ("v_m", 512),
        ("qr", 256), ("s", 1152), ("pT", 768), ("lat", 768), ("kr", 256), ("f", 256), ("fneg", 256), ("bias", 2048)] + TAB1
FFN = EARLY + [("u", 1024), ("g", 512), ("hid", 512)]
ATT2 = [("q", 2048), ("k", 2048), ("v", 2048)] + TAB2 + [("s", 1152), ("pT", 768), ("e", 768), ("lm", 768), ("rot", 512)]
RET = [("q", 2048), ("k", 2048), ("v", 4096)] + TAB3 + [("inner", 768), ("on", 1024), ("rot", 512), ("o", 512)]


TAB1_AT = sum(n for _, n in ATT1[:ATT1.index(TAB1[0])])
TAB2_AT = sum(n for _, n in ATT2[:ATT2.index(TAB2[0])])
TAB3_AT = sum(n for _, n in RET[:RET.index(TAB3[0])])


class Step:

    def __init__(self, j, i=None):
        self.j, self.i = j, i

    def n(self, f):
        if self.i is None:
            return f(self.j)
        by = f(self.j + UNROLL) - f(self.j)
        return self.i * by + f(self.j) if by else f(self.j)


def steps(eng, n, lead, tail, body):
    lead = min(lead, n)
    trips = (n - lead - tail) // UNROLL
    if trips < 2:
        trips = 0
    for c in range(lead):
        body(Step(c))
    if trips:
        with eng.Fori(0, trips) as i:
            for j in range(UNROLL):
                body(Step(lead + j, i))
    for c in range(lead + trips * UNROLL, n):
        body(Step(c))


NORM_GROUPS = [[8], [2, 1], [4, 2, 2], [8], [8], [8], [8], [8], [8], [8], [8]]
PRE, LATENT, GROUP, POST, FFNPRE, FFNPOST, L0, L0F, L1, L1F, FINAL = range(11)
SPLITS = [PRE, LATENT, GROUP, FFNPRE, L0, L0F, L1, L1F]
RESIDUALS = [POST, FFNPOST, FINAL]


def norm_tiles(norm):
    return sum(NORM_GROUPS[norm])


def scaled_before(norm):
    return sum(norm_tiles(i) for i in range(norm))


def tiles_before(norm):
    return sum(norm_tiles(i) for i in SPLITS if i < norm)


def x_before(norm):
    return sum(norm_tiles(i) for i in RESIDUALS if i < norm)


def groups_before(norm):
    return sum(len(NORM_GROUPS[i]) for i in range(norm))


def group_of(norm, k):
    at = 0
    for g, n in enumerate(NORM_GROUPS[norm]):
        if k < at + n:
            return g
        at += n


HEADS1, HEADS2 = 16, 8
SB_HEADS = 8


def build(nc, dram):
    ctx = ExitStack()
    with ctx:
        def sb(name, n, dt=F32, parts=P):
            return ctx.enter_context(nc.sbuf_tensor(name, [parts, n], dt))

        def sem(name):
            return ctx.enter_context(nc.semaphore(name))

        raw = [sb(f"raw{i}", CHUNK) for i in range(RAW_SLOTS)]
        w_hi = [sb(f"w_hi{i}", CHUNK, F32R) for i in range(SPLIT_SLOTS)]
        w_lo = [sb(f"w_lo{i}", CHUNK, F32R) for i in range(SPLIT_SLOTS)]
        h_hi, h_lo = sb("h_hi", DT * S, F32R), sb("h_lo", DT * S, F32R)
        hid_hi, hid_lo = sb("hid_hi", FT * S, F32R), sb("hid_lo", FT * S, F32R)
        x = sb("x", DT * S)
        cols = sb("cols", NCOLS)
        ident, ones = sb("ident", P), sb("ones", S)
        mod = sb("mod", 96)
        gscale = sb("gscale", 32)
        ada_sums = sb("ada_sums", 4)
        diag = sb("diag", 6 * P)
        stat, warm = sb("stat", 32), sb("warm", 16)
        head_stat = sb("head_stat", 3 * 16)
        gn_stat = sb("gn_stat", 2 * 32)
        arena = sb("arena", ARENA)
        cond_silu = arena[:, ADA0 - D:ADA0]
        ada_raw = [arena[:, ADA0 + i * CHUNK:ADA0 + (i + 1) * CHUNK] for i in range(2)]

        def parts(table, end=ADA0 - D):
            at, out = 0, {}
            for name, n in table:
                out[name] = arena[:, at:at + n]
                at += n
            assert at <= end, (at, end)
            return out

        e0, a1, ff, a2, rt = parts(EARLY), parts(ATT1), parts(FFN), parts(ATT2), parts(RET, ADA0)
        rt["g"] = arena[:, ADA0:ARENA]
        band, onehot = arena[0:8, 4096:4096 + BAND], arena[0:BUCKETS + 1, 4096 + BAND:4096 + 2 * BAND]
        S_AT = sum(n for _, n in ATT1[:ATT1.index(("s", 1152))])
        lat_sq, lat_y = arena[:, S_AT:S_AT + 768], arena[:, S_AT + 768:S_AT + 1536]
        GATE_AT = sum(n for _, n in ATT1[:ATT1.index(("kn", 512))])
        gate_tmp = arena[0:4, GATE_AT:GATE_AT + 5 * S]
        a1["mixed"] = arena[:, 0:DT * S]

        def col(name, j, n=1, rows=P):
            o = COLS[name][0]
            return cols[0:rows, o + j:o + j + n]

        psum = [ctx.enter_context(nc.psum_tensor(f"psum{i}", [P, 512], F32)) for i in range(8)]
        lin, sco, tra, att = psum[0:2], psum[2:4], psum[4:6], psum[6:8]
        ssum, rbc = sco[0][:, 0:6], (sco[1][:, 0:S], sco[1][:, S:2 * S], tra[0][:, 0:S])

        x_in, cols_in, tab1_in, tab2_in, tab3_in = (sem(n) for n in ("x_in", "cols_in", "tab1_in", "tab2_in", "tab3_in"))
        onehot_in, ident_in, band_out, bias_in, y_out = sem("onehot_in"), sem("ident_in"), sem("band_out"), sem("bias_in"), sem("y_out")
        raw_in = [sem(f"raw_in{i}") for i in range(RAW_SLOTS)]
        hi_ready, split_ready, half_done = sem("hi_ready"), sem("split_ready"), sem("half_done")
        lin_free = [sem(f"lin_free{i}") for i in range(2)]
        mla_units = sem("mla_units")
        ada_in = [sem(f"ada_in{i}") for i in range(2)]
        ada_sum, ada_out, cond_in, cond_ready = (sem(n) for n in ("ada_sum", "ada_out", "cond_in", "cond_ready"))
        ones_ready, band_ps, band_ready = sem("ones_ready"), sem("band_ps"), sem("band_ready")
        sq_ready, ssum_ready, ms_ready, root_ready = sem("sq_ready"), sem("ssum_ready"), sem("ms_ready"), sem("root_ready")
        diag_ready, rbc_ready, t_ready = sem("diag_ready"), sem("rbc_ready"), sem("t_ready")
        hh_ready, h_tiles, x_tiles = sem("hh_ready"), sem("h_tiles"), sem("x_tiles")
        dve_chain, act_chain = sem("dve_chain"), sem("act_chain")
        rot_ready, rot_done, f_in, f_ln, f_ready = (sem(n) for n in (
            "rot_ready", "rot_done", "f_in", "f_ln", "f_ready"))
        scores, scores_read, exps, probs, trans, trans_out, pv, att_out, o_hi, o_tiles = (sem(n) for n in (
            "scores", "scores_read", "exps", "probs", "trans", "trans_out", "pv", "att_out", "o_hi", "o_tiles"))
        z_ready, z_ln, lm_ready, z_sum, z_masked, stick = (sem(n) for n in (
            "z_ready", "z_ln", "lm_ready", "z_sum", "z_masked", "stick"))
        conv_in, conv_tap, gelu_ready, hid_ready, hid_hh, hid_tiles = (sem(n) for n in (
            "conv_in", "conv_tap", "gelu_ready", "hid_ready", "hid_hh", "hid_tiles"))
        ret_s, ret_inner, ret_o, ret_var, ret_rsq, ret_rstd, ret_norm, ret_tr, ret_y, ret_hh, ret_tiles = (sem(n) for n in (
            "ret_s", "ret_inner", "ret_o", "ret_var", "ret_rsq", "ret_rstd", "ret_norm", "ret_tr", "ret_y", "ret_hh", "ret_tiles"))

        def units_done(eng, unit):
            for b in range(2):
                n = (unit + 1 - b) // 2
                if n > 0:
                    eng.wait_ge(lin_free[b], n)

        def unit_free(eng, ph, step, f):
            if ph.unit0 + f(step.j) >= 2:
                eng.wait_ge(lin_free[(ph.unit0 + f(step.j)) % 2], step.n(lambda c: (ph.unit0 + f(c)) // 2))

        def leave(ins, unit):
            return ins.then_inc(lin_free[unit % 2], 1)

        def v3(ap, n):
            return ap.rearrange("p (a b) -> p a b", a=n)

        def over(ap, n):
            return ap.unsqueeze(1).to_broadcast([ap.shape[0], n, ap.shape[1]])

        def mod_col(layer, which, k):
            return mod[:, 48 * layer + 8 * which + k:48 * layer + 8 * which + k + 1]

        hh, hl = h_hi[:, :], h_lo[:, :]
        no_shift = lambda k: None
        NORM = {
            PRE: (x[:, :], e0["sq"], e0["y"], lambda k: col("pre", k), no_shift, hh, hl),
            LATENT: (a1["lat"], lat_sq, lat_y, lambda k: col("qlat", k) if k < 2 else col("kvlat", 0), no_shift, hid_hi, hid_lo),
            GROUP: (a1["mixed"], a1["bias"], arena[:, 4096:6144], lambda k: col("group", k), no_shift, hh, hl),
            POST: (e0["y"], e0["sq"], e0["y"], lambda k: col("post", k), None, None, None),
            FFNPRE: (x[:, :], e0["sq"], e0["y"], lambda k: col("ffnpre", k), no_shift, hh, hl),
            FFNPOST: (e0["y"], e0["sq"], e0["y"], lambda k: col("ffnpost", k), None, None, None),
            FINAL: (x[:, :], e0["sq"], e0["y"], lambda k: col("final", k), None, None, None),
        }
        for i, layer, which in ((L0, 0, 0), (L0F, 0, 3), (L1, 1, 0), (L1F, 1, 3)):
            NORM[i] = (x[:, :], e0["sq"], e0["y"],
                       lambda k, i=i: gscale[:, 8 * (L0, L0F, L1, L1F).index(i) + k:8 * (L0, L0F, L1, L1F).index(i) + k + 1],
                       lambda k, layer=layer, which=which: mod_col(layer, which, k), hh, hl)

        def half(ap, tile, h):
            return ap[HD * h:HD * h + HD, tile * S:(tile + 1) * S]

        heads1 = []
        for n in range(8):
            pair, h = n // 2, n % 2
            bias = a1["bias"][:, n * S:(n + 1) * S]
            v = v3(a1["v_a"], 2)
            heads1.append(dict(parts=[(half(a1["qa"], pair, h), half(a1["ka"], 0, h))], bias=(bias[:, P:S], bias),
                               sink=col("sinks", n), v=lambda kt, v=v, h=h: v[:, kt, HD * h:HD * h + HD], decay=None))
        mask = a1["mask"]
        for n in range(4):
            v = v3(a1["v_f"], 2)
            heads1.append(dict(parts=[(half(a1["qf"], n // 2, n % 2), half(a1["kf"], n // 2, n % 2))],
                               bias=(mask[:, 0:P], mask[:, P:384]), sink=None, decay=n,
                               v=lambda kt, v=v, n=n: v[:, kt, HD * n:HD * n + HD]))
        for n in range(4):
            v = v3(a1["v_m"], 2)
            rope = slice(ROPE * n, ROPE * n + ROPE)
            heads1.append(dict(parts=[(half(a1["qn"], n // 2, n % 2), half(a1["kn"], n // 2, n % 2)),
                                      (a1["qr"][rope, :], a1["kr"][rope, :])],
                               bias=(mask[:, 0:P], mask[:, P:384]), sink=None, decay=None,
                               v=lambda kt, v=v, n=n: v[:, kt, HD * n:HD * n + HD]))
        heads2 = []
        mask2, v2 = a2["mask"], v3(a2["v"], 2)
        for n in range(8, 16):
            heads2.append(dict(parts=[(half(a2["q"], n // 2, n % 2), half(a2["k"], n // 2, n % 2))],
                               bias=(mask2[:, 0:P], mask2[:, P:384]), sink=None, decay=None,
                               v=lambda kt, n=n: v2[:, kt, HD * n:HD * n + HD]))

        PAIRS1 = HEADS1 // 2
        PAIRS_SB = SB_HEADS // 2

        def three_of(ap, n):
            return ap[:, n % 3 * 384:(n % 3 + 1) * 384]

        def head_stats(n):
            return head_stat[:, 16 * (n % 3):16 * (n % 3) + 16]

        def two(ap, n):
            return ap[:, n % 2 * 384:(n % 2 + 1) * 384]

        block = ctx.enter_context(nc.Block())

        @block.sync
        def _(sp):
            sp.dma_start(x[:, :], dram["x"]).then_inc(x_in, 16)
            sp.dma_start(cols[:, :], dram["cols"]).then_inc(cols_in, 16)
            sp.dma_start(onehot, dram["onehot"]).then_inc(onehot_in, 16)
            sp.dma_start(ident[:, :], dram["ident"]).then_inc(ident_in, 16)
            sp.dma_start(arena[:, TAB1_AT:TAB1_AT + dram["tab1"].shape[1]], dram["tab1"]).then_inc(tab1_in, 16)
            sp.dma_start(cond_silu, dram["cond"]).then_inc(cond_in, 16)

            def load_ada(step, f):
                slot = f(step.j) % 2
                if f(step.j) >= 2:
                    sp.wait_ge(ada_out, step.n(lambda c: f(c) - 1))
                sp.dma_start(ada_raw[slot], dram["ada"][bass.ds(step.n(lambda c: f(c) * P), P), :]).then_inc(ada_in[slot], 16)

            def weights_of(ph):
                def load(step):
                    chunk = ph.chunk0 + step.j
                    slot, n = chunk % RAW_SLOTS, ph.size(step.j)
                    if chunk >= RAW_SLOTS:
                        sp.wait_ge(split_ready, step.n(lambda c: 2 * (ph.chunk0 + c - RAW_SLOTS + 1)))
                    src = dram[ph.name][bass.ds(step.n(lambda c: c * P), P), 0:n]
                    sp.dma_start(raw[slot][:, 0:n], src).then_inc(raw_in[slot], 16)
                return load

            def phase(ph):
                load = weights_of(ph)

                def one(step):
                    load(step)
                    for m in range(ada_here(ph.name, step.j)):
                        load_ada(step, lambda c, m=m: ada_before(ph.name, c) + m)

                steps(sp, ph.n, 4, 0, one)

            for ph in ORDER:
                if ph.name == "up":
                    sp.wait_ge(h_tiles, tiles_before(FFNPRE))
                    sp.dma_start(arena[:, TAB2_AT:TAB2_AT + dram["tab2"].shape[1]], dram["tab2"]).then_inc(tab2_in, 16)
                if ph.name == "gu0":
                    sp.wait_ge(o_tiles, 8)
                    sp.dma_start(arena[:, TAB3_AT:TAB3_AT + dram["tab3"].shape[1]], dram["tab3"]).then_inc(tab3_in, 16)
                attention = {"w_out": "att1", "att_o": "att2"}.get(ph.name)
                if attention:
                    load = weights_of(ph)
                    load(Step(0))
                    for m in range(2):
                        load_ada(Step(0), lambda c, m=m: ada_before(attention, 0) + m)
                    for c in range(1, ph.n):
                        load(Step(c))
                    for m in range(ada_before(attention, 16) - ada_before(attention, 0) - 2):
                        load_ada(Step(0), lambda c, m=m: ada_before(attention, 0) + 2 + m)
                    for c in range(ph.n):
                        for m in range(ada_here(ph.name, c)):
                            load_ada(Step(c), lambda c, m=m: ada_before(ph.name, c) + m)
                else:
                    phase(ph)
            for k in (0, DT // 2):
                sp.wait_ge(x_tiles, x_before(FINAL) + k + DT // 2)
                cut = slice(k * S, (k + DT // 2) * S)
                sp.dma_start(dram["out"][:, cut], e0["y"][:, cut]).then_inc(y_out, 16)
            sp.wait_ge(y_out, 32)

        @block.gpsimd
        def _(pool):
            pool.wait_ge(band_ready, 1)
            pool.dma_start(dram["band"], band).then_inc(band_out, 16)
            pool.wait_ge(band_out, 16)
            pool.dma_start(dram["band_rows"], dram["band_repeat"]).then_inc(band_out, 16)
            pool.wait_ge(band_out, 32)
            pool.dma_start(v3(a1["bias"], 8), dram["band_skew"]).then_inc(bias_in, 16)

        @block.scalar
        def _(act):
            chain = [0]

            def link(ins):
                chain[0] += 1
                ins.then_inc(act_chain, 1)
                act.wait_ge(act_chain, chain[0])

            def hi(chunk, step=None, ph=None):
                if chunk >= CHUNKS:
                    return
                of, c = phase_of(chunk)
                at = (lambda f: f(chunk)) if step is None else (lambda f: step.n(lambda c: f(ph.chunk0 + c + 1)))
                act.wait_ge(raw_in[chunk % RAW_SLOTS], at(lambda k: 16 * (k // RAW_SLOTS + 1)))
                for half, (a, b) in enumerate(of.halves(c)):
                    if chunk >= SPLIT_SLOTS:
                        before, cb = phase_of(chunk - SPLIT_SLOTS)
                        used = 1 if b <= before.halves(cb)[0][1] else 2
                        act.wait_ge(half_done, at(lambda k: 2 * (k - SPLIT_SLOTS) + used))
                    nc.scalar.activation(w_hi[chunk % SPLIT_SLOTS][:, a:b], raw[chunk % RAW_SLOTS][:, a:b], ACT.Copy)\
                        .then_inc(hi_ready, 1)

            def unit_ready(ph, step, f):
                act.wait_ge(half_done, step.n(lambda c: 2 * (ph.chunk0 + f(c) + 1)))

            def square(i, k=0, n=1, src=None):
                to, at = NORM[i][1], slice(k * S, (k + n) * S)
                nc.scalar.activation(to[:, at], NORM[i][0][:, at] if src is None else src, ACT.Square).then_inc(sq_ready, n)

            def root(i):
                n = 2 * len(NORM_GROUPS[i])
                nc.scalar.activation(warm[:, i:i + 1], ones[:, 0:1], ACT.Sqrt)
                act.wait_ge(ms_ready, i + 1)
                nc.scalar.activation(stat[:, 6:6 + n], stat[:, 0:n], ACT.Sqrt).then_inc(root_ready, 1)

            def round_h(i):
                _, _, tmp, _, shift, dst, _ = NORM[i]
                for k in range(norm_tiles(i)):
                    cut = slice(k * S, (k + 1) * S)
                    act.wait_ge(t_ready, scaled_before(i) + k + 1)
                    if shift(k) is None:
                        ins = nc.scalar.activation(dst[:, cut], tmp[:, cut], ACT.Copy)
                    else:
                        ins = nc.scalar.activation(dst[:, cut], tmp[:, cut], ACT.Identity, bias=shift(k))
                    ins.then_inc(hh_ready, 1)

            def square_residual(i, residual):
                for k in range(DT):
                    act.wait_ge(x_tiles, x_before(residual) + k + 1)
                    square(i, k)

            act.wait_ge(band_ps, 1)
            nc.scalar.activation(band, tra[0][0:8, 0:BAND], ACT.Copy).then_inc(band_ready, 1)
            act.wait_ge(x_in, 16)
            for k in range(0, DT, 2):
                square(PRE, k, 2)
            act.wait_ge(ones_ready, 1)
            root(PRE)
            hi(0)
            round_h(PRE)
            act.wait_ge(cond_in, 16)
            nc.scalar.activation(cond_silu, cond_silu, ACT.Silu).then_inc(cond_ready, 1)

            ph = PH["w_in"]
            dst = {0: [(a1["lat"][:, 0:512], 0, 512, 1.0)],
                   1: [(a1["lat"][:, 512:768], 0, 256, 1.0), (a1["kr"], 256, 512, 1.0)],
                   2: [(a1["qa"][:, 0:512], 0, 512, HD ** -0.5)], 3: [(a1["qa"][:, 512:1024], 0, 512, HD ** -0.5)],
                   4: [(a1["qf"], 0, 512, HD ** -0.5)], 5: [(a1["kf"], 0, 512, 1.0)],
                   6: [(a1["ka"], 0, 256, 1.0)], 7: [(a1["v_f"], 0, 512, 1.0)]}

            def leave_w_in(c):
                act.wait_ge(half_done, 2 * (c + 1))
                bank = lin[c % 2]
                if c == 0:
                    act.wait_ge(h_tiles, 8)
                if c == 6:
                    nc.scalar.activation(gate_tmp[:, 0:S], bank[0:4, S:2 * S], ACT.Identity, bias=col("fbias", 0, 1, 4))\
                        .then_inc(f_in, 1)
                if c == 8:
                    ins = nc.scalar.activation(v3(a1["v_a"], 2), v3(bank[:, :], 2)[:, :, 0:P], ACT.Copy)
                else:
                    for to, a, b, scale in dst[c]:
                        ins = nc.scalar.activation(to, bank[:, a:b], ACT.Copy, scale=scale)
                leave(ins, c)

            for c in range(ph.n):
                hi(ph.chunk0 + c + 1)
                if c:
                    leave_w_in(c - 1)
                if c == 3:
                    act.wait_ge(lin_free[0], 1)
                    act.wait_ge(lin_free[1], 1)
                    square(LATENT, 0, 3)
                if c == 4:
                    root(LATENT)
                if c == 5:
                    round_h(LATENT)
                if c == 8:
                    act.wait_ge(f_in, 1)
                    act.wait_ge(band_out, 16)
                    link(nc.scalar.activation(gate_tmp[:, S:2 * S], gate_tmp[:, 0:S], ACT.Abs))
                    link(nc.scalar.activation(gate_tmp[:, 2 * S:3 * S], gate_tmp[:, S:2 * S], ACT.Exp, scale=-1.0))
                    nc.scalar.activation(gate_tmp[:, 3 * S:4 * S], gate_tmp[:, 2 * S:3 * S], ACT.Ln, bias=ones[0:4, 0:1])\
                        .then_inc(f_ln, 1)
            leave_w_in(8)
            hi(PH["w_out"].chunk0)
            u0 = PH["mla"].unit0
            vm = a1["v_m"]
            qscale = (HD + ROPE) ** -0.5
            for u, todo in enumerate([[(a1["qn"], 0, 512, qscale)],
                                      [(a1["qr"], 0, 256, qscale), (a1["kn"][:, 0:256], 256, 512, 1.0)],
                                      [(a1["kn"][:, 256:512], 0, 256, 1.0), (vm[:, 0:256], 256, 512, 1.0)],
                                      [(vm[:, 256:512], 0, 256, 1.0)]]):
                if u == 1:
                    act.wait_ge(f_ready, 1)
                if u < MLA_UNITS - 1:
                    act.wait_ge(mla_units, u + 1)
                else:
                    act.wait_ge(half_done, 2 * (PH["mla"].chunk0 + 1))
                for to, a, b, scale in todo:
                    ins = nc.scalar.activation(to, lin[(u0 + u) % 2][:, a:b], ACT.Copy, scale=scale)
                leave(ins, u0 + u)

            def exp_head(n, base, a, sink):
                hs = head_stats(n)
                s = three_of(a["s"], n)
                act.wait_ge(scores_read, base + n + 1)
                if sink is not None:
                    nc.scalar.activation(hs[:, 6:8], hs[:, 2:4], ACT.Exp, bias=sink)
                nc.scalar.activation(s[:, 0:P], s[:, 0:P], ACT.Exp, bias=hs[:, 2:3], accum_out=hs[:, 4:5])
                nc.scalar.activation(s[:, P:384], s[:, P:384], ACT.Exp, bias=hs[:, 3:4], accum_out=hs[:, 5:6])\
                    .then_inc(exps, 1)

            def copy_head(n, base, a):
                act.wait_ge(trans, base + n + 1)
                if n >= 2:
                    act.wait_ge(pv, base + n - 1)
                nc.scalar.activation(two(a["pT"], n), tra[n % 2][:, 0:384], ACT.Copy).then_inc(trans_out, 1)

            for n in range(HEADS1):
                exp_head(n, 0, a1, heads1[n]["sink"])
                if n:
                    copy_head(n - 1, 0, a1)
                if n in (11, 13, 15):
                    k, many = {11: (0, 4), 13: (4, 1), 15: (5, 1)}[n]
                    act.wait_ge(att_out, k + many)
                    square(GROUP, k, many)
            copy_head(HEADS1 - 1, 0, a1)
            for k in (6, 7):
                act.wait_ge(att_out, k + 1)
                square(GROUP, k)
            root(GROUP)
            round_h(GROUP)

            def copy_units(ph, norm):
                per = ph.per_unit

                def leave_unit(step):
                    u = (step.j + 1) // per - 1
                    act.wait_ge(half_done, step.n(lambda c: 2 * (ph.chunk0 + c + 1)))
                    w = 512 // per
                    cut = bass.ds(step.n(lambda c: ((c + 1) // per - 1) * w), w)
                    bank = lin[(ph.unit0 + u) % 2][:, 0:w]
                    nc.scalar.activation(NORM[norm][1][:, cut], bank, ACT.Square).then_inc(sq_ready, w // S)
                    leave(nc.scalar.activation(e0["y"][:, cut], bank, ACT.Copy), ph.unit0 + u)
                return leave_unit

            ph = PH["w_out"]
            out_unit = copy_units(ph, POST)
            for c in range(ph.n):
                hi(ph.chunk0 + c + 1)
                if c:
                    out_unit(Step(c - 1))
            out_unit(Step(ph.n - 1))
            root(POST)
            square_residual(FFNPRE, POST)
            root(FFNPRE)
            round_h(FFNPRE)

            ph = PH["up"]
            cw, cb = COLS["conv_w"][0], COLS["conv_b"][0]

            def at_col(v):
                return cols[:, bass.ds(v, 1)]

            def conv_start(step):
                j = step.j - 1
                act.wait_ge(half_done, step.n(lambda c: 2 * (ph.chunk0 + c)))
                if j >= 2:
                    act.wait_ge(hid_ready, step.n(lambda c: c - 2))
                for s in range(2):
                    ins = nc.scalar.activation(
                        ff["u"][:, 512 * (j % 2) + S * s:512 * (j % 2) + S * s + S],
                        lin[(ph.unit0 + j) % 2][:, S * s:S * s + S], ACT.Identity,
                        scale=at_col(step.n(lambda c: cw + 88 + 2 * (c - 1) + s)),
                        bias=at_col(step.n(lambda c: cb + 2 * (c - 1) + s)))
                ins.then_inc(conv_in, 1)

            def gelu(step):
                j = step.j - 2
                act.wait_ge(lin_free[(ph.unit0 + j) % 2], step.n(lambda c: (ph.unit0 + c - 2) // 2 + 1))
                nc.scalar.activation(ff["g"][:, S * (j % 2):S * (j % 2) + S],
                                     ff["u"][:, 512 * (j % 2):512 * (j % 2) + S], ACT.Gelu_apprx_tanh)\
                    .then_inc(gelu_ready, 1)

            def round_hid(step, lag, unit0=None):
                j = step.j - lag
                if unit0 is None:
                    act.wait_ge(hid_ready, step.n(lambda c: c - lag + 1))
                else:
                    act.wait_ge(lin_free[(unit0 + j) % 2], step.n(lambda c: (unit0 + c - lag) // 2 + 1))
                nc.scalar.activation(hid_hi[:, bass.ds(step.n(lambda c: (c - lag) * S), S)],
                                     ff["hid"][:, S * (j % 2):S * (j % 2) + S], ACT.Copy).then_inc(hid_hh, 1)

            def up_step(step):
                c = step.j
                if c < ph.n:
                    hi(ph.chunk0 + c + 1, step if step.i is not None else None, ph)
                if c >= 2:
                    gelu(step)
                if 1 <= c <= ph.n:
                    conv_start(step)
                if c >= 2:
                    round_hid(step, 2)

            steps(act, ph.n, 2, 1, up_step)
            up_step(Step(ph.n))
            up_step(Step(ph.n + 1))

            ph = PH["down"]
            out_unit = copy_units(ph, FFNPOST)

            def down_step(step):
                hi(ph.chunk0 + step.j + 1, step if step.i is not None else None, ph)
                if step.j >= 2 and step.j % 2 == 0:
                    out_unit(Step(step.j - 1, step.i))

            steps(act, ph.n, 4, 1, down_step)
            out_unit(Step(ph.n - 1))
            root(FFNPOST)

            square_residual(L0, FFNPOST)
            root(L0)
            round_h(L0)
            ph = PH["qkv"]

            def qkv_unit(c):
                act.wait_ge(half_done, 2 * (ph.chunk0 + c + 1))
                bank = lin[(ph.unit0 + c) % 2]
                if c == 0:
                    act.wait_ge(h_tiles, tiles_before(L0F))
                if c < 8:
                    to = a2["q" if c < 4 else "k"][:, c % 4 * 512:c % 4 * 512 + 512]
                    ins = nc.scalar.activation(to, bank[:, :], ACT.Copy, scale=HD ** -0.5 if c < 4 else 1.0)
                else:
                    to = v2[:, :, (c - 8) * S:(c - 7) * S]
                    ins = nc.scalar.activation(to, v3(bank[:, :], 2), ACT.Copy)
                leave(ins, ph.unit0 + c)

            for c in range(ph.n):
                hi(ph.chunk0 + c + 1)
                if c:
                    qkv_unit(c - 1)
            qkv_unit(ph.n - 1)

            def round_pair(j, pair):
                act.wait_ge(pv, HEADS1 + 2 * j + 2)
                nc.scalar.activation(h_hi[:, j * S:(j + 1) * S], att[pair % 2][:, 0:S], ACT.Copy).then_inc(o_hi, 1)

            def square_unit(ph, norm, unit, step=Step(0)):
                at = (lambda f: f(unit)) if step.i is None else (lambda f: step.n(lambda c: f(c // 2 - 2)))
                act.wait_ge(lin_free[(ph.unit0 + unit) % 2], at(lambda u: (ph.unit0 + u) // 2 + 1))
                w = DT // ph.units * S
                cut = bass.ds(at(lambda u: u * w), w)
                nc.scalar.activation(NORM[norm][1][:, cut], x[:, cut], ACT.Square).then_inc(sq_ready, w // S)

            for n in range(SB_HEADS + 1):
                if n < SB_HEADS:
                    e = two(a2["e"], n)
                    act.wait_ge(z_ready, n + 1)
                    if n >= 2:
                        act.wait_ge(lm_ready, n - 1)
                    link(nc.scalar.activation(e, sco[n % 2][:, 0:384], ACT.Abs))
                    link(nc.scalar.activation(e, e, ACT.Exp, scale=-1.0))
                    nc.scalar.activation(e, e, ACT.Ln, bias=ones[:, 0:1]).then_inc(z_ln, 1)
                if n:
                    act.wait_ge(z_masked, n)
                    if n >= 3:
                        act.wait_ge(pv, HEADS1 + n - 2)
                    nc.scalar.activation(two(a2["pT"], n - 1), two(a2["s"], n - 1), ACT.Exp).then_inc(stick, 1)
                if n >= 3 and n % 2:
                    round_pair((n - 3) // 2, PAIRS1 + (n - 3) // 2)
            round_pair(3, PAIRS1 + 3)
            base = HEADS1
            for n in range(HEADS2):
                exp_head(n, base, a2, None)
                if n:
                    act.wait_ge(trans, base + n)
                    act.wait_ge(pv, HEADS1 + SB_HEADS + max(n - 2, 0))
                    nc.scalar.activation(two(a2["pT"], n - 1), tra[(n - 1) % 2][:, 0:384], ACT.Copy).then_inc(trans_out, 1)
                if n >= 3 and n % 2:
                    j = PAIRS_SB + (n - 3) // 2
                    round_pair(j, PAIRS1 + j)
            n = HEADS2
            act.wait_ge(trans, base + n)
            act.wait_ge(pv, HEADS1 + SB_HEADS + n - 2)
            nc.scalar.activation(two(a2["pT"], n - 1), tra[(n - 1) % 2][:, 0:384], ACT.Copy).then_inc(trans_out, 1)
            round_pair(7, PAIRS1 + 7)

            ph = PH["att_o"]
            for c in range(ph.n):
                hi(ph.chunk0 + c + 1)
                if c >= 2:
                    square_unit(ph, L0F, c - 2)
            square_unit(ph, L0F, 2)
            square_unit(ph, L0F, 3)

            def swiglu(ph):
                def silu(step):
                    j = step.j - 1
                    act.wait_ge(half_done, step.n(lambda c: 2 * (ph.chunk0 + c)))
                    nc.scalar.activation(ff["g"][:, S * (j % 2):S * (j % 2) + S], lin[(ph.unit0 + j) % 2][:, 0:S], ACT.Silu)\
                        .then_inc(gelu_ready, 1)

                def step_(step):
                    hi(ph.chunk0 + step.j + 1, step if step.i is not None else None, ph)
                    if step.j >= 1:
                        silu(step)
                        round_hid(step, 1, ph.unit0)

                steps(act, ph.n, 2, 1, step_)
                silu(Step(ph.n))
                round_hid(Step(ph.n), 1, ph.unit0)

            def down(ph, norm):
                def one(step):
                    hi(ph.chunk0 + step.j + 1, step if step.i is not None else None, ph)
                    if step.j >= 4 and step.j % 2 == 0:
                        square_unit(ph, norm, step.j // 2 - 2, step)

                steps(act, ph.n, 4, 1, one)
                square_unit(ph, norm, DT - 2)
                square_unit(ph, norm, DT - 1)

            root(L0F)
            round_h(L0F)
            swiglu(PH["gu0"])
            down(PH["dn0"], L1)

            root(L1)
            round_h(L1)
            ph = PH["ret_in"]

            def ret_unit(step):
                c = step.j - 1
                bank = lin[(ph.unit0 + c) % 2]
                act.wait_ge(half_done, step.n(lambda c: 2 * (ph.chunk0 + c)))
                if c < 16:
                    to = v3(rt["v"], 2)[:, :, (c - 8) * S:(c - 7) * S]
                    ins = nc.scalar.activation(to, v3(bank[:, :], 2), ACT.Copy)
                else:
                    ins = nc.scalar.activation(rt["g"][:, (c - 16) * 512:(c - 15) * 512], bank[:, :], ACT.Silu)
                leave(ins, ph.unit0 + c)

            for c in range(ph.n):
                hi(ph.chunk0 + c + 1)
                if c > 8:
                    ret_unit(Step(c))
            ret_unit(Step(ph.n))

            for h in range(RET_H):
                gs = gn_stat[:, 32 * (h % 2):32 * (h % 2) + 32]
                act.wait_ge(ret_var, h + 1)
                link(nc.scalar.activation(gs[:, 18:20], gs[:, 16:18], ACT.Ln))
                nc.scalar.activation(gs[:, 20:22], gs[:, 18:20], ACT.Exp, scale=-0.5).then_inc(ret_rsq, 1)
                act.wait_ge(ret_rstd, h + 1)
                if h:
                    act.wait_ge(ret_tr, 2 * h)
                for q in range(2):
                    nc.scalar.activation(rt["on"][:, 512 * q:512 * q + 512], (tra + att)[2 * (h % 2) + q][:, :], ACT.Identity,
                                         scale=gs[:, 24 + q:25 + q], bias=gs[:, 28 + q:29 + q]).then_inc(ret_norm, 1)
                for m in range(2):
                    act.wait_ge(ret_y, 2 * h + m + 1)
                    t = (4 * h + 2 * m) * S
                    nc.scalar.activation(hid_hi[:, t:t + 512], rt["o"] if m == 0 else rt["rot"], ACT.Copy).then_inc(ret_hh, 1)

            ph = PH["ret_o"]
            for c in range(ph.n):
                hi(ph.chunk0 + c + 1)
                if c >= 2:
                    square_unit(ph, L1F, c - 2)
            square_unit(ph, L1F, ph.n - 2)
            square_unit(ph, L1F, ph.n - 1)
            root(L1F)
            round_h(L1F)
            swiglu(PH["gu1"])
            down(PH["dn1"], FINAL)
            root(FINAL)

        @block.tensor
        def _(pe):
            def three(out, w, hc, lc, start, stop):
                nc.tensor.matmul(out, w[0], hc, start=start, stop=False, skip_group_check=True)
                nc.tensor.matmul(out, w[0], lc, start=False, stop=False, skip_group_check=True)
                return nc.tensor.matmul(out, w[1], hc, start=False, stop=stop, skip_group_check=True)

            def weights(chunk, step, ph):
                pe.wait_ge(split_ready, step.n(lambda c: 2 * (ph.chunk0 + c) + 1))
                s = chunk % SPLIT_SLOTS
                return w_hi[s], w_lo[s]

            def second_half(ph, step):
                pe.wait_ge(split_ready, step.n(lambda c: 2 * (ph.chunk0 + c) + 2))

            def by_feature(ph, step, first_tiles=None, rhs=None, k0=lambda c: 0):
                j = step.j
                f = lambda c: (c + ph.per_unit) // ph.per_unit - 1
                whi, wlo = weights(ph.chunk0 + j, step, ph)
                if j % ph.per_unit == 0:
                    unit_free(pe, ph, step, f)
                bank = lin[(ph.unit0 + f(j)) % 2]
                r_hi, r_lo = rhs or (h_hi, h_lo)
                blocks = ph.nb * ph.kt
                cut2 = ph.halves(j)[1][0] // P
                for b in range(ph.nb):
                    for k in range(ph.kt):
                        at = b * ph.kt + k
                        if at == cut2:
                            second_half(ph, step)
                        if first_tiles is not None and b == 0:
                            pe.wait_ge(first_tiles[0], first_tiles[1] + k + 1)
                        cut = slice(at * P, at * P + P)
                        t = slice((k0(j) + k) * S, (k0(j) + k + 1) * S)
                        ins = three(bank[:, b * S:(b + 1) * S], (whi[:, cut], wlo[:, cut]), r_hi[:, t], r_lo[:, t],
                                    start=(k == 0 and j % ph.per_unit == 0),
                                    stop=(k == ph.kt - 1 and j % ph.per_unit == ph.per_unit - 1))
                        if at in (cut2 - 1, blocks - 1):
                            ins.then_inc(half_done, 1)

            def by_row(ph, step, nb=2):
                j = step.j
                whi, wlo = weights(ph.chunk0 + j, step, ph)
                unit_free(pe, ph, step, lambda c: c)
                bank = lin[(ph.unit0 + j) % 2]
                width = nb * P
                for r in range(2):
                    for k in range(ph.kt):
                        if r == 0 and k == ph.kt // 2:
                            second_half(ph, step)
                        w = slice(k * width, (k + 1) * width)
                        t = slice(k * S + r * P, k * S + r * P + P)
                        out = bank[:, r * S:r * S + width]
                        nc.tensor.matmul(out, h_hi[:, t], whi[:, w], start=k == 0, stop=False, skip_group_check=True)
                        nc.tensor.matmul(out, h_hi[:, t], wlo[:, w], start=False, stop=False, skip_group_check=True)
                        ins = nc.tensor.matmul(out, h_lo[:, t], whi[:, w], start=False, stop=k == ph.kt - 1,
                                               skip_group_check=True)
                        if r == 1 and k in (ph.kt // 2 - 1, ph.kt - 1):
                            ins.then_inc(half_done, 1)

            def sums(i):
                sq, k = NORM[i][1], 0
                for g, nt in enumerate(NORM_GROUPS[i]):
                    for m in range(nt):
                        pe.wait_ge(sq_ready, scaled_before(i) + k + 1)
                        for r in range(2):
                            ins = nc.tensor.matmul(ssum[:, 2 * g + r:2 * g + r + 1], sq[:, k * S + r * P:k * S + r * P + P], ones[:, 0:1],
                                                   start=k == 0 and r == 0, stop=k == norm_tiles(i) - 1 and r == 1,
                                                   skip_group_check=True)
                        k += 1
                ins.then_inc(ssum_ready, 1)

            def spread(i):
                for g in range(len(NORM_GROUPS[i])):
                    for r in range(2):
                        pe.wait_ge(diag_ready, 2 * (groups_before(i) + g) + r + 1)
                        at = slice((2 * g + r) * P, (2 * g + r + 1) * P)
                        ins = nc.tensor.matmul(rbc[g][:, r * P:(r + 1) * P], ones[:, 0:P], diag[:, at], start=True, stop=True)
                ins.then_inc(rbc_ready, 1)

            def norm(i):
                sums(i)
                spread(i)

            def rotate(n, perm, src, width=S):
                return nc.tensor.matmul(tra[n % 2][:, 0:width], perm, src, start=True, stop=True)

            pe.wait_ge(cols_in, 16)
            pe.wait_ge(onehot_in, 16)
            nc.tensor.matmul(tra[0][0:8, 0:BAND], col("rel", 0, 8, BUCKETS + 1), onehot, start=True, stop=True).then_inc(band_ps, 1)
            pe.wait_ge(ones_ready, 1)
            norm(PRE)
            ph = PH["w_in"]
            for c in range(ph.n):
                if c < 7:
                    by_feature(ph, Step(c), (h_tiles, 0) if c == 0 else None)
                else:
                    by_row(ph, Step(c), 2 if c == 7 else 1)
                if c == 3:
                    sums(LATENT)
                if c == 4:
                    spread(LATENT)
                    pe.wait_ge(band_ready, 1)
                    units_done(pe, 2)
                    rotate(0, a1["perm"], a1["kr"]).then_inc(rot_ready, 1)

            ph = PH["mla"]
            whi, wlo = weights(ph.chunk0, Step(0), ph)
            pe.wait_ge(h_tiles, tiles_before(GROUP))
            up, wide = 2 * 384, 384

            def latent(unit, at, out_cols, w0, tiles, width):
                for n, k in enumerate(tiles):
                    w = slice(w0 + n * width, w0 + n * width + P)
                    t = slice(k * S, (k + 1) * S)
                    ins = three(lin[(ph.unit0 + unit) % 2][:, at * S:(at + 1) * S], (whi[:, w], wlo[:, w]),
                                hid_hi[:, t], hid_lo[:, t], n == 0, n == len(tiles) - 1)
                return ins

            def latent_v(unit, at, r):
                t = slice(2 * S + r * P, 2 * S + r * P + P)
                w = slice(up + 2 * P, up + 4 * P)
                out = lin[(ph.unit0 + unit) % 2][:, at * S:(at + 1) * S]
                nc.tensor.matmul(out, hid_hi[:, t], whi[:, w], start=True, stop=False, skip_group_check=True)
                nc.tensor.matmul(out, hid_hi[:, t], wlo[:, w], start=False, stop=False, skip_group_check=True)
                return nc.tensor.matmul(out, hid_lo[:, t], whi[:, w], start=False, stop=True, skip_group_check=True)

            for u in range(MLA_UNITS):
                unit_free(pe, ph, Step(u), lambda c: c)
                if u == 0:
                    latent(u, 0, None, 0, (0, 1), wide)
                    ins = latent(u, 1, None, P, (0, 1), wide)
                elif u == 1:
                    latent(u, 0, None, 2 * P, (0, 1), wide).then_inc(half_done, 1)
                    second_half(ph, Step(0))
                    ins = latent(u, 1, None, up, (2,), P)
                elif u == 2:
                    latent(u, 0, None, up + P, (2,), P)
                    ins = latent_v(u, 1, 0)
                else:
                    ins = latent_v(u, 0, 1)
                ins.then_inc(mla_units if u < MLA_UNITS - 1 else half_done, 1)
            units_done(pe, ph.unit0 + 2)
            rotate(1, a1["perm"], a1["qr"]).then_inc(rot_ready, 1)

            def score_head(n, base, head):
                out = sco[n % 2]
                if n >= 2:
                    pe.wait_ge(scores_read, base + n - 1)
                first, todo = True, []
                for q, k in head["parts"]:
                    todo.append((out[:, 0:P], q[:, 0:P], k[:, 0:P]))
                    todo.append((out[:, P:384], q[:, P:S], k))
                if head["decay"] is not None:
                    pick = ident[0:4, head["decay"]:head["decay"] + 1]
                    f, fneg = a1["f"][0:4, :], a1["fneg"][0:4, :]
                    for o, q, k in ((out[:, 0:P], slice(0, P), slice(0, P)), (out[:, P:384], slice(P, S), slice(0, S))):
                        n_k = k.stop - k.start
                        todo.append((o, f[:, q], pick.to_broadcast([4, n_k])))
                        todo.append((o, pick.to_broadcast([4, P]), fneg[:, k]))
                for m, (o, q, k) in enumerate(todo):
                    ins = nc.tensor.matmul(o, q, k, start=first, stop=m == len(todo) - 1, skip_group_check=True)
                    first = False
                ins.then_inc(scores, 1)

            def turn_head(n, base, a):
                s = three_of(a["s"], n)
                pe.wait_ge(probs, base + n + 1)
                if n >= 2:
                    pe.wait_ge(trans_out, base + n - 1)
                for m in range(3):
                    ins = nc.tensor.transpose(tra[n % 2][:, m * P:(m + 1) * P], s[:, m * P:(m + 1) * P], ident[:, :])
                ins.then_inc(trans, 1)

            def values(n, pT, v, pair):
                h = n % 2
                if pair >= 2 and h == 0:
                    if pair - 2 < PAIRS1:
                        pe.wait_ge(att_out, pair - 1)
                    else:
                        pe.wait_ge(o_tiles, pair - 1 - PAIRS1)
                o = att[pair % 2][HD * h:HD * h + HD, 0:S]
                nc.tensor.matmul(o, v(0), pT[:, 0:S], start=True, stop=False, skip_group_check=True)
                nc.tensor.matmul(o[:, P:S], v(1), pT[:, S:384], start=False, stop=True, skip_group_check=True)\
                    .then_inc(pv, 1)

            def softmax_heads(heads, base, a, pair0):
                score_head(0, base, heads[0])
                score_head(1, base, heads[1])
                for n in range(len(heads) + 1):
                    if n + 2 < len(heads):
                        score_head(n + 2, base, heads[n + 2])
                    if n < len(heads):
                        turn_head(n, base, a)
                    if n:
                        pe.wait_ge(trans_out, base + n)
                        values(n - 1, two(a["pT"], n - 1), heads[n - 1]["v"], pair0 + (n - 1) // 2)

            units_done(pe, ph.unit0 + ph.units)
            pe.wait_ge(rot_done, 2)
            pe.wait_ge(f_ready, 1)
            softmax_heads(heads1, 0, a1, 0)

            pe.wait_ge(scores_read, HEADS1)
            norm(GROUP)
            ph = PH["w_out"]
            for c in range(ph.n):
                by_feature(ph, Step(c), (h_tiles, tiles_before(GROUP)) if c == 0 else None)
            norm(POST)
            norm(FFNPRE)

            def up_phase(name, i):
                ph = PH[name]
                by_feature(ph, Step(0), (h_tiles, tiles_before(i)))
                steps(pe, ph.n, 1, 1, lambda s: by_feature(ph, s) if s.i is not None or s.j else None)

            def down_phase(name, base):
                ph = PH[name]

                def one(step):
                    if step.i is None and step.j < 2:
                        pe.wait_ge(hid_tiles, base + HALF * (step.j + 1))
                    by_feature(ph, step, rhs=(hid_hi, hid_lo), k0=lambda c: HALF * (c % 2))

                steps(pe, ph.n, 4, 0, one)

            up_phase("up", FFNPRE)
            down_phase("down", 0)
            norm(FFNPOST)
            norm(L0)
            ph = PH["qkv"]
            pe.wait_ge(tab2_in, 16)
            for c in range(ph.n):
                if c < 8:
                    by_feature(ph, Step(c), (h_tiles, tiles_before(L0)) if c == 0 else None)
                else:
                    by_row(ph, Step(c))
                if c >= 8:
                    r = c - 8
                    units_done(pe, ph.unit0 + 8)
                    if r >= 2:
                        pe.wait_ge(rot_done, 2 + r - 1)
                    t = a2["q" if r < 2 else "k"][:, (4 + r % 2 * 2) * S:(6 + r % 2 * 2) * S]
                    rotate(r, a2["perm"], t, 512).then_inc(rot_ready, 1)
            units_done(pe, ph.unit0 + ph.units)

            def stick_scores(n):
                if n >= 2:
                    pe.wait_ge(z_masked, n - 1)
                q, k = half(a2["q"], n // 2, n % 2), half(a2["k"], n // 2, n % 2)
                nc.tensor.matmul(sco[n % 2][:, 0:S], k[:, 0:P], q, start=True, stop=False, skip_group_check=True)
                nc.tensor.matmul(sco[n % 2][:, S:384], k[:, P:S], q[:, P:S], start=False, stop=False, skip_group_check=True)\
                    .then_inc(z_ready, 1)

            def stick_sums(n):
                out, lm = sco[n % 2], two(a2["lm"], n)
                pe.wait_ge(lm_ready, n + 1)
                nc.tensor.matmul(out[:, 0:S], a2["tri"], lm[:, 0:S], start=False, stop=False, skip_group_check=True)
                nc.tensor.matmul(out[:, S:384], a2["tri"], lm[:, S:384], start=False, stop=False, skip_group_check=True)
                nc.tensor.matmul(out[:, P:S], ones[:, 0:P], lm[:, S:384], start=False, stop=True, skip_group_check=True)\
                    .then_inc(z_sum, 1)

            stick_scores(0)
            stick_scores(1)
            for n in range(SB_HEADS + 1):
                if n < SB_HEADS:
                    stick_sums(n)
                if n:
                    pe.wait_ge(stick, n)
                    values(n - 1, two(a2["pT"], n - 1), lambda kt, n=n: v2[:, kt, HD * (n - 1):HD * n], PAIRS1 + (n - 1) // 2)
                if n + 2 < SB_HEADS:
                    stick_scores(n + 2)
            pe.wait_ge(z_masked, SB_HEADS)
            pe.wait_ge(rot_done, 6)
            softmax_heads(heads2, HEADS1, a2, PAIRS1 + PAIRS_SB)

            ph = PH["att_o"]
            for c in range(ph.n):
                by_feature(ph, Step(c), (o_tiles, 0) if c == 0 else None)
            pe.wait_ge(scores_read, HEADS1 + HEADS2)
            norm(L0F)
            up_phase("gu0", L0F)
            down_phase("dn0", FT)

            norm(L1)
            ph = PH["ret_in"]
            for c in range(ph.n):
                if 8 <= c < 16:
                    by_row(ph, Step(c))
                else:
                    by_feature(ph, Step(c), (h_tiles, tiles_before(L1)) if c == 0 else None)
            units_done(pe, ph.unit0 + ph.units)
            rv = v3(rt["v"], 2)

            def ret_scores(h):
                out = sco[h % 2]
                if h >= 2:
                    pe.wait_ge(ret_inner, h - 1)
                for kt, (a, b) in enumerate(((0, S), (S, 384))):
                    for d in range(2):
                        t = (2 * h + d) * S
                        ins = nc.tensor.matmul(out[:, a:b], rt["k"][:, t + kt * P:t + kt * P + P], rt["q"][:, t + kt * P:t + S],
                                               start=kt == 0 and d == 0, stop=kt == 1 and d == 1, skip_group_check=True)
                ins.then_inc(ret_s, 1)

            ret_scores(0)
            for h in range(RET_H):
                if h + 1 < RET_H:
                    ret_scores(h + 1)
                inner = two(rt["inner"], h)
                pe.wait_ge(ret_inner, h + 1)
                if h >= 2:
                    pe.wait_ge(ret_norm, 2 * (h - 1))
                o = (tra + att)[2 * (h % 2):2 * (h % 2) + 2]
                v = slice(h * RET_DV, (h + 1) * RET_DV)
                nc.tensor.matmul(o[0][:, :], inner[:, 0:P], rv[:, 0, v], start=True, stop=True).then_inc(ret_o, 1)
                nc.tensor.matmul(o[1][:, :], inner[:, P:S], rv[:, 0, v], start=True, stop=False)
                nc.tensor.matmul(o[1][:, :], inner[:, S:384], rv[:, 1, v], start=False, stop=True).then_inc(ret_o, 1)
                pe.wait_ge(ret_norm, 2 * h + 2)
                for m in range(2):
                    if h:
                        pe.wait_ge(ret_y, 2 * (h - 1) + m + 1)
                    for b in range(2):
                        for q in range(2):
                            src = rt["on"][:, 512 * q + (2 * m + b) * P:512 * q + (2 * m + b + 1) * P]
                            ins = nc.tensor.transpose(lin[m][:, b * S + q * P:b * S + q * P + P], src, ident[:, :])
                    ins.then_inc(ret_tr, 1)

            ph = PH["ret_o"]
            pe.wait_ge(ret_tiles, 8)
            for c in range(ph.n):
                by_feature(ph, Step(c), rhs=(hid_hi, hid_lo))
            norm(L1F)
            up_phase("gu1", L1F)
            down_phase("dn1", 2 * FT)
            norm(FINAL)

        @block.vector
        def _(dve):
            chain = [0]

            def link(ins):
                chain[0] += 1
                ins.then_inc(dve_chain, 1)
                dve.wait_ge(dve_chain, chain[0])

            tt, stt, ts = nc.vector.tensor_tensor, nc.vector.scalar_tensor_tensor, nc.vector.tensor_scalar

            def lo(chunk, step=None, ph=None):
                if chunk >= CHUNKS:
                    return
                of, c = phase_of(chunk)
                at = (lambda f: f(chunk)) if step is None else (lambda f: step.n(lambda c: f(ph.chunk0 + c + 1)))
                s = chunk % SPLIT_SLOTS
                for half, (a, b) in enumerate(of.halves(c)):
                    dve.wait_ge(hi_ready, at(lambda k: 2 * k + half + 1))
                    tt(w_lo[s][:, a:b], raw[chunk % RAW_SLOTS][:, a:b], w_hi[s][:, a:b].bitcast(F32), ALU.subtract)\
                        .then_inc(split_ready, 1)

            def rstd(i):
                sizes = NORM_GROUPS[i]
                n = 2 * len(sizes)
                dve.wait_ge(ssum_ready, i + 1)
                for g, nt in enumerate(sizes):
                    ins = ts(stat[:, 2 * g:2 * g + 2], ssum[:, 2 * g:2 * g + 2], 1.0 / (nt * P), EPS, ALU.mult, ALU.add)
                ins.then_inc(ms_ready, 1)
                refine(root_ready, i + 1, stat, n)
                if i:
                    dve.wait_ge(rbc_ready, i)
                for c in range(n):
                    ts(diag[:, c * P:(c + 1) * P], ident[:, :], stat[:, 24 + c:25 + c], -0.5, ALU.mult, ALU.mult).then_inc(diag_ready, 1)

            def refine(ready, count, st, n):
                m, r, a = st[:, 0:n], st[:, 12:12 + n], st[:, 18:18 + n]
                dve.wait_ge(ready, count)
                link(nc.vector.reciprocal(r, st[:, 6:6 + n]))
                link(tt(a, r, m, ALU.mult))
                link(tt(a, a, r, ALU.mult))
                link(stt(st[:, 24:24 + n], a, -3.0, r, ALU.add, ALU.mult))

            def scale_tile(i, k):
                src, _, tmp, gain_ = NORM[i][:4]
                cut = slice(k * S, (k + 1) * S)
                return stt(tmp[:, cut], src[:, cut], gain_(k), rbc[group_of(i, k)], ALU.mult, ALU.mult)

            def scale_tiles(i, then):
                dve.wait_ge(rbc_ready, i + 1)
                n = norm_tiles(i)
                for k in range(n + 1):
                    if k < n:
                        scale_tile(i, k).then_inc(t_ready, 1)
                    if k:
                        then(k - 1)

            def norm_h(i):
                _, _, tmp, _, shift, hi_, lo_ = NORM[i]

                def rest_of(k):
                    cut = slice(k * S, (k + 1) * S)
                    dve.wait_ge(hh_ready, tiles_before(i) + k + 1)
                    if shift(k) is None:
                        ins = tt(lo_[:, cut], tmp[:, cut], hi_[:, cut].bitcast(F32), ALU.subtract)
                    else:
                        ins = stt(lo_[:, cut], tmp[:, cut], shift(k), hi_[:, cut].bitcast(F32), ALU.add, ALU.subtract)
                    ins.then_inc(h_tiles, 1)

                rstd(i)
                scale_tiles(i, rest_of)

            def norm_residual(i):
                def add(k):
                    cut = slice(k * S, (k + 1) * S)
                    dve.wait_ge(t_ready, scaled_before(i) + k + 1)
                    tt(x[:, cut], x[:, cut], e0["y"][:, cut], ALU.add).then_inc(x_tiles, 1)

                rstd(i)
                scale_tiles(i, add)

            def piece(step, f):
                slot = f(step.j) % 2
                sums, o = ada_sums[:, 2 * slot:2 * slot + 2], COLS["ada_b"][0]
                dve.wait_ge(ada_in[slot], step.n(lambda c: 16 * (f(c) // 2 + 1)))
                for b in range(2):
                    w = ada_raw[slot][:, b * D:(b + 1) * D]
                    ins = nc.vector.tensor_tensor_reduce(w, w, cond_silu, 1.0, 0.0, ALU.mult, ALU.add, sums[:, b:b + 1])
                ins.then_inc(ada_sum, 1)
                dve.wait_ge(ada_sum, step.n(lambda c: f(c) + 1))
                tt(mod[:, bass.ds(step.n(lambda c: 2 * f(c)), 2)], sums, cols[:, bass.ds(step.n(lambda c: o + 2 * f(c)), 2)],
                   ALU.add).then_inc(ada_out, 1)

            def pieces(name, step):
                for m in range(ada_here(name, step.j)):
                    piece(step, lambda c, m=m: ada_before(name, c) + m)

            link(nc.vector.memset(ones[:, :], 1.0))
            dve.wait_ge(cols_in, 16)
            nc.vector.memset(diag[:, 0:1], 0.0).then_inc(ones_ready, 1)
            dve.wait_ge(cols_in, 16)
            dve.wait_ge(ident_in, 16)
            dve.wait_ge(x_in, 16)
            norm_h(PRE)
            lo(0)
            dve.wait_ge(tab1_in, 16)
            dve.wait_ge(cond_ready, 1)
            ph = PH["w_in"]

            def rotary(n, tile, cos, sin, nt):
                dve.wait_ge(rot_ready, n + 1)
                rot = tra[ROT_BANK[n]][:, 0:nt * S]
                link(tt(v3(tile, nt), v3(tile, nt), over(cos, nt), ALU.mult))
                tmp = ROT_TMP[n]
                link(tt(v3(tmp, nt), v3(rot, nt), over(sin, nt), ALU.mult))
                tt(tile, tile, tmp, ALU.add).then_inc(rot_done, 1)

            ROT_BANK = [0, 1, 0, 1, 0, 1]
            ROT_TMP = [a1["pT"][:, 2 * S:3 * S]] * 2 + [a2["rot"]] * 4
            for c in range(ph.n):
                lo(ph.chunk0 + c + 1)
                if c == 4:
                    rstd(LATENT)
                if c == 5:
                    _, _, lat_t, _, _, lat_hi, lat_lo = NORM[LATENT]

                    def lat_rest(k):
                        cut = slice(k * S, (k + 1) * S)
                        dve.wait_ge(hh_ready, tiles_before(LATENT) + k + 1)
                        tt(lat_lo[:, cut], lat_t[:, cut], lat_hi[:, cut].bitcast(F32), ALU.subtract).then_inc(h_tiles, 1)

                    scale_tiles(LATENT, lat_rest)
                if c == 6:
                    rotary(0, a1["kr"], a1["cos"], a1["sin"], 1)
                pieces(ph.name, Step(c))
            dve.wait_ge(f_ln, 1)
            link(stt(gate_tmp[:, 4 * S:5 * S], gate_tmp[:, 0:S], 0.0, gate_tmp[:, 3 * S:4 * S], ALU.min, ALU.subtract))
            link(nc.vector.tensor_tensor_scan(a1["f"][0:4, :], ones[0:4, :], gate_tmp[:, 4 * S:5 * S], 0.0, ALU.mult, ALU.add))
            ts(a1["fneg"][0:4, :], a1["f"][0:4, :], -1.0, None, ALU.mult).then_inc(f_ready, 1)
            lo(PH["w_out"].chunk0)
            rotary(1, a1["qr"], a1["cos"], a1["sin"], 1)

            def score_head(n, base, head, a):
                hs = head_stats(n)
                s, out = three_of(a["s"], n), sco[n % 2]
                dve.wait_ge(scores, base + n + 1)
                if n >= 3:
                    dve.wait_ge(trans, base + n - 2)
                first = NEG * 3 if head["sink"] is None else head["sink"]
                nc.vector.tensor_tensor_reduce(s[:, 0:P], out[:, 0:P], head["bias"][0], 1.0, first, ALU.add, ALU.max, hs[:, 0:1])
                link(nc.vector.tensor_tensor_reduce(s[:, P:384], out[:, P:384], head["bias"][1], 1.0, first, ALU.add, ALU.max,
                                                    hs[:, 1:2]))
                ts(hs[:, 2:4], hs[:, 0:2], -1.0, None, ALU.mult).then_inc(scores_read, 1)

            def weigh_head(n, base, head, a):
                hs = head_stats(n)
                s = three_of(a["s"], n)
                dve.wait_ge(exps, base + n + 1)
                total = hs[:, 4:6]
                if head["sink"] is not None:
                    link(tt(hs[:, 8:10], hs[:, 4:6], hs[:, 6:8], ALU.add))
                    total = hs[:, 8:10]
                link(nc.vector.reciprocal(hs[:, 10:12], total))
                ts(s[:, 0:P], s[:, 0:P], hs[:, 10:11], None, ALU.mult)
                ts(s[:, P:384], s[:, P:384], hs[:, 11:12], None, ALU.mult).then_inc(probs, 1)

            def softmax_heads(heads, base, a, pair_out, attention, head0=0):
                score_head(0, base, heads[0], a)
                for n in range(len(heads)):
                    if n + 1 < len(heads):
                        score_head(n + 1, base, heads[n + 1], a)
                    weigh_head(n, base, heads[n], a)
                    if n >= 3 and n % 2:
                        pair_out((n - 3) // 2)
                    pieces(attention, Step(head0 + n))
                pair_out(len(heads) // 2 - 1)

            def pair_to_mixed(j):
                dve.wait_ge(pv, 2 * j + 2)
                nc.vector.tensor_copy(a1["mixed"][:, j * S:(j + 1) * S], att[j % 2][:, 0:S]).then_inc(att_out, 1)

            dve.wait_ge(bias_in, 16)
            softmax_heads(heads1, 0, a1, pair_to_mixed, "att1")
            norm_h(GROUP)
            ph = PH["w_out"]
            for c in range(ph.n):
                lo(ph.chunk0 + c + 1)
                pieces(ph.name, Step(c))
            units_done(dve, ph.unit0 + ph.units)
            norm_residual(POST)
            norm_h(FFNPRE)

            ph = PH["up"]
            cw = COLS["conv_w"][0]

            def taps(step):
                j = step.j - 1
                bank = lin[(ph.unit0 + j) % 2]
                dve.wait_ge(conv_in, step.n(lambda c: c))
                for back in (1, 2):
                    for s in range(2):
                        u = ff["u"][:, 512 * (j % 2) + S * s:512 * (j % 2) + S * s + S]
                        w = cols[:, bass.ds(step.n(lambda c: cw + 44 * (2 - back) + 2 * (c - 1) + s), 1)]
                        if back == 2:
                            dve.wait_ge(conv_tap, step.n(lambda c: 2 * (c - 1) + s + 1))
                        ins = stt(u[:, back:S], bank[:, S * s:S * s + S - back], w, u[:, back:S], ALU.mult, ALU.add)
                        if back == 1:
                            ins.then_inc(conv_tap, 1)
                ins.then_inc(lin_free[(ph.unit0 + j) % 2], 1)

            def product(step, lag, base, up):
                j = step.j - lag
                dve.wait_ge(gelu_ready, step.n(lambda c: base + c - lag + 1))
                return tt(ff["hid"][:, S * (j % 2):S * (j % 2) + S], up, ff["g"][:, S * (j % 2):S * (j % 2) + S], ALU.mult)

            def rest(step, lag, base):
                j = step.j - lag
                dve.wait_ge(hid_hh, step.n(lambda c: base + c - lag + 1))
                cut = bass.ds(step.n(lambda c: (c - lag) * S), S)
                tt(hid_lo[:, cut], ff["hid"][:, S * (j % 2):S * (j % 2) + S], hid_hi[:, cut].bitcast(F32), ALU.subtract)\
                    .then_inc(hid_tiles, 1)

            def u_up(step, lag):
                j = step.j - lag
                return ff["u"][:, 512 * (j % 2) + S:512 * (j % 2) + 2 * S]

            def up_step(step):
                c = step.j
                if c < ph.n:
                    lo(ph.chunk0 + c + 1, step if step.i is not None else None, ph)
                if c >= 2:
                    product(step, 2, 0, u_up(step, 2)).then_inc(hid_ready, 1)
                if 1 <= c <= ph.n:
                    taps(step)
                if c >= 2:
                    rest(step, 2, 0)

            steps(dve, ph.n, 2, 1, up_step)
            up_step(Step(ph.n))
            up_step(Step(ph.n + 1))

            ph = PH["down"]

            def down_step(ph, step, out):
                lo(ph.chunk0 + step.j + 1, step if step.i is not None else None, ph)
                if out is not None and step.j >= 2 and step.j % 2 == 0:
                    out(Step(step.j - 1, step.i))
                pieces(ph.name, step)

            steps(dve, ph.n, 4, 1, lambda s: down_step(ph, s, None))
            units_done(dve, ph.unit0 + ph.units)
            norm_residual(FFNPOST)

            def gain(i):
                n = (L0, L0F, L1, L1F).index(i)
                layer, which = n // 2, 1 + 3 * (n % 2)
                dve.wait_ge(ada_out, ADA_PIECES * layer + 4 * (which + 1))
                at = 48 * layer + 8 * which
                link(stt(gscale[:, 8 * n:8 * n + 8], mod[:, at:at + 8], 1.0, col("norms2", 8 * n, 8), ALU.add, ALU.mult))

            def residual_units(ph, layer, which):
                w = 2 // ph.per_unit if ph.nb == 2 else 1

                def out(step):
                    u = (step.j + 1) // ph.per_unit - 1
                    dve.wait_ge(half_done, step.n(lambda c: 2 * (ph.chunk0 + c + 1)))
                    for b in range(w):
                        k = lambda c, b=b: ((c + 1) // ph.per_unit - 1) * w + b
                        xk = x[:, bass.ds(step.n(lambda c: k(c) * S), S)]
                        gate = mod[:, bass.ds(step.n(lambda c: 48 * layer + 8 * which + k(c)), 1)]
                        ins = stt(xk, lin[(ph.unit0 + u) % 2][:, b * S:(b + 1) * S], gate, xk, ALU.mult, ALU.add)
                    leave(ins, ph.unit0 + u)
                return out

            gain(L0)
            norm_h(L0)
            ph = PH["qkv"]
            dve.wait_ge(tab2_in, 16)
            for c in range(ph.n):
                lo(ph.chunk0 + c + 1)
                if c >= 9:
                    r = c - 9
                    rotary(2 + r, a2["q" if r < 2 else "k"][:, (4 + r % 2 * 2) * S:(6 + r % 2 * 2) * S], a2["cos"], a2["sin"], 2)
                pieces(ph.name, Step(c))
            rotary(5, a2["k"][:, 6 * S:8 * S], a2["cos"], a2["sin"], 2)

            def pair_to_split(j):
                dve.wait_ge(o_hi, j + 1)
                tt(h_lo[:, j * S:(j + 1) * S], att[(PAIRS1 + j) % 2][:, 0:S], h_hi[:, j * S:(j + 1) * S].bitcast(F32), ALU.subtract)\
                    .then_inc(o_tiles, 1)

            for n in range(SB_HEADS + 1):
                if n < SB_HEADS:
                    lm, z = two(a2["lm"], n), sco[n % 2][:, 0:384]
                    dve.wait_ge(z_ln, n + 1)
                    if n >= 2:
                        dve.wait_ge(z_sum, n - 1)
                    link(stt(lm, z, 0.0, two(a2["e"], n), ALU.max, ALU.add))
                    tt(lm, lm, a2["strict"], ALU.mult).then_inc(lm_ready, 1)
                if n:
                    dve.wait_ge(z_sum, n)
                    if n >= 3:
                        dve.wait_ge(stick, n - 2)
                    tt(two(a2["s"], n - 1), sco[(n - 1) % 2][:, 0:384], a2["strictneg"], ALU.add).then_inc(z_masked, 1)
                if n >= 3 and n % 2:
                    pair_to_split((n - 3) // 2)
                if n < SB_HEADS:
                    pieces("att2", Step(n))
            pair_to_split(3)
            softmax_heads(heads2, HEADS1, a2, lambda j: pair_to_split(PAIRS_SB + j), "att2", SB_HEADS)

            ph = PH["att_o"]
            out = residual_units(ph, 0, 2)
            dve.wait_ge(ada_out, 12)
            for c in range(ph.n):
                lo(ph.chunk0 + c + 1)
                if c:
                    out(Step(c - 1))
                pieces(ph.name, Step(c))
            out(Step(ph.n - 1))
            units_done(dve, ph.unit0 + ph.units)
            gain(L0F)
            norm_h(L0F)

            def swiglu(ph, base):
                def one(step):
                    c = step.j
                    if c < ph.n:
                        lo(ph.chunk0 + c + 1, step if step.i is not None else None, ph)
                    if c >= 1:
                        bank = (ph.unit0 + c - 1) % 2
                        product(step, 1, base, lin[bank][:, S:2 * S]).then_inc(lin_free[bank], 1)
                        rest(step, 1, base)
                    if c < ph.n:
                        pieces(ph.name, step)

                steps(dve, ph.n, 2, 1, one)
                one(Step(ph.n))

            def down(ph, layer):
                out = residual_units(ph, layer, 5)
                dve.wait_ge(ada_out, ADA_PIECES * (layer + 1))
                steps(dve, ph.n, 4, 1, lambda s: down_step(ph, s, out))
                out(Step(ph.n - 1))

            swiglu(PH["gu0"], FT)
            down(PH["dn0"], 0)
            units_done(dve, PH["dn0"].unit0 + PH["dn0"].units)
            gain(L1)
            norm_h(L1)
            ph = PH["ret_in"]
            dve.wait_ge(tab3_in, 16)

            def ret_rotary(c):
                bank = v3(lin[(ph.unit0 + c) % 2][:, :], 2)
                to = v3(rt["q" if c < 4 else "k"][:, c % 4 * 512:c % 4 * 512 + 512], 2)
                rot = v3(rt["rot"], 2)
                dve.wait_ge(half_done, 2 * (ph.chunk0 + c + 1))
                link(tt(to, bank, over(rt["cos"], 2), ALU.mult))
                leave(tt(rot, bank, over(rt["sin"], 2), ALU.mult), ph.unit0 + c)
                dve.wait_ge(lin_free[(ph.unit0 + c) % 2], (ph.unit0 + c) // 2 + 1)
                tt(to[:, 0, :], to[:, 0, :], rot[:, 1, :], ALU.subtract)
                link(tt(to[:, 1, :], to[:, 1, :], rot[:, 0, :], ALU.add))

            for c in range(ph.n):
                lo(ph.chunk0 + c + 1)
                if 1 <= c <= 8:
                    ret_rotary(c - 1)

            def ret_decay(h):
                dve.wait_ge(ret_s, h + 1)
                if h >= 2:
                    dve.wait_ge(ret_o, 2 * (h - 1))
                tt(two(rt["inner"], h), sco[h % 2][:, 0:384], rt["decay"][:, h * 384:(h + 1) * 384], ALU.mult)\
                    .then_inc(ret_inner, 1)

            ret_decay(0)
            for h in range(RET_H):
                if h + 1 < RET_H:
                    ret_decay(h + 1)
                gs = gn_stat[:, 32 * (h % 2):32 * (h % 2) + 32]
                o = (tra + att)[2 * (h % 2):2 * (h % 2) + 2]
                dve.wait_ge(ret_o, 2 * h + 2)
                for q in range(2):
                    link(nc.vector.bn_stats(gs[:, 6 * q:6 * q + 6], o[q][:, :]))
                    link(nc.vector.bn_aggr(gs[:, 12 + 2 * q:14 + 2 * q], gs[:, 6 * q:6 * q + 6]))
                mv = v3(gs[:, 12:16], 2)
                ts(gs[:, 16:18], mv[:, :, 1], GN_EPS, None, ALU.add).then_inc(ret_var, 1)
                dve.wait_ge(ret_rsq, h + 1)
                link(tt(gs[:, 22:24], gs[:, 20:22], gs[:, 20:22], ALU.mult))
                link(tt(gs[:, 22:24], gs[:, 22:24], gs[:, 16:18], ALU.mult))
                link(ts(gs[:, 22:24], gs[:, 22:24], -0.5, 1.5, ALU.mult, ALU.add))
                link(tt(gs[:, 24:26], gs[:, 22:24], gs[:, 20:22], ALU.mult))
                stt(gs[:, 28:30], mv[:, :, 0], -1.0, gs[:, 24:26], ALU.mult, ALU.mult).then_inc(ret_rstd, 1)
                for m in range(2):
                    dve.wait_ge(ret_tr, 2 * h + m + 1)
                    to = rt["o"] if m == 0 else rt["rot"]
                    for b in range(2):
                        t = 4 * h + 2 * m + b
                        ins = stt(to[:, b * S:(b + 1) * S], lin[m][:, b * S:(b + 1) * S], col("gn", t), rt["g"][:, t * S:(t + 1) * S],
                                  ALU.mult, ALU.mult)
                    ins.then_inc(ret_y, 1)
                    t = (4 * h + 2 * m) * S
                    dve.wait_ge(ret_hh, 2 * h + m + 1)
                    tt(hid_lo[:, t:t + 512], to, hid_hi[:, t:t + 512].bitcast(F32), ALU.subtract).then_inc(ret_tiles, 1)

            ph = PH["ret_o"]
            out = residual_units(ph, 1, 2)
            for c in range(ph.n):
                lo(ph.chunk0 + c + 1)
                if c:
                    out(Step(c - 1))
            out(Step(ph.n - 1))
            units_done(dve, ph.unit0 + ph.units)
            gain(L1F)
            norm_h(L1F)
            swiglu(PH["gu1"], 2 * FT)
            down(PH["dn1"], 1)
            units_done(dve, PH["dn1"].unit0 + PH["dn1"].units)
            rstd(FINAL)
            dve.wait_ge(rbc_ready, FINAL + 1)
            for k in range(DT):
                scale_tile(FINAL, k).then_inc(x_tiles, 1)


def tables():
    f32 = np.float32
    key, query = np.arange(P)[:, None], np.arange(P)[None, :]
    zero, full = np.zeros((P, P), f32), np.ones((P, P), f32)
    causal = np.where(query <= key, 0.0, NEG).astype(f32)
    mask = np.concatenate([causal, zero, causal], 1)
    earlier = (key < query).astype(f32)
    strict = np.concatenate([earlier, full, earlier], 1)
    strict_neg = np.where(strict > 0, 0.0, NEG).astype(f32)

    def rope(dim, repeat):
        inv = (f32(THETA) ** (-(np.arange(dim // 2, dtype=f32) * f32(2.0) / f32(dim)))).astype(f32)
        ang = np.arange(S, dtype=f32)[None, :] * inv[:, None]
        c, s = np.cos(ang.astype(np.float64)).astype(f32), np.sin(ang.astype(np.float64)).astype(f32)
        return np.tile(c, (repeat, 1)), np.tile(s, (repeat, 1))

    def swap(dim):
        m = np.zeros((P, P), f32)
        for o in range(P):
            half = dim // 2
            if o % dim < half:
                m[o + half, o] = -1.0
            else:
                m[o - half, o] = 1.0
        return m

    dist = 255 - np.arange(BAND)
    exact = BUCKETS // 2
    near = np.maximum(dist, 1).astype(f32) / f32(exact)
    ratio = np.log(near).astype(f32) / f32(math.log(MAX_DIST / exact))
    large = np.minimum(exact + (ratio * f32(BUCKETS - exact)).astype(np.int32), BUCKETS - 1)
    bucket = np.where(dist < exact, np.maximum(dist, 0), large)
    inside = (dist >= 0) & (dist < WINDOW)
    onehot = np.zeros((BUCKETS + 1, BAND), f32)
    onehot[:BUCKETS] = (np.arange(BUCKETS)[:, None] == bucket[None, :]) & inside[None, :]
    onehot[BUCKETS] = np.where(inside, 0.0, NEG)
    decay = []
    pos = np.arange(S)
    for h in range(RET_H):
        diff = pos[None, :] - pos[:, None]
        full_decay = np.where(diff >= 0, np.exp(math.log(1.0 - 2.0 ** (-5 - h)) * np.maximum(diff, 0)), 0.0)
        full_decay = (full_decay / 16.0).astype(f32)
        decay += [full_decay[:P, :], full_decay[P:, P:]]
    c1, s1 = rope(ROPE, 8)
    c2, s2 = rope(HD, 4)
    c3, s3 = rope(256, 1)
    return {
        "ident": np.eye(P, dtype=f32),
        "tab1": np.concatenate([mask, c1, s1, swap(ROPE)], 1),
        "onehot": onehot,
        "tab2": np.concatenate([mask, c2, s2, swap(HD), (key >= query).astype(f32), -strict, strict_neg], 1),
        "tab3": np.concatenate([c3, s3] + decay, 1),
    }


def lay_out(i):
    f32 = np.float32

    def chunks(w, width):
        k, n = w.shape
        a = w.reshape(k // P, P, n // width, width).transpose(2, 1, 0, 3)
        return np.ascontiguousarray(a).reshape(n // width * P, k // P * width)

    def blocks(w):
        k, n = w.shape
        a = w.reshape(k // P, P, n // 256, 2, P).transpose(2, 1, 3, 0, 4)
        return np.ascontiguousarray(a).reshape(n // 256 * P, k // P * 256)

    def mixed_chunks(name, w):
        return np.concatenate([(chunks(w[:, 256 * c:256 * c + 256], 256) if PH[name].row(c) else blocks(w[:, 256 * c:256 * c + 256]))
                               for c in range(w.shape[1] // 256)], 0)

    def pad(a, n):
        return np.concatenate([a, np.zeros(a.shape[:-1] + (n - a.shape[-1],), f32)], -1)

    def columns(v):
        return np.ascontiguousarray(v.reshape(-1, P).T)

    arrays = tables()
    arrays["cond"] = np.tile(i["c_2"][0], (P, 1))
    arrays["x"] = np.ascontiguousarray(i["x"][0].T.reshape(DT, P, S).transpose(1, 0, 2)).reshape(P, DT * S)
    order = np.concatenate([np.r_[j * HD:(j + 1) * HD, (4 + j) * HD:(5 + j) * HD] for j in range(4)])
    heads = np.array([n // 2 + 4 * (n % 2) for n in range(8)])
    w = i["w_in"][0]
    a, f, m = w[:, :768], w[:, 768:1540], w[:, 1540:]
    w_in = np.concatenate([m[:, :384], np.tile(m[:, 384:416], (1, 4)), a[:, order], f[:, :512], a[:, 512:640],
                           pad(f[:, 768:772], P), f[:, 512:768], pad(a[:, 640:768], 2 * P)], 1)
    last = chunks(w_in[:, -256:-128], P)
    arrays["w_in"] = np.concatenate([mixed_chunks("w_in", w_in[:, :-256]), pad(last, CHUNK)], 0)
    uq = i["w_uq"][0].reshape(256, 4, 96)
    uq = np.concatenate([uq[:, :, :64].reshape(256, 256), uq[:, :, 64:].reshape(256, 128)], 1)
    ukv = i["w_ukv"][0].reshape(128, 4, 2, 64).transpose(0, 2, 1, 3).reshape(128, 512)
    arrays["mla"] = np.concatenate([chunks(uq, 384), ukv], 1)
    mixed = np.concatenate([order, np.arange(512, 1024)])
    arrays["w_out"] = blocks(i["w_out"][0][mixed])

    def paired(w):
        k, n = w.shape
        return w.reshape(k, 2, FT, P).transpose(0, 2, 1, 3).reshape(k, n)

    def halves(w):
        a = w.reshape(2, HALF, P, DT, P).transpose(3, 0, 2, 1, 4)
        return np.ascontiguousarray(a).reshape(2 * DT * P, HALF * P)

    arrays["up"] = blocks(paired(i["w_up"][0]))
    arrays["down"] = halves(i["w_down"][0])
    arrays["qkv"] = mixed_chunks("qkv", i["att_w_qkv_2"][0])
    arrays["att_o"] = blocks(i["att_w_o_2"][0])
    arrays["ret_in"] = mixed_chunks("ret_in", i["ret_w_in_2"][0])
    arrays["ret_o"] = chunks(i["ret_w_o_2"][0], P)
    for n in range(2):
        arrays[f"gu{n}"] = blocks(paired(i["ffn_w_gate_up_2"][n]))
        arrays[f"dn{n}"] = halves(i["ffn_w_down_2"][n])
    arrays["ada"] = np.concatenate([np.ascontiguousarray(w.T).reshape(ADA_PIECES, 2, P, D).transpose(0, 2, 1, 3).reshape(-1, 2 * D)
                                    for w in i["ada_w_2"]], 0)

    def conv(v):
        return columns(paired(v[None, :])[0])

    def rows(v):
        return np.concatenate([v, np.zeros((P - v.shape[0], v.shape[1]), f32)], 0)

    rel = np.concatenate([i["rel_bias"][:, heads], np.ones((1, 8), f32)], 0)
    vectors = {
        "pre": columns(i["attn_pre_norm"][0]), "qlat": columns(i["q_latent_norm"][0]),
        "kvlat": columns(i["kv_latent_norm"][0]), "group": columns(i["group_norm"][0][mixed]),
        "post": columns(i["attn_post_norm"][0]), "ffnpre": columns(i["ffn_pre_norm"][0]),
        "conv_w": np.concatenate([conv(i["conv_w"][0, t]) for t in range(3)], 1), "conv_b": conv(i["conv_b"][0]),
        "ffnpost": columns(i["ffn_post_norm"][0]), "norms2": columns(i["norm_gains_2"]),
        "ada_b": columns(i["ada_b_2"]), "gn": columns(i["ret_gn_2"][0]), "final": columns(i["final_norm_2"]),
        "sinks": np.tile(i["swa_sinks"][0][heads], (P, 1)),
        "fbias": rows(i["forget_bias"][0][:, None]), "rel": rows(rel),
    }
    arrays["cols"] = np.concatenate([vectors[n].astype(f32) for n in COLS], 1)
    return {n: np.ascontiguousarray(a) for n, a in arrays.items()}


def program(nc, arrays):
    dram = {n: nc.dram_tensor(f"in_{n}", a.shape, F32, kind="ExternalInput").ap() for n, a in arrays.items()}
    dram["out"] = nc.dram_tensor("out_0", (P, DT * S), F32, kind="ExternalOutput").ap()
    band = nc.dram_tensor("band", (8, BAND), F32, kind="Internal")
    rows = nc.dram_tensor("band_rows", (P, 8 * BAND), F32, kind="Internal")
    dram["band"], dram["band_rows"] = band.ap(), rows.ap()
    dram["band_repeat"] = bass.AP(band, 0, [[0, P], [1, 8 * BAND]])
    dram["band_skew"] = bass.AP(rows, P - 1, [[8 * BAND - 1, P], [BAND, 8], [1, S]])
    build(nc, dram)


def kernel(**inputs):
    import concourse.bacc as bacc
    from concourse.bass_utils import run_bass_kernel_spmd

    arrays = lay_out({n: np.asarray(a) for n, a in inputs.items()})
    nc = bacc.Bacc("TRN2", target_bir_lowering=False, num_devices=1)
    program(nc, arrays)
    result = run_bass_kernel_spmd(nc, [{f"in_{n}": a for n, a in arrays.items()}], core_ids=[0]).results[0]["out_0"]
    return np.ascontiguousarray(result.reshape(P, DT, S).transpose(2, 1, 0)).reshape(1, S, D)
```

```python
import math
from contextlib import ExitStack

import concourse.bass as bass
import numpy as np
from concourse import mybir

F32 = mybir.dt.float32
F32R = mybir.dt.float32r
ACT = mybir.ActivationFunctionType
ALU = mybir.AluOpType

P = 128
S = 256
D = 1024
DT = D // P
FF = 2816
FT = FF // P
HALF = FT // 2
EPS = 1e-6
GN_EPS = 1e-5
NEG = -1e30
HD = 64
ROPE = 32
BUCKETS, MAX_DIST, WINDOW = 32, 128, 128
BAND = 384
RET_H, RET_DV = 4, 512
THETA = 10000.0

RAW_SLOTS, SPLIT_SLOTS = 4, 2
CHUNK = 2048
UNROLL = 4

PHASES = [
    ("w_in", 9, DT, 2, 1), ("mla", 1, 1, 10, 1), ("w_out", 4, DT, 2, 1),
    ("up", 22, DT, 2, 1), ("down", 16, HALF, 1, 2),
    ("qkv", 12, DT, 2, 1), ("att_o", 4, DT, 2, 1), ("gu0", 22, DT, 2, 1), ("dn0", 16, HALF, 1, 2),
    ("ret_in", 24, DT, 2, 1), ("ret_o", 8, 2 * DT, 1, 1), ("gu1", 22, DT, 2, 1), ("dn1", 16, HALF, 1, 2),
]
MLA_UNITS = 4
ROW_CHUNKS = {"w_in": (7, 8), "qkv": range(8, 12), "ret_in": range(8, 16)}


class Phase:

    def __init__(self, name, n, kt, nb, per_unit, chunk0, unit0):
        self.name, self.n, self.kt, self.nb, self.per_unit = name, n, kt, nb, per_unit
        self.chunk0, self.unit0 = chunk0, unit0
        self.units = MLA_UNITS if name == "mla" else n // per_unit

    def size(self, c):
        if self.name == "w_in" and c == self.n - 1:
            return DT * P
        return self.kt * self.nb * P

    def row(self, c):
        return c in ROW_CHUNKS.get(self.name, ())

    def halves(self, c):
        n = self.size(c)
        if self.name == "mla":
            at = 2 * 3 * P
        else:
            at = n // 2 if n // P % 2 == 0 else (n // P + 1) // 2 * P
        return (0, at), (at, n)


def lay_out_phases():
    out, chunk, unit = {}, 0, 0
    for name, n, kt, nb, per in PHASES:
        ph = out[name] = Phase(name, n, kt, nb, per, chunk, unit)
        chunk, unit = chunk + n, unit + ph.units
    return out


PH = lay_out_phases()
ORDER = list(PH.values())
CHUNKS = sum(ph.n for ph in ORDER)


def phase_of(chunk):
    for ph in ORDER:
        if chunk < ph.chunk0 + ph.n:
            return ph, chunk - ph.chunk0


ADA_PIECES = 24
ADA_STEPS = [("w_in", 9, lambda c: int(c < 8) * (c % 2)), ("up", 22, lambda c: c % 2), ("down", 16, lambda c: c % 2),
             ("qkv", 12, lambda c: int(c < 5)), ("gu0", 22, lambda c: int(c % 2 or c == 0)), ("dn0", 16, lambda c: c % 2)]
ADA_AT = {name: f for name, _, f in ADA_STEPS}



def ada_before(name, c):
    n = 0
    for at, steps_, f in ADA_STEPS:
        if at == name:
            return n + sum(f(i) for i in range(c))
        n += sum(f(i) for i in range(steps_))


def ada_here(name, c):
    return ADA_AT[name](c) if name in ADA_AT else 0


COLS = {}
for _name, _n in [("pre", 8), ("qlat", 2), ("kvlat", 1), ("group", 8), ("post", 8), ("ffnpre", 8), ("conv_w", 132),
                  ("conv_b", 44), ("ffnpost", 8), ("norms2", 32), ("ada_b", 96), ("gn", 16), ("final", 8),
                  ("sinks", 8), ("fbias", 1), ("rel", 8)]:
    COLS[_name] = (sum(v[1] for v in COLS.values()), _n)
NCOLS = sum(v[1] for v in COLS.values())

TAB1 = [("mask", 384), ("cos", S), ("sin", S), ("perm", P)]
TAB2 = [("mask", 384), ("cos", S), ("sin", S), ("perm", P), ("tri", P), ("negones", P), ("strict", 384)]
TAB3 = [("cos", S), ("sin", S), ("decay", RET_H * 384)]

ARENA = 17152
ADA0 = ARENA - 2 * CHUNK
EARLY = [("y", 2048), ("sq", 2048)]
ATT1 = [("qa", 1024), ("qf", 512), ("qn", 512), ("ka", 256), ("kf", 512), ("v_a", 256), ("v_f", 512), ("kn", 512), ("v_m", 512),
        ("qr", 256), ("s", 1152), ("pT", 768), ("lat", 768), ("kr", 256), ("f", 256), ("fneg", 256), ("bias", 2048)] + TAB1
FFN = EARLY + [("u", 1024), ("g", 512), ("hid", 512)]
ATT2 = [("q", 2048), ("k", 2048), ("v", 2048)] + TAB2 + [("z", 384 * 8), ("s", 1152)]
RET = [("q", 2048), ("k", 2048), ("v", 4096)] + TAB3 + [("inner", 1536), ("t", 2048), ("sq", 1024), ("g", 2048), ("rb", S)]


TAB1_AT = sum(n for _, n in ATT1[:ATT1.index(TAB1[0])])
TAB2_AT = sum(n for _, n in ATT2[:ATT2.index(TAB2[0])])
TAB3_AT = sum(n for _, n in RET[:RET.index(TAB3[0])])


class Step:

    def __init__(self, j, i=None):
        self.j, self.i = j, i

    def n(self, f):
        if self.i is None:
            return f(self.j)
        by = f(self.j + UNROLL) - f(self.j)
        return self.i * by + f(self.j) if by else f(self.j)


def steps(eng, n, lead, tail, body):
    lead = min(lead, n)
    trips = (n - lead - tail) // UNROLL
    if trips < 2:
        trips = 0
    for c in range(lead):
        body(Step(c))
    if trips:
        with eng.Fori(0, trips) as i:
            for j in range(UNROLL):
                body(Step(lead + j, i))
    for c in range(lead + trips * UNROLL, n):
        body(Step(c))


NORM_GROUPS = [[8], [2, 1], [4, 2, 2], [8], [8], [8], [8], [8], [8], [8], [8]]
PRE, LATENT, GROUP, POST, FFNPRE, FFNPOST, L0, L0F, L1, L1F, FINAL = range(11)
AHEAD = {PRE: "w_in", GROUP: "w_out", FFNPRE: "up", L0: "qkv", L0F: "gu0", L1: "ret_in", L1F: "gu1"}
SPLIT_AHEAD = {norm: PH[name].chunk0 + 1 for norm, name in AHEAD.items()}
SPLITS = [PRE, LATENT, GROUP, FFNPRE, L0, L0F, L1, L1F]
RESIDUALS = [POST, FFNPOST, FINAL]


def norm_tiles(norm):
    return sum(NORM_GROUPS[norm])


def scaled_before(norm):
    return sum(norm_tiles(i) for i in range(norm))


def tiles_before(norm):
    return sum(norm_tiles(i) for i in SPLITS if i < norm)


def x_before(norm):
    return sum(norm_tiles(i) for i in RESIDUALS if i < norm)


def groups_before(norm):
    return sum(len(NORM_GROUPS[i]) for i in range(norm))


def gathered_before(norm):
    return sum(additions(i, n) for i in range(norm) for n in NORM_GROUPS[i])


def additions(norm, n):
    return max(n - 1 - (1 if norm == GROUP else 3), 0)


def group_of(norm, k):
    at = 0
    for g, n in enumerate(NORM_GROUPS[norm]):
        if k < at + n:
            return g
        at += n


HEADS1, HEADS2 = 16, 8
SB_HEADS, STICK = 8, 4
FILL = 3


def build(nc, dram):
    ctx = ExitStack()
    with ctx:
        def sb(name, n, dt=F32, parts=P):
            return ctx.enter_context(nc.sbuf_tensor(name, [parts, n], dt))

        def sem(name):
            return ctx.enter_context(nc.semaphore(name))

        raw = [sb(f"raw{i}", CHUNK) for i in range(RAW_SLOTS)]
        w_hi = [sb(f"w_hi{i}", CHUNK, F32R) for i in range(SPLIT_SLOTS)]
        w_lo = [sb(f"w_lo{i}", CHUNK, F32R) for i in range(SPLIT_SLOTS)]
        h_hi, h_lo = sb("h_hi", DT * S, F32R), sb("h_lo", DT * S, F32R)
        hid_hi, hid_lo = sb("hid_hi", FT * S, F32R), sb("hid_lo", FT * S, F32R)
        x = sb("x", DT * S)
        cols = sb("cols", NCOLS)
        ident, ones = sb("ident", P), sb("ones", S)
        mod = sb("mod", 96)
        gscale = sb("gscale", 32)
        ada_sums = sb("ada_sums", 4)
        diag = sb("diag", 6 * P)
        stat, warm = sb("stat", 32), sb("warm", 16)
        busy = sb("busy", S, F32R)
        head_stat = sb("head_stat", 3 * 16)
        ret_stat, v_sums = sb("ret_stat", 2 * 32), sb("v_sums", 24)
        arena = sb("arena", ARENA)
        cond_silu = arena[:, ADA0 - D:ADA0]
        ada_raw = [arena[:, ADA0 + i * CHUNK:ADA0 + (i + 1) * CHUNK] for i in range(2)]

        def parts(table, end=ADA0 - D):
            at, out = 0, {}
            for name, n in table:
                out[name] = arena[:, at:at + n]
                at += n
            assert at <= end, (at, end)
            return out

        e0, a1, ff, a2, rt = parts(EARLY), parts(ATT1), parts(FFN), parts(ATT2), parts(RET, ARENA)
        a2["e"], a2["pT"] = arena[:, ADA0:ADA0 + 3072], arena[:, ADA0 + 3072:ADA0 + 3840]
        a2["rot"] = diag[:, 0:2 * S]
        rt["rot"] = rt["t"][:, 0:2 * S]
        band, onehot = arena[0:8, 4096:4096 + BAND], arena[0:BUCKETS + 1, 4096 + BAND:4096 + 2 * BAND]
        S_AT = sum(n for _, n in ATT1[:ATT1.index(("s", 1152))])
        lat_sq, lat_y = arena[:, S_AT:S_AT + 768], arena[:, S_AT + 768:S_AT + 1536]
        GATE_AT = sum(n for _, n in ATT1[:ATT1.index(("kn", 512))])
        gate_tmp = arena[0:4, GATE_AT:GATE_AT + 5 * S]
        a1["mixed"] = arena[:, 0:DT * S]

        def col(name, j, n=1, rows=P):
            o = COLS[name][0]
            return cols[0:rows, o + j:o + j + n]

        psum = [ctx.enter_context(nc.psum_tensor(f"psum{i}", [P, 512], F32)) for i in range(8)]
        lin, sco, tra, att = psum[0:2], psum[2:4], psum[4:6], psum[6:8]
        ssum, rbc = sco[0][:, 0:6], (sco[1][:, 0:S], sco[1][:, S:2 * S], tra[0][:, 0:S])

        x_in = [sem(f"x_in{i}") for i in range(2)]
        cols_in, tab1_in, tab2_in, tab3_in = (sem(n) for n in ("cols_in", "tab1_in", "tab2_in", "tab3_in"))
        onehot_in, ident_in, band_out, bias_in, y_out = sem("onehot_in"), sem("ident_in"), sem("band_out"), sem("bias_in"), sem("y_out")
        raw_in = [sem(f"raw_in{i}") for i in range(RAW_SLOTS)]
        hi_ready, split_ready, half_done = sem("hi_ready"), sem("split_ready"), sem("half_done")
        lin_free = [sem(f"lin_free{i}") for i in range(2)]
        mla_units = sem("mla_units")
        ada_in = [sem(f"ada_in{i}") for i in range(2)]
        ada_sum, ada_out, cond_in, cond_ready = (sem(n) for n in ("ada_sum", "ada_out", "cond_in", "cond_ready"))
        ones_filled, band_ps, band_ready = sem("ones_filled"), sem("band_ps"), sem("band_ready")
        sq_ready, ssum_ready, ms_ready, root_ready = sem("sq_ready"), sem("ssum_ready"), sem("ms_ready"), sem("root_ready")
        diag_ready, rbc_ready, t_ready = sem("diag_ready"), sem("rbc_ready"), sem("t_ready")
        hh_ready, h_tiles, x_tiles = sem("hh_ready"), sem("h_tiles"), sem("x_tiles")
        sq_added, busy_ready = sem("sq_added"), sem("busy_ready")
        dve_chain, act_chain = sem("dve_chain"), sem("act_chain")
        rot_ready, rot_done, f_in, f_ln, f_ready = (sem(n) for n in (
            "rot_ready", "rot_done", "f_in", "f_ln", "f_ready"))
        scores, scores_read, exps, probs, trans, trans_out, pv, att_out, o_hi, o_tiles = (sem(n) for n in (
            "scores", "scores_read", "exps", "probs", "trans", "trans_out", "pv", "att_out", "o_hi", "o_tiles"))
        z_ready, z_masked, z_neg, z_exp, z_ln, lm_ready, z_sum, z_sticks, stick = (sem(n) for n in (
            "z_ready", "z_masked", "z_neg", "z_exp", "z_ln", "lm_ready", "z_sum", "z_sticks", "stick"))
        conv_in, conv_tap, gelu_ready, hid_ready, hid_hh, hid_tiles = (sem(n) for n in (
            "conv_in", "conv_tap", "gelu_ready", "hid_ready", "hid_hh", "hid_tiles"))
        ret_rot, ret_s, ret_inner, v_centred, ret_o, ret_sq, ret_added, ret_ssum, ret_ms, ret_root, ret_diag, ret_rbc = (
            sem(n) for n in ("ret_rot", "ret_s", "ret_inner", "v_centred", "ret_o", "ret_sq", "ret_added", "ret_ssum", "ret_ms",
                             "ret_root", "ret_diag", "ret_rbc"))
        ret_t, ret_y, ret_hh, ret_tiles = (sem(n) for n in ("ret_t", "ret_y", "ret_hh", "ret_tiles"))

        def units_done(eng, unit):
            for b in range(2):
                n = (unit + 1 - b) // 2
                if n > 0:
                    eng.wait_ge(lin_free[b], n)

        def unit_free(eng, ph, step, f):
            if ph.unit0 + f(step.j) >= 2:
                eng.wait_ge(lin_free[(ph.unit0 + f(step.j)) % 2], step.n(lambda c: (ph.unit0 + f(c)) // 2))

        def leave(ins, unit):
            return ins.then_inc(lin_free[unit % 2], 1)

        def v3(ap, n):
            return ap.rearrange("p (a b) -> p a b", a=n)

        def over(ap, n):
            return ap.unsqueeze(1).to_broadcast([ap.shape[0], n, ap.shape[1]])

        def mod_col(layer, which, k):
            return mod[:, 48 * layer + 8 * which + k:48 * layer + 8 * which + k + 1]

        hh, hl = h_hi[:, :], h_lo[:, :]
        no_shift = lambda k: None
        NORM = {
            PRE: (x[:, :], e0["sq"], e0["y"], lambda k: col("pre", k), no_shift, hh, hl),
            LATENT: (a1["lat"], lat_sq, lat_y, lambda k: col("qlat", k) if k < 2 else col("kvlat", 0), no_shift, hid_hi, hid_lo),
            GROUP: (a1["mixed"], a1["bias"], arena[:, 4096:6144], lambda k: col("group", k), no_shift, hh, hl),
            POST: (e0["y"], e0["sq"], e0["y"], lambda k: col("post", k), None, None, None),
            FFNPRE: (x[:, :], e0["sq"], e0["y"], lambda k: col("ffnpre", k), no_shift, hh, hl),
            FFNPOST: (e0["y"], e0["sq"], e0["y"], lambda k: col("ffnpost", k), None, None, None),
            FINAL: (x[:, :], e0["sq"], e0["y"], lambda k: col("final", k), None, None, None),
        }
        for i, layer, which in ((L0, 0, 0), (L0F, 0, 3), (L1, 1, 0), (L1F, 1, 3)):
            NORM[i] = (x[:, :], e0["sq"], e0["y"],
                       lambda k, i=i: gscale[:, 8 * (L0, L0F, L1, L1F).index(i) + k:8 * (L0, L0F, L1, L1F).index(i) + k + 1],
                       lambda k, layer=layer, which=which: mod_col(layer, which, k), hh, hl)

        def half(ap, tile, h):
            return ap[HD * h:HD * h + HD, tile * S:(tile + 1) * S]

        heads1 = []
        for n in range(8):
            pair, h = n // 2, n % 2
            bias = a1["bias"][:, n * S:(n + 1) * S]
            v = v3(a1["v_a"], 2)
            heads1.append(dict(parts=[(half(a1["qa"], pair, h), half(a1["ka"], 0, h))], bias=(bias[:, P:S], bias),
                               sink=col("sinks", n), v=lambda kt, v=v, h=h: v[:, kt, HD * h:HD * h + HD], decay=None))
        mask = a1["mask"]
        for n in range(4):
            v = v3(a1["v_f"], 2)
            heads1.append(dict(parts=[(half(a1["qf"], n // 2, n % 2), half(a1["kf"], n // 2, n % 2))],
                               bias=(mask[:, 0:P], mask[:, P:384]), sink=None, decay=n, needs=(f_ready, 1),
                               v=lambda kt, v=v, n=n: v[:, kt, HD * n:HD * n + HD]))
        for n in range(4):
            v = v3(a1["v_m"], 2)
            rope = slice(ROPE * n, ROPE * n + ROPE)
            heads1.append(dict(parts=[(half(a1["qn"], n // 2, n % 2), half(a1["kn"], n // 2, n % 2)),
                                      (a1["qr"][rope, :], a1["kr"][rope, :])],
                               bias=(mask[:, 0:P], mask[:, P:384]), sink=None, decay=None, needs=(rot_done, 2),
                               v=lambda kt, v=v, n=n: v[:, kt, HD * n:HD * n + HD]))
        heads2 = []
        mask2, v2 = a2["mask"], v3(a2["v"], 2)
        for n in range(8, 16):
            heads2.append(dict(parts=[(half(a2["q"], n // 2, n % 2), half(a2["k"], n // 2, n % 2))],
                               bias=(mask2[:, 0:P], mask2[:, P:384]), sink=None, decay=None,
                               v=lambda kt, n=n: v2[:, kt, HD * n:HD * n + HD]))

        PAIRS1 = HEADS1 // 2
        PAIRS_SB = SB_HEADS // 2

        def three_of(ap, n):
            return ap[:, n % 3 * 384:(n % 3 + 1) * 384]

        def head_stats(n):
            return head_stat[:, 16 * (n % 3):16 * (n % 3) + 16]

        def two(ap, n):
            return ap[:, n % 2 * 384:(n % 2 + 1) * 384]

        def ret_head(first):
            return lambda c: (c - first) // 2 if c >= first and (c - first) % 2 == 0 and c < first + 2 * RET_H else None

        AT_SCORES = {10 + h: h for h in range(RET_H)}
        AT_DECAY = {11 + h: h for h in range(RET_H)}
        at_centre, at_values, at_squares, at_sums = ret_head(11), ret_head(12), ret_head(13), ret_head(14)
        at_rstd, at_spread = ret_head(14), ret_head(14)
        AT_T = {15: 0, 17: 1, 20: 2, 22: 3}
        AT_Y = {19: 0, 21: 1, 23: 2, 24: 3}

        def ret_bank(h):
            return (tra, att)[h % 2]

        ret_rbc_of = lambda h: sco[1][:, h % 2 * S:h % 2 * S + S]

        def of_head(ap, n):
            return ap[:, n * 384:(n + 1) * 384]

        B0, B1 = range(0, STICK), range(STICK, SB_HEADS)
        PE_Z, PE_ROTATE, PE_SUMS = {4: B0, 5: B1}, {6: (0, 1), 7: (2,), 8: (3,)}, {9: B0, 10: B1}
        DVE_MASK, DVE_SOFTPLUS, DVE_REST = {5: B0, 6: B1}, {9: B0, 10: B1}, {10: B0, 11: B1}
        DVE_ROTATE = {7: (0, 1), 8: (2,), 9: (3,)}
        ACT_EXP, ACT_LN, ACT_WEIGHTS = {6: B0, 7: B1}, {8: B0, 9: B1}, {11: B0}
        stick_bank = lambda n: (sco + tra)[n % 4][:, 0:384]

        def rotated(r):
            return a2["q" if r < 2 else "k"][:, (4 + r % 2 * 2) * S:(6 + r % 2 * 2) * S]

        block = ctx.enter_context(nc.Block())

        @block.sync
        def _(sp):
            for k in (0, DT // 2):
                cut = slice(k * S, (k + DT // 2) * S)
                sp.dma_start(x[:, cut], dram["x"][:, cut]).then_inc(x_in[2 * k // DT], 16)
            sp.dma_start(cols[:, :], dram["cols"]).then_inc(cols_in, 16)
            sp.dma_start(onehot, dram["onehot"]).then_inc(onehot_in, 16)
            sp.dma_start(ident[:, :], dram["ident"]).then_inc(ident_in, 16)

            def load_ada(step, f):
                slot = f(step.j) % 2
                if f(step.j) >= 2:
                    sp.wait_ge(ada_out, step.n(lambda c: f(c) - 1))
                sp.dma_start(ada_raw[slot], dram["ada"][bass.ds(step.n(lambda c: f(c) * P), P), :]).then_inc(ada_in[slot], 16)

            def weights_of(ph):
                def load(step):
                    chunk = ph.chunk0 + step.j
                    slot, n = chunk % RAW_SLOTS, ph.size(step.j)
                    if chunk >= RAW_SLOTS:
                        sp.wait_ge(split_ready, step.n(lambda c: 2 * (ph.chunk0 + c - RAW_SLOTS + 1)))
                    src = dram[ph.name][bass.ds(step.n(lambda c: c * P), P), 0:n]
                    sp.dma_start(raw[slot][:, 0:n], src).then_inc(raw_in[slot], 16)
                return load

            def phase(ph):
                load = weights_of(ph)

                def one(step):
                    load(step)
                    if ph.name == "w_in" and step.j == 0:
                        sp.dma_start(cond_silu, dram["cond"]).then_inc(cond_in, 16)
                    if ph.name == "w_in" and step.j == 2:
                        sp.dma_start(arena[:, TAB1_AT:TAB1_AT + dram["tab1"].shape[1]], dram["tab1"]).then_inc(tab1_in, 16)
                    for m in range(ada_here(ph.name, step.j)):
                        load_ada(step, lambda c, m=m: ada_before(ph.name, c) + m)

                if ph.name == "qkv":
                    for c in range(ph.n):
                        load(Step(c))
                        for m in range(ada_here(ph.name, c - 2) if c >= 2 else 0):
                            load_ada(Step(c - 2), lambda c, m=m: ada_before(ph.name, c) + m)
                else:
                    steps(sp, ph.n, 4, 0, one)

            for ph in ORDER:
                if ph.name == "up":
                    sp.wait_ge(h_tiles, tiles_before(FFNPRE))
                    sp.dma_start(arena[:, TAB2_AT:TAB2_AT + dram["tab2"].shape[1]], dram["tab2"]).then_inc(tab2_in, 16)
                if ph.name == "gu0":
                    sp.wait_ge(o_tiles, 8)
                    sp.dma_start(arena[:, TAB3_AT:TAB3_AT + dram["tab3"].shape[1]], dram["tab3"]).then_inc(tab3_in, 16)
                phase(ph)
            for k in (0, DT // 2):
                sp.wait_ge(x_tiles, x_before(FINAL) + k + DT // 2)
                cut = slice(k * S, (k + DT // 2) * S)
                sp.dma_start(dram["out"][:, cut], e0["y"][:, cut]).then_inc(y_out, 16)
            sp.wait_ge(y_out, 32)

        @block.gpsimd
        def _(pool):
            added = [0]

            def add_squares(i):
                sq, k0 = NORM[i][1], 0
                for n in NORM_GROUPS[i]:
                    acc = sq[:, k0 * S:(k0 + 1) * S]
                    for k in range(k0 + 1, k0 + 1 + additions(i, n)):
                        pool.wait_ge(sq_ready, scaled_before(i) + k + 1)
                        if k > k0 + 1:
                            pool.wait_ge(sq_added, added[0])
                        nc.gpsimd.tensor_tensor(acc, acc, sq[:, k * S:(k + 1) * S], ALU.add).then_inc(sq_added, 1)
                        added[0] += 1
                    k0 += n

            def rest_ahead(chunk):
                of, c = phase_of(chunk)
                if chunk:
                    pool.wait_ge(split_ready, 2 * chunk)
                for half, (a, b) in enumerate(of.halves(c)):
                    pool.wait_ge(hi_ready, 2 * chunk + half + 1)
                    nc.gpsimd.tensor_tensor(w_lo[chunk % SPLIT_SLOTS][:, a:b], raw[chunk % RAW_SLOTS][:, a:b],
                                            w_hi[chunk % SPLIT_SLOTS][:, a:b].bitcast(F32), ALU.subtract).then_inc(split_ready, 1)

            def hidden(step):
                j = step.j
                at, cut = S * (j % 2), bass.ds(step.n(lambda c: c * S), S)
                hid = ff["hid"][:, at:at + S]
                pool.wait_ge(gelu_ready, step.n(lambda c: c + 1))
                nc.gpsimd.tensor_tensor(hid, ff["u"][:, 2 * at + S:2 * at + 2 * S], ff["g"][:, at:at + S], ALU.mult)\
                    .then_inc(hid_ready, 1)
                pool.wait_ge(hid_hh, step.n(lambda c: c + 1))
                nc.gpsimd.tensor_tensor(hid_lo[:, cut], hid, hid_hi[:, cut].bitcast(F32), ALU.subtract).then_inc(hid_tiles, 1)

            add_squares(PRE)
            pool.wait_ge(band_ready, 1)
            pool.dma_start(dram["band"], band).then_inc(band_out, 16)
            rest_ahead(0)
            rest_ahead(SPLIT_AHEAD[PRE])
            pool.wait_ge(band_out, 16)
            pool.dma_start(dram["band_rows"], dram["band_repeat"]).then_inc(band_out, 16)
            pool.wait_ge(band_out, 32)
            pool.dma_start(v3(a1["bias"], 8), dram["band_skew"]).then_inc(bias_in, 16)
            for i in range(len(NORM_GROUPS)):
                if i != PRE:
                    add_squares(i)
                if i in SPLIT_AHEAD and i != PRE:
                    rest_ahead(SPLIT_AHEAD[i])
                if i == L1:
                    for h in range(RET_H):
                        pool.wait_ge(ret_sq, 2 * h + 2)
                        nc.gpsimd.tensor_tensor(rt["sq"][:, 0:512], rt["sq"][:, 0:512], rt["sq"][:, 512:1024], ALU.add)\
                            .then_inc(ret_added, 1)
                if i == FFNPRE:
                    steps(pool, PH["up"].n, 2, 1, hidden)

        @block.scalar
        def _(act):
            chain = [0]

            def link(ins):
                chain[0] += 1
                ins.then_inc(act_chain, 1)
                act.wait_ge(act_chain, chain[0])

            def hi(chunk, step=None, ph=None, ahead=False):
                if chunk >= CHUNKS or chunk in SPLIT_AHEAD.values() and not ahead:
                    return
                of, c = phase_of(chunk)
                at = (lambda f: f(chunk)) if step is None else (lambda f: step.n(lambda c: f(ph.chunk0 + c + 1)))
                act.wait_ge(raw_in[chunk % RAW_SLOTS], at(lambda k: 16 * (k // RAW_SLOTS + 1)))
                for half, (a, b) in enumerate(of.halves(c)):
                    if chunk >= SPLIT_SLOTS:
                        before, cb = phase_of(chunk - SPLIT_SLOTS)
                        used = 1 if b <= before.halves(cb)[0][1] else 2
                        act.wait_ge(half_done, at(lambda k: 2 * (k - SPLIT_SLOTS) + used))
                    nc.scalar.activation(w_hi[chunk % SPLIT_SLOTS][:, a:b], raw[chunk % RAW_SLOTS][:, a:b], ACT.Copy)\
                        .then_inc(hi_ready, 1)

            def square(i, k=0, n=1, src=None):
                to, at = NORM[i][1], slice(k * S, (k + n) * S)
                nc.scalar.activation(to[:, at], NORM[i][0][:, at] if src is None else src, ACT.Square).then_inc(sq_ready, n)

            def root(i):
                n = 2 * len(NORM_GROUPS[i])
                nc.scalar.activation(warm[:, i:i + 1], ones[:, 0:1], ACT.Sqrt)
                act.wait_ge(ms_ready, i + 1)
                nc.scalar.activation(stat[:, 6:6 + n], stat[:, 0:n], ACT.Sqrt).then_inc(root_ready, 1)

            def round_h(i):
                _, _, tmp, _, shift, dst, _ = NORM[i]
                if i in SPLIT_AHEAD:
                    hi(SPLIT_AHEAD[i], ahead=True)
                for k in range(norm_tiles(i)):
                    cut = slice(k * S, (k + 1) * S)
                    act.wait_ge(t_ready, scaled_before(i) + k + 1)
                    if shift(k) is None:
                        ins = nc.scalar.activation(dst[:, cut], tmp[:, cut], ACT.Copy)
                    else:
                        ins = nc.scalar.activation(dst[:, cut], tmp[:, cut], ACT.Identity, bias=shift(k))
                    ins.then_inc(hh_ready, 1)

            def square_residual(i, residual):
                for k in range(DT):
                    act.wait_ge(x_tiles, x_before(residual) + k + 1)
                    square(i, k)

            act.wait_ge(ones_filled, 1)
            nc.scalar.activation(busy[:, :], ones[:, :], ACT.Copy).then_inc(busy_ready, 1)
            for k in range(0, DT, 2):
                if k % 4 == 0:
                    act.wait_ge(x_in[k // 4], 16)
                square(PRE, k, 2)
            act.wait_ge(band_ps, 1)
            nc.scalar.activation(band, tra[0][0:8, 0:BAND], ACT.Copy).then_inc(band_ready, 1)
            hi(0)
            root(PRE)
            round_h(PRE)
            act.wait_ge(cond_in, 16)
            nc.scalar.activation(cond_silu, cond_silu, ACT.Silu).then_inc(cond_ready, 1)

            ph = PH["w_in"]
            dst = {0: [(a1["lat"][:, 0:512], 0, 512, 1.0)],
                   1: [(a1["lat"][:, 512:768], 0, 256, 1.0), (a1["kr"], 256, 512, 1.0)],
                   2: [(a1["qa"][:, 0:512], 0, 512, HD ** -0.5)], 3: [(a1["qa"][:, 512:1024], 0, 512, HD ** -0.5)],
                   4: [(a1["qf"], 0, 512, HD ** -0.5)], 5: [(a1["kf"], 0, 512, 1.0)],
                   6: [(a1["ka"], 0, 256, 1.0)], 7: [(a1["v_f"], 0, 512, 1.0)]}

            def leave_w_in(c):
                act.wait_ge(half_done, 2 * (c + 1))
                bank = lin[c % 2]
                if c == 0:
                    act.wait_ge(h_tiles, 8)
                if c == 6:
                    nc.scalar.activation(gate_tmp[:, 0:S], bank[0:4, S:2 * S], ACT.Identity, bias=col("fbias", 0, 1, 4))\
                        .then_inc(f_in, 1)
                if c == 8:
                    ins = nc.scalar.activation(v3(a1["v_a"], 2), v3(bank[:, :], 2)[:, :, 0:P], ACT.Copy)
                else:
                    for to, a, b, scale in dst[c]:
                        ins = nc.scalar.activation(to, bank[:, a:b], ACT.Copy, scale=scale)
                leave(ins, c)

            for c in range(ph.n):
                hi(ph.chunk0 + c + 1)
                if c:
                    leave_w_in(c - 1)
                if c == 3:
                    act.wait_ge(lin_free[0], 1)
                    act.wait_ge(lin_free[1], 1)
                    square(LATENT, 0, 3)
                if c == 4:
                    root(LATENT)
                if c == 5:
                    round_h(LATENT)
                if c == 7:
                    act.wait_ge(f_in, 1)
                    act.wait_ge(band_out, 16)
                    link(nc.scalar.activation(gate_tmp[:, S:2 * S], gate_tmp[:, 0:S], ACT.Abs))
                    link(nc.scalar.activation(gate_tmp[:, 2 * S:3 * S], gate_tmp[:, S:2 * S], ACT.Exp, scale=-1.0))
                    nc.scalar.activation(gate_tmp[:, 3 * S:4 * S], gate_tmp[:, 2 * S:3 * S], ACT.Ln, bias=ones[0:4, 0:1])\
                        .then_inc(f_ln, 1)
            leave_w_in(8)
            hi(PH["w_out"].chunk0)
            u0 = PH["mla"].unit0
            vm = a1["v_m"]
            qscale = (HD + ROPE) ** -0.5
            for u, todo in enumerate([[(a1["qn"], 0, 512, qscale)],
                                      [(a1["qr"], 0, 256, qscale), (a1["kn"][:, 0:256], 256, 512, 1.0)],
                                      [(a1["kn"][:, 256:512], 0, 256, 1.0), (vm[:, 0:256], 256, 512, 1.0)],
                                      [(vm[:, 256:512], 0, 256, 1.0)]]):
                if u == 1:
                    act.wait_ge(f_ready, 1)
                if u < MLA_UNITS - 1:
                    act.wait_ge(mla_units, u + 1)
                else:
                    act.wait_ge(half_done, 2 * (PH["mla"].chunk0 + 1))
                for to, a, b, scale in todo:
                    ins = nc.scalar.activation(to, lin[(u0 + u) % 2][:, a:b], ACT.Copy, scale=scale)
                leave(ins, u0 + u)

            def exp_head(n, base, a, sink):
                hs = head_stats(n)
                s = three_of(a["s"], n)
                act.wait_ge(scores_read, base + n + 1)
                if sink is not None:
                    nc.scalar.activation(hs[:, 6:8], hs[:, 2:4], ACT.Exp, bias=sink)
                nc.scalar.activation(s[:, 0:P], s[:, 0:P], ACT.Exp, bias=hs[:, 2:3], accum_out=hs[:, 4:5])
                nc.scalar.activation(s[:, P:384], s[:, P:384], ACT.Exp, bias=hs[:, 3:4], accum_out=hs[:, 5:6])\
                    .then_inc(exps, 1)

            def copy_head(n, base, a):
                act.wait_ge(trans, base + n + 1)
                if n >= 2:
                    act.wait_ge(pv, base + n - 1)
                nc.scalar.activation(two(a["pT"], n), tra[n % 2][:, 0:384], ACT.Copy).then_inc(trans_out, 1)

            for n in range(HEADS1):
                exp_head(n, 0, a1, heads1[n]["sink"])
                if n:
                    copy_head(n - 1, 0, a1)
                if n in (11, 13, 15):
                    k, many = {11: (0, 4), 13: (4, 1), 15: (5, 1)}[n]
                    act.wait_ge(att_out, k + many)
                    square(GROUP, k, many)
            copy_head(HEADS1 - 1, 0, a1)
            for k in (6, 7):
                act.wait_ge(att_out, k + 1)
                square(GROUP, k)
            root(GROUP)
            round_h(GROUP)

            def copy_units(ph, norm):
                per = ph.per_unit

                def leave_unit(step):
                    u = (step.j + 1) // per - 1
                    act.wait_ge(half_done, step.n(lambda c: 2 * (ph.chunk0 + c + 1)))
                    w = 512 // per
                    cut = bass.ds(step.n(lambda c: ((c + 1) // per - 1) * w), w)
                    bank = lin[(ph.unit0 + u) % 2][:, 0:w]
                    nc.scalar.activation(NORM[norm][1][:, cut], bank, ACT.Square).then_inc(sq_ready, w // S)
                    leave(nc.scalar.activation(e0["y"][:, cut], bank, ACT.Copy), ph.unit0 + u)
                return leave_unit

            ph = PH["w_out"]
            out_unit = copy_units(ph, POST)
            for c in range(ph.n):
                hi(ph.chunk0 + c + 1)
                if c:
                    out_unit(Step(c - 1))
            out_unit(Step(ph.n - 1))
            root(POST)
            square_residual(FFNPRE, POST)
            root(FFNPRE)
            round_h(FFNPRE)

            ph = PH["up"]
            cw, cb = COLS["conv_w"][0], COLS["conv_b"][0]

            def at_col(v):
                return cols[:, bass.ds(v, 1)]

            def conv_start(step):
                j = step.j - 1
                act.wait_ge(half_done, step.n(lambda c: 2 * (ph.chunk0 + c)))
                if j >= 2:
                    act.wait_ge(hid_ready, step.n(lambda c: c - 2))
                for s in range(2):
                    ins = nc.scalar.activation(
                        ff["u"][:, 512 * (j % 2) + S * s:512 * (j % 2) + S * s + S],
                        lin[(ph.unit0 + j) % 2][:, S * s:S * s + S], ACT.Identity,
                        scale=at_col(step.n(lambda c: cw + 88 + 2 * (c - 1) + s)),
                        bias=at_col(step.n(lambda c: cb + 2 * (c - 1) + s)))
                ins.then_inc(conv_in, 1)

            def gelu(step):
                j = step.j - 2
                act.wait_ge(lin_free[(ph.unit0 + j) % 2], step.n(lambda c: (ph.unit0 + c - 2) // 2 + 1))
                nc.scalar.activation(ff["g"][:, S * (j % 2):S * (j % 2) + S],
                                     ff["u"][:, 512 * (j % 2):512 * (j % 2) + S], ACT.Gelu_apprx_tanh)\
                    .then_inc(gelu_ready, 1)

            def round_hid(step, lag, unit0=None):
                j = step.j - lag
                if unit0 is None:
                    act.wait_ge(hid_ready, step.n(lambda c: c - lag + 1))
                else:
                    act.wait_ge(lin_free[(unit0 + j) % 2], step.n(lambda c: (unit0 + c - lag) // 2 + 1))
                nc.scalar.activation(hid_hi[:, bass.ds(step.n(lambda c: (c - lag) * S), S)],
                                     ff["hid"][:, S * (j % 2):S * (j % 2) + S], ACT.Copy).then_inc(hid_hh, 1)

            def up_step(step):
                c = step.j
                if c < ph.n:
                    hi(ph.chunk0 + c + 1, step if step.i is not None else None, ph)
                if c >= 2:
                    gelu(step)
                if 1 <= c <= ph.n:
                    conv_start(step)
                if c >= 2:
                    round_hid(step, 2)

            steps(act, ph.n, 2, 1, up_step)
            up_step(Step(ph.n))
            hi(PH["down"].chunk0 + 1)
            up_step(Step(ph.n + 1))

            ph = PH["down"]
            out_unit = copy_units(ph, FFNPOST)

            def down_step(step):
                if step.j or step.i is not None:
                    hi(ph.chunk0 + step.j + 1, step if step.i is not None else None, ph)
                if step.j >= 2 and step.j % 2 == 0:
                    out_unit(Step(step.j - 1, step.i))

            steps(act, ph.n, 4, 1, down_step)
            out_unit(Step(ph.n - 1))
            root(FFNPOST)

            square_residual(L0, FFNPOST)
            root(L0)
            round_h(L0)
            ph = PH["qkv"]

            def qkv_unit(c):
                act.wait_ge(half_done, 2 * (ph.chunk0 + c + 1))
                bank = lin[(ph.unit0 + c) % 2]
                if c == 0:
                    act.wait_ge(h_tiles, tiles_before(L0F))
                if c < 8:
                    to = a2["qk"[c % 4 // 2]][:, (2 * (c // 4) + c % 2) * 512:(2 * (c // 4) + c % 2 + 1) * 512]
                    ins = nc.scalar.activation(to, bank[:, :], ACT.Copy, scale=HD ** -0.5 if c % 4 < 2 else 1.0)
                else:
                    to = v2[:, :, (c - 8) * S:(c - 7) * S]
                    ins = nc.scalar.activation(to, v3(bank[:, :], 2), ACT.Copy)
                leave(ins, ph.unit0 + c)

            def stick_exp(n):
                act.wait_ge(z_neg, n + 1)
                nc.scalar.activation(of_head(a2["e"], n), of_head(a2["e"], n), ACT.Exp).then_inc(z_exp, 1)

            def stick_ln(n):
                act.wait_ge(z_exp, n + 1)
                nc.scalar.activation(of_head(a2["e"], n), of_head(a2["e"], n), ACT.Ln, bias=ones[:, 0:1]).then_inc(z_ln, 1)

            def stick_weights(n):
                act.wait_ge(z_sticks, n + 1)
                nc.scalar.activation(of_head(a2["z"], n), of_head(a2["z"], n), ACT.Exp).then_inc(stick, 1)

            for c in range(ph.n):
                hi(ph.chunk0 + c + 1)
                if c:
                    qkv_unit(c - 1)
                for stage, heads in ((stick_exp, ACT_EXP), (stick_ln, ACT_LN), (stick_weights, ACT_WEIGHTS)):
                    for n in heads.get(c, ()):
                        stage(n)
            qkv_unit(ph.n - 1)
            for n in B1:
                stick_weights(n)

            def round_pair(j, pair):
                act.wait_ge(pv, HEADS1 + 2 * j + 2)
                nc.scalar.activation(h_hi[:, j * S:(j + 1) * S], att[pair % 2][:, 0:S], ACT.Copy).then_inc(o_hi, 1)

            def square_unit(ph, norm, unit, step=Step(0)):
                at = (lambda f: f(unit)) if step.i is None else (lambda f: step.n(lambda c: f(c // 2 - 2)))
                act.wait_ge(lin_free[(ph.unit0 + unit) % 2], at(lambda u: (ph.unit0 + u) // 2 + 1))
                w = DT // ph.units * S
                cut = bass.ds(at(lambda u: u * w), w)
                nc.scalar.activation(NORM[norm][1][:, cut], x[:, cut], ACT.Square).then_inc(sq_ready, w // S)

            round_pair(0, PAIRS1)
            round_pair(1, PAIRS1 + 1)
            base = HEADS1
            for n in range(HEADS2):
                exp_head(n, base, a2, None)
                if n == 0:
                    round_pair(2, PAIRS1 + 2)
                    round_pair(3, PAIRS1 + 3)
                if n:
                    act.wait_ge(trans, base + n)
                    act.wait_ge(pv, HEADS1 + SB_HEADS + max(n - 2, 0))
                    nc.scalar.activation(two(a2["pT"], n - 1), tra[(n - 1) % 2][:, 0:384], ACT.Copy).then_inc(trans_out, 1)
                if n >= 3 and n % 2:
                    j = PAIRS_SB + (n - 3) // 2
                    round_pair(j, PAIRS1 + j)
            n = HEADS2
            act.wait_ge(trans, base + n)
            act.wait_ge(pv, HEADS1 + SB_HEADS + n - 2)
            nc.scalar.activation(two(a2["pT"], n - 1), tra[(n - 1) % 2][:, 0:384], ACT.Copy).then_inc(trans_out, 1)
            round_pair(7, PAIRS1 + 7)

            ph = PH["att_o"]
            for c in range(ph.n):
                hi(ph.chunk0 + c + 1)
                if c >= 2:
                    square_unit(ph, L0F, c - 2)
            square_unit(ph, L0F, 2)
            square_unit(ph, L0F, 3)

            def swiglu(ph):
                def silu(step):
                    j = step.j - 1
                    act.wait_ge(half_done, step.n(lambda c: 2 * (ph.chunk0 + c)))
                    nc.scalar.activation(ff["g"][:, S * (j % 2):S * (j % 2) + S], lin[(ph.unit0 + j) % 2][:, 0:S], ACT.Silu)\
                        .then_inc(gelu_ready, 1)

                def step_(step):
                    hi(ph.chunk0 + step.j + 1, step if step.i is not None else None, ph)
                    if step.j >= 1:
                        silu(step)
                        round_hid(step, 1, ph.unit0)

                steps(act, ph.n, 2, 1, step_)
                silu(Step(ph.n))
                round_hid(Step(ph.n), 1, ph.unit0)

            def down(ph, norm):
                def one(step):
                    hi(ph.chunk0 + step.j + 1, step if step.i is not None else None, ph)
                    if step.j >= 4 and step.j % 2 == 0:
                        square_unit(ph, norm, step.j // 2 - 2, step)

                steps(act, ph.n, 4, 1, one)
                square_unit(ph, norm, DT - 2)
                square_unit(ph, norm, DT - 1)

            root(L0F)
            round_h(L0F)
            swiglu(PH["gu0"])
            down(PH["dn0"], L1)

            root(L1)
            round_h(L1)
            ph = PH["ret_in"]

            def ret_unit(c):
                bank = lin[(ph.unit0 + c) % 2]
                act.wait_ge(half_done, 2 * (ph.chunk0 + c + 1))
                if c < 16:
                    j = c - 8
                    for r in range(2):
                        ins = nc.scalar.activation(v3(rt["v"], 2)[:, r, j * S:(j + 1) * S], bank[:, r * S:(r + 1) * S], ACT.Copy,
                                                   accum_out=v_sums[:, 4 * (j // 2) + 2 * r + j % 2:4 * (j // 2) + 2 * r + j % 2 + 1])
                else:
                    j = c - 16
                    if j >= 4:
                        act.wait_ge(ret_y, 2 * (j // 2 - 1))
                    ins = nc.scalar.activation(rt["g"][:, j % 4 * 512:(j % 4 + 1) * 512], bank[:, :], ACT.Silu)
                leave(ins, ph.unit0 + c)

            def ret_squares(h):
                for m in range(2):
                    act.wait_ge(ret_o, 2 * h + m + 1)
                    if h:
                        act.wait_ge(ret_ssum, h)
                    nc.scalar.activation(rt["sq"][:, 512 * m:512 * m + 512], ret_bank(h)[m][:, :], ACT.Square).then_inc(ret_sq, 1)

            def ret_round(h):
                for m in range(2):
                    act.wait_ge(ret_y, 2 * h + m + 1)
                    t = (4 * h + 2 * m) * S
                    y = rt["t"][:, D * (h % 2) + 512 * m:D * (h % 2) + 512 * m + 512]
                    nc.scalar.activation(hid_hi[:, t:t + 512], y, ACT.Copy).then_inc(ret_hh, 1)

            for c in range(ph.n + 1):
                if c < ph.n:
                    hi(ph.chunk0 + c + 1)
                if c > 8:
                    ret_unit(c - 1)
                if at_squares(c) is not None:
                    ret_squares(at_squares(c))
                if at_rstd(c) is not None:
                    h = at_rstd(c)
                    st = ret_stat[:, 32 * (h % 2):32 * (h % 2) + 32]
                    act.wait_ge(ret_ms, h + 1)
                    nc.scalar.activation(st[:, 6:8], st[:, 0:2], ACT.Sqrt).then_inc(ret_root, 1)
                if c in AT_Y:
                    ret_round(AT_Y[c])

            ph = PH["ret_o"]
            for c in range(ph.n):
                hi(ph.chunk0 + c + 1)
                if c >= 2:
                    square_unit(ph, L1F, c - 2)
            square_unit(ph, L1F, ph.n - 2)
            square_unit(ph, L1F, ph.n - 1)
            root(L1F)
            round_h(L1F)
            swiglu(PH["gu1"])
            down(PH["dn1"], FINAL)
            root(FINAL)

        @block.tensor
        def _(pe):
            def three(out, w, hc, lc, start, stop):
                nc.tensor.matmul(out, w[0], hc, start=start, stop=False, skip_group_check=True)
                nc.tensor.matmul(out, w[0], lc, start=False, stop=False, skip_group_check=True)
                return nc.tensor.matmul(out, w[1], hc, start=False, stop=stop, skip_group_check=True)

            def weights(chunk, step, ph):
                pe.wait_ge(split_ready, step.n(lambda c: 2 * (ph.chunk0 + c) + 1))
                s = chunk % SPLIT_SLOTS
                return w_hi[s], w_lo[s]

            def second_half(ph, step):
                pe.wait_ge(split_ready, step.n(lambda c: 2 * (ph.chunk0 + c) + 2))

            def by_feature(ph, step, first_tiles=None, rhs=None, k0=lambda c: 0, midway=None):
                j = step.j
                f = lambda c: (c + ph.per_unit) // ph.per_unit - 1
                whi, wlo = weights(ph.chunk0 + j, step, ph)
                if j % ph.per_unit == 0:
                    unit_free(pe, ph, step, f)
                bank = lin[(ph.unit0 + f(j)) % 2]
                r_hi, r_lo = rhs or (h_hi, h_lo)
                blocks = ph.nb * ph.kt
                cut2 = ph.halves(j)[1][0] // P
                order = [(b, k) for b in range(ph.nb) for k in range(ph.kt)]
                if first_tiles is not None:
                    order.sort(key=lambda o: o[1])
                half_at = 0
                for n, (b, k) in enumerate(order):
                    if midway and n == blocks // 2:
                        midway()
                    at = b * ph.kt + k
                    if at >= cut2 and half_at == 0:
                        half_at = 1
                        second_half(ph, step)
                    if first_tiles is not None and b == 0:
                        pe.wait_ge(first_tiles[0], first_tiles[1] + k + 1)
                    cut = slice(at * P, at * P + P)
                    t = slice((k0(j) + k) * S, (k0(j) + k + 1) * S)
                    first = n == 0 if first_tiles is not None else k == 0
                    ins = three(bank[:, b * S:(b + 1) * S], (whi[:, cut], wlo[:, cut]), r_hi[:, t], r_lo[:, t],
                                start=first and j % ph.per_unit == 0,
                                stop=(k == ph.kt - 1 and j % ph.per_unit == ph.per_unit - 1))
                    if at in (cut2 - 1, blocks - 1):
                        ins.then_inc(half_done, 1)

            def by_row(ph, step, nb=2, midway=None):
                j = step.j
                whi, wlo = weights(ph.chunk0 + j, step, ph)
                unit_free(pe, ph, step, lambda c: c)
                bank = lin[(ph.unit0 + j) % 2]
                width = nb * P
                for r in range(2):
                    if midway and r:
                        midway()
                    for k in range(ph.kt):
                        if r == 0 and k == ph.kt // 2:
                            second_half(ph, step)
                        w = slice(k * width, (k + 1) * width)
                        t = slice(k * S + r * P, k * S + r * P + P)
                        out = bank[:, r * S:r * S + width]
                        nc.tensor.matmul(out, h_hi[:, t], whi[:, w], start=k == 0, stop=False, skip_group_check=True)
                        nc.tensor.matmul(out, h_hi[:, t], wlo[:, w], start=False, stop=False, skip_group_check=True)
                        ins = nc.tensor.matmul(out, h_lo[:, t], whi[:, w], start=False, stop=k == ph.kt - 1,
                                               skip_group_check=True)
                        if r == 1 and k in (ph.kt // 2 - 1, ph.kt - 1):
                            ins.then_inc(half_done, 1)

            def keep_busy(n, bank=tra[1]):
                for _ in range(n):
                    nc.tensor.matmul(bank[:, 0:S], busy[:, 0:P], busy[:, :], start=True, stop=True)

            def sums(i, wait=0):
                sq, k0, added = NORM[i][1], 0, gathered_before(i)
                keep_busy(wait)
                for g, n in enumerate(NORM_GROUPS[i]):
                    gathered = additions(i, n)
                    added += gathered
                    for k in [k0] + list(range(k0 + 1 + gathered, k0 + n)):
                        pe.wait_ge(sq_ready, scaled_before(i) + k + 1)
                        if gathered and k == k0:
                            pe.wait_ge(sq_added, added)
                        for r in range(2):
                            ins = nc.tensor.matmul(ssum[:, 2 * g + r:2 * g + r + 1], sq[:, k * S + r * P:k * S + r * P + P], ones[:, 0:1],
                                                   start=k == 0 and r == 0, stop=k == norm_tiles(i) - 1 and r == 1,
                                                   skip_group_check=True)
                    k0 += n
                ins.then_inc(ssum_ready, 1)

            def spread(i):
                for g in range(len(NORM_GROUPS[i])):
                    for r in range(2):
                        pe.wait_ge(diag_ready, 2 * (groups_before(i) + g) + r + 1)
                        at = slice((2 * g + r) * P, (2 * g + r + 1) * P)
                        ins = nc.tensor.matmul(rbc[g][:, r * P:(r + 1) * P], ones[:, 0:P], diag[:, at], start=True, stop=True)
                ins.then_inc(rbc_ready, 1)

            def norm(i, wait=8, chain=16, tiles=8):
                sums(i, wait)
                keep_busy(chain)
                spread(i)
                keep_busy(tiles)

            def rotate(n, perm, src, width=S):
                return nc.tensor.matmul(tra[n % 2][:, 0:width], perm, src, start=True, stop=True)

            pe.wait_ge(busy_ready, 1)
            keep_busy(16)
            pe.wait_ge(cols_in, 16)
            pe.wait_ge(onehot_in, 16)
            nc.tensor.matmul(tra[0][0:8, 0:BAND], col("rel", 0, 8, BUCKETS + 1), onehot, start=True, stop=True).then_inc(band_ps, 1)
            pe.wait_ge(ones_filled, 1)
            norm(PRE, 0, 8, 4)
            ph = PH["w_in"]
            for c in range(ph.n):
                if c < 7:
                    by_feature(ph, Step(c), (h_tiles, 0) if c == 0 else None)
                else:
                    by_row(ph, Step(c), 2 if c == 7 else 1)
                if c == 3:
                    sums(LATENT)
                if c == 4:
                    spread(LATENT)
                    pe.wait_ge(band_ready, 1)
                    pe.wait_ge(tab1_in, 16)
                    units_done(pe, 2)
                    rotate(0, a1["perm"], a1["kr"]).then_inc(rot_ready, 1)

            def score_head(n, base, head):
                out = sco[n % 2]
                if n >= 2:
                    pe.wait_ge(scores_read, base + n - 1)
                if "needs" in head:
                    pe.wait_ge(*head["needs"])
                first, todo = True, []
                for q, k in head["parts"]:
                    todo.append((out[:, 0:P], q[:, 0:P], k[:, 0:P]))
                    todo.append((out[:, P:384], q[:, P:S], k))
                if head["decay"] is not None:
                    pick = ident[0:4, head["decay"]:head["decay"] + 1]
                    f, fneg = a1["f"][0:4, :], a1["fneg"][0:4, :]
                    for o, q, k in ((out[:, 0:P], slice(0, P), slice(0, P)), (out[:, P:384], slice(P, S), slice(0, S))):
                        n_k = k.stop - k.start
                        todo.append((o, f[:, q], pick.to_broadcast([4, n_k])))
                        todo.append((o, pick.to_broadcast([4, P]), fneg[:, k]))
                for m, (o, q, k) in enumerate(todo):
                    ins = nc.tensor.matmul(o, q, k, start=first, stop=m == len(todo) - 1, skip_group_check=True)
                    first = False
                ins.then_inc(scores, 1)

            def turn_head(n, base, a):
                s = three_of(a["s"], n)
                pe.wait_ge(probs, base + n + 1)
                if n >= 2:
                    pe.wait_ge(trans_out, base + n - 1)
                for m in range(3):
                    ins = nc.tensor.transpose(tra[n % 2][:, m * P:(m + 1) * P], s[:, m * P:(m + 1) * P], ident[:, :])
                ins.then_inc(trans, 1)

            def values(n, pT, v, pair):
                h = n % 2
                if pair >= 2 and h == 0:
                    if pair - 2 < PAIRS1:
                        pe.wait_ge(att_out, pair - 1)
                    else:
                        pe.wait_ge(o_tiles, pair - 1 - PAIRS1)
                o = att[pair % 2][HD * h:HD * h + HD, 0:S]
                nc.tensor.matmul(o, v(0), pT[:, 0:S], start=True, stop=False, skip_group_check=True)
                nc.tensor.matmul(o[:, P:S], v(1), pT[:, S:384], start=False, stop=True, skip_group_check=True)\
                    .then_inc(pv, 1)

            def softmax_heads(heads, base, a, pair0, scored=0):
                for n in range(scored, 2):
                    score_head(n, base, heads[n])
                for n in range(len(heads) + 1):
                    if n + 2 < len(heads):
                        score_head(n + 2, base, heads[n + 2])
                    if n < len(heads):
                        keep_busy(FILL if a is a1 else 0, lin[1])
                        turn_head(n, base, a)
                    if n:
                        keep_busy(FILL if a is a1 else 0, lin[1])
                        pe.wait_ge(trans_out, base + n)
                        values(n - 1, two(a["pT"], n - 1), heads[n - 1]["v"], pair0 + (n - 1) // 2)

            ph = PH["mla"]
            whi, wlo = weights(ph.chunk0, Step(0), ph)
            pe.wait_ge(h_tiles, tiles_before(GROUP))
            units_done(pe, ph.unit0)
            score_head(0, 0, heads1[0])
            score_head(1, 0, heads1[1])
            up, wide = 2 * 384, 384

            def latent(unit, at, out_cols, w0, tiles, width):
                for n, k in enumerate(tiles):
                    w = slice(w0 + n * width, w0 + n * width + P)
                    t = slice(k * S, (k + 1) * S)
                    ins = three(lin[(ph.unit0 + unit) % 2][:, at * S:(at + 1) * S], (whi[:, w], wlo[:, w]),
                                hid_hi[:, t], hid_lo[:, t], n == 0, n == len(tiles) - 1)
                return ins

            def latent_v(unit, at, r):
                t = slice(2 * S + r * P, 2 * S + r * P + P)
                w = slice(up + 2 * P, up + 4 * P)
                out = lin[(ph.unit0 + unit) % 2][:, at * S:(at + 1) * S]
                nc.tensor.matmul(out, hid_hi[:, t], whi[:, w], start=True, stop=False, skip_group_check=True)
                nc.tensor.matmul(out, hid_hi[:, t], wlo[:, w], start=False, stop=False, skip_group_check=True)
                return nc.tensor.matmul(out, hid_lo[:, t], whi[:, w], start=False, stop=True, skip_group_check=True)

            for u in range(MLA_UNITS):
                unit_free(pe, ph, Step(u), lambda c: c)
                if u == 0:
                    latent(u, 0, None, 0, (0, 1), wide)
                    ins = latent(u, 1, None, P, (0, 1), wide)
                elif u == 1:
                    latent(u, 0, None, 2 * P, (0, 1), wide).then_inc(half_done, 1)
                    second_half(ph, Step(0))
                    ins = latent(u, 1, None, up, (2,), P)
                elif u == 2:
                    latent(u, 0, None, up + P, (2,), P)
                    ins = latent_v(u, 1, 0)
                else:
                    ins = latent_v(u, 0, 1)
                ins.then_inc(mla_units if u < MLA_UNITS - 1 else half_done, 1)
            units_done(pe, ph.unit0 + 2)
            rotate(1, a1["perm"], a1["qr"]).then_inc(rot_ready, 1)

            units_done(pe, ph.unit0 + ph.units)
            softmax_heads(heads1, 0, a1, 0, 2)

            pe.wait_ge(scores_read, HEADS1)
            norm(GROUP)
            ph = PH["w_out"]
            for c in range(ph.n):
                by_feature(ph, Step(c), (h_tiles, tiles_before(GROUP)) if c == 0 else None)
            norm(POST)
            norm(FFNPRE, 50)

            def up_phase(name, i):
                ph = PH[name]
                by_feature(ph, Step(0), (h_tiles, tiles_before(i)))
                steps(pe, ph.n, 1, 1, lambda s: by_feature(ph, s) if s.i is not None or s.j else None)

            def down_phase(name, base):
                ph = PH[name]

                def one(step):
                    if step.i is None and step.j < 2:
                        pe.wait_ge(hid_tiles, base + HALF * (step.j + 1))
                    by_feature(ph, step, rhs=(hid_hi, hid_lo), k0=lambda c: HALF * (c % 2))

                steps(pe, ph.n, 4, 0, one)

            up_phase("up", FFNPRE)
            down_phase("down", 0)
            norm(FFNPOST)
            norm(L0, 50)
            ph = PH["qkv"]
            pe.wait_ge(tab2_in, 16)

            def stick_scores(n):
                units_done(pe, ph.unit0 + 4)
                if n >= STICK:
                    pe.wait_ge(z_masked, n - STICK + 1)
                out, q, k = stick_bank(n), half(a2["q"], n // 2, n % 2), half(a2["k"], n // 2, n % 2)
                nc.tensor.matmul(out[:, 0:S], k[:, 0:P], q, start=True, stop=False, skip_group_check=True)
                nc.tensor.matmul(out[:, S:384], k[:, P:S], q[:, P:S], start=False, stop=True, skip_group_check=True)\
                    .then_inc(z_ready, 1)

            def stick_sums(n):
                out, lm = stick_bank(n), of_head(a2["e"], n)
                pe.wait_ge(lm_ready, n + 1)
                pe.wait_ge(z_masked, SB_HEADS)
                if n >= STICK:
                    pe.wait_ge(z_sticks, n - STICK + 1)
                nc.tensor.matmul(out[:, 0:S], a2["tri"], lm[:, 0:S], start=True, stop=False, skip_group_check=True)
                nc.tensor.matmul(out[:, S:384], a2["tri"], lm[:, S:384], start=False, stop=False, skip_group_check=True)
                nc.tensor.matmul(out[:, P:S], a2["negones"], lm[:, S:384], start=False, stop=True, skip_group_check=True)\
                    .then_inc(z_sum, 1)

            def rotate_heads(r):
                units_done(pe, ph.unit0 + 4 + r + 1)
                if r >= 2:
                    pe.wait_ge(rot_done, 2 + r - 1)
                nc.tensor.matmul(att[r % 2][:, :], a2["perm"], rotated(r), start=True, stop=True).then_inc(rot_ready, 1)

            def stick_values(n):
                pe.wait_ge(stick, n + 1)
                values(n, of_head(a2["z"], n), lambda kt, n=n: v2[:, kt, HD * n:HD * n + HD], PAIRS1 + n // 2)

            for c in range(ph.n):
                if ph.row(c):
                    by_row(ph, Step(c))
                else:
                    by_feature(ph, Step(c), (h_tiles, tiles_before(L0)) if c == 0 else None)
                for stage, which in ((stick_scores, PE_Z), (rotate_heads, PE_ROTATE), (stick_sums, PE_SUMS)):
                    for n in which.get(c, ()):
                        stage(n)
            pe.wait_ge(rot_done, 6)
            units_done(pe, ph.unit0 + ph.units)
            for n in B0:
                stick_values(n)
            pe.wait_ge(z_sticks, SB_HEADS)
            score_head(0, HEADS1, heads2[0])
            score_head(1, HEADS1, heads2[1])
            for n in B1:
                stick_values(n)
            softmax_heads(heads2, HEADS1, a2, PAIRS1 + PAIRS_SB, 2)

            ph = PH["att_o"]
            for c in range(ph.n):
                by_feature(ph, Step(c), (o_tiles, 0) if c == 0 else None)
            pe.wait_ge(scores_read, HEADS1 + HEADS2)
            norm(L0F)
            up_phase("gu0", L0F)
            down_phase("dn0", FT)

            norm(L1)
            ph = PH["ret_in"]
            rv = v3(rt["v"], 2)

            def ret_scores(h):
                out = sco[h % 2]
                pe.wait_ge(ret_rot, 4 + h + 1)
                if h >= 2:
                    pe.wait_ge(ret_inner, h - 1)
                for kt, (a, b) in enumerate(((0, S), (S, 384))):
                    for d in range(2):
                        t = (2 * h + d) * S
                        ins = nc.tensor.matmul(out[:, a:b], rt["k"][:, t + kt * P:t + kt * P + P], rt["q"][:, t + kt * P:t + S],
                                               start=kt == 0 and d == 0, stop=kt == 1 and d == 1, skip_group_check=True)
                ins.then_inc(ret_s, 1)

            def ret_values(h):
                inner = rt["inner"][:, h * 384:(h + 1) * 384]
                pe.wait_ge(ret_inner, h + 1)
                pe.wait_ge(v_centred, h + 1)
                if h >= 2:
                    pe.wait_ge(ret_t, h - 1)
                for f in range(4):
                    o = ret_bank(h)[f // 2][:, f % 2 * S:f % 2 * S + S]
                    v = slice(h * RET_DV + f * P, h * RET_DV + f * P + P)
                    nc.tensor.matmul(o, rv[:, 0, v], inner[:, 0:S], start=f % 2 == 0, stop=False, skip_group_check=True)
                    ins = nc.tensor.matmul(o[:, P:S], rv[:, 1, v], inner[:, S:384], start=False, stop=f % 2 == 1, skip_group_check=True)
                    if f % 2:
                        ins.then_inc(ret_o, 1)

            def ret_sums(h):
                pe.wait_ge(ret_inner, RET_H)
                pe.wait_ge(ret_added, h + 1)
                for f in range(2):
                    for r in range(2):
                        ins = nc.tensor.matmul(ssum[:, r:r + 1], rt["sq"][:, f * S + r * P:f * S + r * P + P], ones[:, 0:1],
                                               start=f == 0 and r == 0, stop=f == 1 and r == 1, skip_group_check=True)
                ins.then_inc(ret_ssum, 1)

            def ret_spread(h):
                if h:
                    pe.wait_ge(ret_t, h)
                for r in range(2):
                    pe.wait_ge(ret_diag, 2 * h + r + 1)
                    ins = nc.tensor.matmul(ret_rbc_of(h)[:, r * P:(r + 1) * P], ones[:, 0:P], diag[:, r * P:(r + 1) * P],
                                           start=True, stop=True)
                ins.then_inc(ret_rbc, 1)

            for c in range(ph.n):
                sums_of = (lambda h=at_sums(c): ret_sums(h)) if at_sums(c) is not None else None
                if ph.row(c):
                    by_row(ph, Step(c), midway=sums_of)
                else:
                    by_feature(ph, Step(c), (h_tiles, tiles_before(L1)) if c == 0 else None, midway=sums_of)
                if c in AT_SCORES:
                    ret_scores(AT_SCORES[c])
                if at_spread(c) is not None:
                    ret_spread(at_spread(c))
                if at_values(c) is not None:
                    ret_values(at_values(c))

            ph = PH["ret_o"]
            for c in range(ph.n):
                by_feature(ph, Step(c), (ret_tiles, 0) if c == 0 else None, rhs=(hid_hi, hid_lo))
            norm(L1F)
            up_phase("gu1", L1F)
            down_phase("dn1", 2 * FT)
            norm(FINAL)

        @block.vector
        def _(dve):
            chain = [0]

            def link(ins):
                chain[0] += 1
                ins.then_inc(dve_chain, 1)
                dve.wait_ge(dve_chain, chain[0])

            tt, stt, ts = nc.vector.tensor_tensor, nc.vector.scalar_tensor_tensor, nc.vector.tensor_scalar

            def lo(chunk, step=None, ph=None):
                if chunk >= CHUNKS or chunk in SPLIT_AHEAD.values():
                    return
                if chunk - 1 in SPLIT_AHEAD.values():
                    dve.wait_ge(split_ready, 2 * chunk)
                of, c = phase_of(chunk)
                at = (lambda f: f(chunk)) if step is None else (lambda f: step.n(lambda c: f(ph.chunk0 + c + 1)))
                s = chunk % SPLIT_SLOTS
                for half, (a, b) in enumerate(of.halves(c)):
                    dve.wait_ge(hi_ready, at(lambda k: 2 * k + half + 1))
                    tt(w_lo[s][:, a:b], raw[chunk % RAW_SLOTS][:, a:b], w_hi[s][:, a:b].bitcast(F32), ALU.subtract)\
                        .then_inc(split_ready, 1)

            def rstd(i):
                sizes = NORM_GROUPS[i]
                n = 2 * len(sizes)
                dve.wait_ge(ssum_ready, i + 1)
                for g, nt in enumerate(sizes):
                    ins = ts(stat[:, 2 * g:2 * g + 2], ssum[:, 2 * g:2 * g + 2], 1.0 / (nt * P), EPS, ALU.mult, ALU.add)
                ins.then_inc(ms_ready, 1)
                refine(root_ready, i + 1, stat, n)
                if i:
                    dve.wait_ge(rbc_ready, i)
                for c in range(n):
                    ts(diag[:, c * P:(c + 1) * P], ident[:, :], stat[:, 24 + c:25 + c], -0.5, ALU.mult, ALU.mult).then_inc(diag_ready, 1)

            def refine(ready, count, st, n):
                m, r, a = st[:, 0:n], st[:, 12:12 + n], st[:, 18:18 + n]
                dve.wait_ge(ready, count)
                link(nc.vector.reciprocal(r, st[:, 6:6 + n]))
                link(tt(a, r, m, ALU.mult))
                link(tt(a, a, r, ALU.mult))
                link(stt(st[:, 24:24 + n], a, -3.0, r, ALU.add, ALU.mult))

            def scale_tile(i, k):
                src, _, tmp, gain_ = NORM[i][:4]
                cut = slice(k * S, (k + 1) * S)
                return stt(tmp[:, cut], src[:, cut], gain_(k), rbc[group_of(i, k)], ALU.mult, ALU.mult)

            def scale_tiles(i, then):
                dve.wait_ge(rbc_ready, i + 1)
                n = norm_tiles(i)
                for k in range(n + 1):
                    if k < n:
                        scale_tile(i, k).then_inc(t_ready, 1)
                    if k:
                        then(k - 1)

            def norm_h(i):
                _, _, tmp, _, shift, hi_, lo_ = NORM[i]

                def rest_of(k):
                    cut = slice(k * S, (k + 1) * S)
                    dve.wait_ge(hh_ready, tiles_before(i) + k + 1)
                    if shift(k) is None:
                        ins = tt(lo_[:, cut], tmp[:, cut], hi_[:, cut].bitcast(F32), ALU.subtract)
                    else:
                        ins = stt(lo_[:, cut], tmp[:, cut], shift(k), hi_[:, cut].bitcast(F32), ALU.add, ALU.subtract)
                    ins.then_inc(h_tiles, 1)

                rstd(i)
                scale_tiles(i, rest_of)

            def norm_residual(i):
                def add(k):
                    cut = slice(k * S, (k + 1) * S)
                    dve.wait_ge(t_ready, scaled_before(i) + k + 1)
                    tt(x[:, cut], x[:, cut], e0["y"][:, cut], ALU.add).then_inc(x_tiles, 1)

                rstd(i)
                scale_tiles(i, add)

            def piece(step, f):
                slot = f(step.j) % 2
                sums, o = ada_sums[:, 2 * slot:2 * slot + 2], COLS["ada_b"][0]
                dve.wait_ge(ada_in[slot], step.n(lambda c: 16 * (f(c) // 2 + 1)))
                for b in range(2):
                    w = ada_raw[slot][:, b * D:(b + 1) * D]
                    ins = nc.vector.tensor_tensor_reduce(w, w, cond_silu, 1.0, 0.0, ALU.mult, ALU.add, sums[:, b:b + 1])
                ins.then_inc(ada_sum, 1)
                dve.wait_ge(ada_sum, step.n(lambda c: f(c) + 1))
                tt(mod[:, bass.ds(step.n(lambda c: 2 * f(c)), 2)], sums, cols[:, bass.ds(step.n(lambda c: o + 2 * f(c)), 2)],
                   ALU.add).then_inc(ada_out, 1)

            def pieces(name, step):
                for m in range(ada_here(name, step.j)):
                    piece(step, lambda c, m=m: ada_before(name, c) + m)

            nc.vector.memset(ones[:, :], 1.0).then_inc(ones_filled, 1)
            dve.wait_ge(cols_in, 16)
            dve.wait_ge(ident_in, 16)
            dve.wait_ge(x_in[0], 16)
            dve.wait_ge(x_in[1], 16)
            norm_h(PRE)
            dve.wait_ge(cond_ready, 1)
            ph = PH["w_in"]

            def rotary(n, tile, cos, sin, nt):
                dve.wait_ge(rot_ready, n + 1)
                rot = ROT_BANK[n][:, 0:nt * S]
                link(tt(v3(tile, nt), v3(tile, nt), over(cos, nt), ALU.mult))
                tmp = ROT_TMP[n]
                link(tt(v3(tmp, nt), v3(rot, nt), over(sin, nt), ALU.mult))
                tt(tile, tile, tmp, ALU.add).then_inc(rot_done, 1)

            ROT_BANK = tra + att + att
            ROT_TMP = [a1["pT"][:, 2 * S:3 * S]] * 2 + [a2["rot"]] * 4
            for c in range(ph.n):
                lo(ph.chunk0 + c + 1)
                if c == 4:
                    rstd(LATENT)
                if c == 5:
                    _, _, lat_t, _, _, lat_hi, lat_lo = NORM[LATENT]

                    def lat_rest(k):
                        cut = slice(k * S, (k + 1) * S)
                        dve.wait_ge(hh_ready, tiles_before(LATENT) + k + 1)
                        tt(lat_lo[:, cut], lat_t[:, cut], lat_hi[:, cut].bitcast(F32), ALU.subtract).then_inc(h_tiles, 1)

                    scale_tiles(LATENT, lat_rest)
                if c == 6:
                    dve.wait_ge(tab1_in, 16)
                    rotary(0, a1["kr"], a1["cos"], a1["sin"], 1)
                if c == 8:
                    dve.wait_ge(f_ln, 1)
                    link(stt(gate_tmp[:, 4 * S:5 * S], gate_tmp[:, 0:S], 0.0, gate_tmp[:, 3 * S:4 * S], ALU.min, ALU.subtract))
                    link(nc.vector.tensor_tensor_scan(a1["f"][0:4, :], ones[0:4, :], gate_tmp[:, 4 * S:5 * S], 0.0, ALU.mult, ALU.add))
                    ts(a1["fneg"][0:4, :], a1["f"][0:4, :], -1.0, None, ALU.mult).then_inc(f_ready, 1)
                pieces(ph.name, Step(c))
            lo(PH["w_out"].chunk0)

            def score_head(n, base, head, a):
                hs = head_stats(n)
                s, out = three_of(a["s"], n), sco[n % 2]
                dve.wait_ge(scores, base + n + 1)
                if n >= 3:
                    dve.wait_ge(trans, base + n - 2)
                first = NEG * 3 if head["sink"] is None else head["sink"]
                nc.vector.tensor_tensor_reduce(s[:, 0:P], out[:, 0:P], head["bias"][0], 1.0, first, ALU.add, ALU.max, hs[:, 0:1])
                link(nc.vector.tensor_tensor_reduce(s[:, P:384], out[:, P:384], head["bias"][1], 1.0, first, ALU.add, ALU.max,
                                                    hs[:, 1:2]))
                ts(hs[:, 2:4], hs[:, 0:2], -1.0, None, ALU.mult).then_inc(scores_read, 1)

            def weigh_head(n, base, head, a):
                hs = head_stats(n)
                s = three_of(a["s"], n)
                dve.wait_ge(exps, base + n + 1)
                total = hs[:, 4:6]
                if head["sink"] is not None:
                    link(tt(hs[:, 8:10], hs[:, 4:6], hs[:, 6:8], ALU.add))
                    total = hs[:, 8:10]
                link(nc.vector.reciprocal(hs[:, 10:12], total))
                ts(s[:, 0:P], s[:, 0:P], hs[:, 10:11], None, ALU.mult)
                ts(s[:, P:384], s[:, P:384], hs[:, 11:12], None, ALU.mult).then_inc(probs, 1)

            def softmax_heads(heads, base, a, pair_out, after_first=None):
                score_head(0, base, heads[0], a)
                for n in range(len(heads)):
                    if n + 1 < len(heads):
                        score_head(n + 1, base, heads[n + 1], a)
                    weigh_head(n, base, heads[n], a)
                    if n >= 3 and n % 2:
                        pair_out((n - 3) // 2)
                    if n == 0 and after_first:
                        after_first()
                pair_out(len(heads) // 2 - 1)

            def pair_to_mixed(j):
                dve.wait_ge(pv, 2 * j + 2)
                nc.vector.tensor_copy(a1["mixed"][:, j * S:(j + 1) * S], att[j % 2][:, 0:S]).then_inc(att_out, 1)

            dve.wait_ge(bias_in, 16)
            softmax_heads(heads1, 0, a1, pair_to_mixed, lambda: rotary(1, a1["qr"], a1["cos"], a1["sin"], 1))
            norm_h(GROUP)
            ph = PH["w_out"]
            for c in range(ph.n):
                lo(ph.chunk0 + c + 1)
                pieces(ph.name, Step(c))
            units_done(dve, ph.unit0 + ph.units)
            norm_residual(POST)
            norm_h(FFNPRE)

            ph = PH["up"]
            cw = COLS["conv_w"][0]

            def taps(step):
                j = step.j - 1
                bank = lin[(ph.unit0 + j) % 2]
                dve.wait_ge(conv_in, step.n(lambda c: c))
                for back in (1, 2):
                    for s in range(2):
                        u = ff["u"][:, 512 * (j % 2) + S * s:512 * (j % 2) + S * s + S]
                        w = cols[:, bass.ds(step.n(lambda c: cw + 44 * (2 - back) + 2 * (c - 1) + s), 1)]
                        if back == 2:
                            dve.wait_ge(conv_tap, step.n(lambda c: 2 * (c - 1) + s + 1))
                        ins = stt(u[:, back:S], bank[:, S * s:S * s + S - back], w, u[:, back:S], ALU.mult, ALU.add)
                        if back == 1:
                            ins.then_inc(conv_tap, 1)
                ins.then_inc(lin_free[(ph.unit0 + j) % 2], 1)

            def product(step, lag, base, up):
                j = step.j - lag
                dve.wait_ge(gelu_ready, step.n(lambda c: base + c - lag + 1))
                return tt(ff["hid"][:, S * (j % 2):S * (j % 2) + S], up, ff["g"][:, S * (j % 2):S * (j % 2) + S], ALU.mult)

            def rest(step, lag, base):
                j = step.j - lag
                dve.wait_ge(hid_hh, step.n(lambda c: base + c - lag + 1))
                cut = bass.ds(step.n(lambda c: (c - lag) * S), S)
                tt(hid_lo[:, cut], ff["hid"][:, S * (j % 2):S * (j % 2) + S], hid_hi[:, cut].bitcast(F32), ALU.subtract)\
                    .then_inc(hid_tiles, 1)

            def up_step(step):
                c = step.j
                if c < ph.n:
                    lo(ph.chunk0 + c + 1, step if step.i is not None else None, ph)
                if 1 <= c <= ph.n:
                    taps(step)
                if c < ph.n:
                    pieces(ph.name, step)

            steps(dve, ph.n, 2, 1, up_step)
            up_step(Step(ph.n))
            lo(PH["down"].chunk0 + 1)

            ph = PH["down"]

            def down_step(ph, step, out):
                if step.j or step.i is not None or out is not None:
                    lo(ph.chunk0 + step.j + 1, step if step.i is not None else None, ph)
                if out is not None and step.j >= 2 and step.j % 2 == 0:
                    out(Step(step.j - 1, step.i))
                pieces(ph.name, step)

            steps(dve, ph.n, 4, 1, lambda s: down_step(ph, s, None))
            units_done(dve, ph.unit0 + ph.units)
            norm_residual(FFNPOST)

            def gain(i):
                n = (L0, L0F, L1, L1F).index(i)
                layer, which = n // 2, 1 + 3 * (n % 2)
                dve.wait_ge(ada_out, ADA_PIECES * layer + 4 * (which + 1))
                at = 48 * layer + 8 * which
                link(stt(gscale[:, 8 * n:8 * n + 8], mod[:, at:at + 8], 1.0, col("norms2", 8 * n, 8), ALU.add, ALU.mult))

            def residual_units(ph, layer, which):
                w = 2 // ph.per_unit if ph.nb == 2 else 1

                def out(step):
                    u = (step.j + 1) // ph.per_unit - 1
                    dve.wait_ge(half_done, step.n(lambda c: 2 * (ph.chunk0 + c + 1)))
                    for b in range(w):
                        k = lambda c, b=b: ((c + 1) // ph.per_unit - 1) * w + b
                        xk = x[:, bass.ds(step.n(lambda c: k(c) * S), S)]
                        gate = mod[:, bass.ds(step.n(lambda c: 48 * layer + 8 * which + k(c)), 1)]
                        ins = stt(xk, lin[(ph.unit0 + u) % 2][:, b * S:(b + 1) * S], gate, xk, ALU.mult, ALU.add)
                    leave(ins, ph.unit0 + u)
                return out

            gain(L0)
            norm_h(L0)
            ph = PH["qkv"]
            dve.wait_ge(tab2_in, 16)

            def stick_mask(n):
                dve.wait_ge(z_ready, n + 1)
                tt(of_head(a2["z"], n), stick_bank(n), a2["strict"], ALU.add).then_inc(z_masked, 1)

            def stick_negative(n):
                dve.wait_ge(z_masked, n + 1)
                z = of_head(a2["z"], n)
                stt(of_head(a2["e"], n), z, -1.0, z, ALU.mult, ALU.min).then_inc(z_neg, 1)

            def stick_softplus(n):
                dve.wait_ge(z_ln, n + 1)
                e = of_head(a2["e"], n)
                stt(e, of_head(a2["z"], n), 0.0, e, ALU.max, ALU.add).then_inc(lm_ready, 1)

            def stick_rest(n):
                dve.wait_ge(z_sum, n + 1)
                tt(of_head(a2["z"], n), stick_bank(n), of_head(a2["z"], n), ALU.add).then_inc(z_sticks, 1)

            def rotate_heads(r):
                rotary(2 + r, rotated(r), a2["cos"], a2["sin"], 2)

            for c in range(ph.n):
                lo(ph.chunk0 + c + 1)
                for stage, which in ((stick_mask, DVE_MASK), (stick_negative, DVE_MASK), (stick_softplus, DVE_SOFTPLUS),
                                     (rotate_heads, DVE_ROTATE), (stick_rest, DVE_REST)):
                    for n in which.get(c, ()):
                        stage(n)
                pieces(ph.name, Step(c))

            def pair_to_split(j):
                dve.wait_ge(o_hi, j + 1)
                tt(h_lo[:, j * S:(j + 1) * S], att[(PAIRS1 + j) % 2][:, 0:S], h_hi[:, j * S:(j + 1) * S].bitcast(F32), ALU.subtract)\
                    .then_inc(o_tiles, 1)

            pair_to_split(0)
            pair_to_split(1)

            def stick_pairs():
                pair_to_split(2)
                pair_to_split(3)

            softmax_heads(heads2, HEADS1, a2, lambda j: pair_to_split(PAIRS_SB + j), stick_pairs)

            ph = PH["att_o"]
            out = residual_units(ph, 0, 2)
            dve.wait_ge(ada_out, 12)
            for c in range(ph.n):
                lo(ph.chunk0 + c + 1)
                if c:
                    out(Step(c - 1))
                pieces(ph.name, Step(c))
            out(Step(ph.n - 1))
            units_done(dve, ph.unit0 + ph.units)
            gain(L0F)
            norm_h(L0F)

            def swiglu(ph, base):
                def one(step):
                    c = step.j
                    if c < ph.n:
                        lo(ph.chunk0 + c + 1, step if step.i is not None else None, ph)
                    if c >= 1:
                        bank = (ph.unit0 + c - 1) % 2
                        product(step, 1, base, lin[bank][:, S:2 * S]).then_inc(lin_free[bank], 1)
                        rest(step, 1, base)
                    if c < ph.n:
                        pieces(ph.name, step)

                steps(dve, ph.n, 2, 1, one)
                one(Step(ph.n))

            def down(ph, layer):
                out = residual_units(ph, layer, 5)
                dve.wait_ge(ada_out, ADA_PIECES * (layer + 1))
                steps(dve, ph.n, 4, 1, lambda s: down_step(ph, s, out))
                out(Step(ph.n - 1))

            swiglu(PH["gu0"], FT)
            down(PH["dn0"], 0)
            units_done(dve, PH["dn0"].unit0 + PH["dn0"].units)
            gain(L1)
            norm_h(L1)
            ph = PH["ret_in"]
            dve.wait_ge(tab3_in, 16)

            def ret_rotary(c):
                bank = v3(lin[(ph.unit0 + c) % 2][:, :], 2)
                to = v3(rt["q" if c < 4 else "k"][:, c % 4 * 512:c % 4 * 512 + 512], 2)
                rot = v3(rt["rot"], 2)
                dve.wait_ge(half_done, 2 * (ph.chunk0 + c + 1))
                link(tt(to, bank, over(rt["cos"], 2), ALU.mult))
                leave(tt(rot, bank, over(rt["sin"], 2), ALU.mult), ph.unit0 + c)
                dve.wait_ge(lin_free[(ph.unit0 + c) % 2], (ph.unit0 + c) // 2 + 1)
                tt(to[:, 0, :], to[:, 0, :], rot[:, 1, :], ALU.subtract)
                tt(to[:, 1, :], to[:, 1, :], rot[:, 0, :], ALU.add).then_inc(ret_rot, 1)

            def ret_decay(h):
                dve.wait_ge(ret_s, h + 1)
                tt(rt["inner"][:, h * 384:(h + 1) * 384], sco[h % 2][:, 0:384], rt["decay"][:, h * 384:(h + 1) * 384], ALU.mult)\
                    .then_inc(ret_inner, 1)

            def ret_centre(h):
                units_done(dve, ph.unit0 + 8 + 2 * h + 2)
                s4, mean = v_sums[:, 4 * h:4 * h + 4], v_sums[:, 16 + 2 * (h % 2):18 + 2 * (h % 2)]
                link(stt(mean, s4[:, 0:4:2], 1.0, s4[:, 1:4:2], ALU.mult, ALU.add))
                link(ts(mean, mean, 1.0 / RET_DV, None, ALU.mult))
                for r in range(2):
                    v = v3(rt["v"], 2)[:, r, h * RET_DV:(h + 1) * RET_DV]
                    ins = ts(v, v, mean[:, r:r + 1], None, ALU.subtract)
                ins.then_inc(v_centred, 1)

            def ret_rstd(h):
                st = ret_stat[:, 32 * (h % 2):32 * (h % 2) + 32]
                dve.wait_ge(ret_ssum, h + 1)
                ts(st[:, 0:2], ssum[:, 0:2], 1.0 / RET_DV, GN_EPS, ALU.mult, ALU.add).then_inc(ret_ms, 1)
                refine(ret_root, h + 1, st, 2)
                if h:
                    dve.wait_ge(ret_rbc, h)
                else:
                    dve.wait_ge(rbc_ready, L1 + 1)
                for r in range(2):
                    ts(diag[:, r * P:(r + 1) * P], ident[:, :], st[:, 24 + r:25 + r], -0.5, ALU.mult, ALU.mult).then_inc(ret_diag, 1)

            def ret_scale(h):
                dve.wait_ge(ret_rbc, h + 1)
                if h >= 2:
                    dve.wait_ge(ret_hh, 2 * (h - 1))
                link(nc.vector.tensor_copy(rt["rb"], ret_rbc_of(h)))
                for m in range(2):
                    dve.wait_ge(ret_o, 2 * h + m + 1)
                    t = rt["t"][:, D * (h % 2) + 512 * m:D * (h % 2) + 512 * m + 512]
                    ins = tt(v3(t, 2), v3(ret_bank(h)[m][:, :], 2), over(rt["rb"], 2), ALU.mult)
                ins.then_inc(ret_t, 1)

            def ret_gate(h):
                dve.wait_ge(ret_t, h + 1)
                t = rt["t"][:, D * (h % 2):D * (h % 2) + D]
                g = rt["g"][:, D * (h % 2):D * (h % 2) + D]
                for m in range(2):
                    units_done(dve, ph.unit0 + 16 + 2 * h + m + 1)
                    for f in (2 * m, 2 * m + 1):
                        cut = slice(f * S, (f + 1) * S)
                        ins = stt(t[:, cut], t[:, cut], col("gn", 4 * h + f), g[:, cut], ALU.mult, ALU.mult)
                    ins.then_inc(ret_y, 1)
                for m in range(2):
                    to = slice((4 * h + 2 * m) * S, (4 * h + 2 * m) * S + 512)
                    dve.wait_ge(ret_hh, 2 * h + m + 1)
                    tt(hid_lo[:, to], t[:, 512 * m:512 * m + 512], hid_hi[:, to].bitcast(F32), ALU.subtract).then_inc(ret_tiles, 2)

            for c in range(ph.n + 1):
                if c < ph.n:
                    lo(ph.chunk0 + c + 1)
                if 1 <= c <= 8:
                    ret_rotary(c - 1)
                if c in AT_DECAY:
                    ret_decay(AT_DECAY[c])
                if at_centre(c) is not None:
                    ret_centre(at_centre(c))
                if at_rstd(c) is not None:
                    ret_rstd(at_rstd(c))
                if c in AT_Y:
                    ret_gate(AT_Y[c])
                if c in AT_T:
                    ret_scale(AT_T[c])

            ph = PH["ret_o"]
            out = residual_units(ph, 1, 2)
            for c in range(ph.n):
                lo(ph.chunk0 + c + 1)
                if c:
                    out(Step(c - 1))
            out(Step(ph.n - 1))
            units_done(dve, ph.unit0 + ph.units)
            gain(L1F)
            norm_h(L1F)
            swiglu(PH["gu1"], 2 * FT)
            down(PH["dn1"], 1)
            units_done(dve, PH["dn1"].unit0 + PH["dn1"].units)
            rstd(FINAL)
            dve.wait_ge(rbc_ready, FINAL + 1)
            for k in range(DT):
                scale_tile(FINAL, k).then_inc(x_tiles, 1)


def tables():
    f32 = np.float32
    key, query = np.arange(P)[:, None], np.arange(P)[None, :]
    zero, full = np.zeros((P, P), f32), np.ones((P, P), f32)
    causal = np.where(query <= key, 0.0, NEG).astype(f32)
    mask = np.concatenate([causal, zero, causal], 1)
    earlier = (key < query).astype(f32)
    strict = np.concatenate([earlier, full, earlier], 1)
    strict_neg = np.where(strict > 0, 0.0, NEG).astype(f32)

    def rope(dim, repeat):
        inv = (f32(THETA) ** (-(np.arange(dim // 2, dtype=f32) * f32(2.0) / f32(dim)))).astype(f32)
        ang = np.arange(S, dtype=f32)[None, :] * inv[:, None]
        c, s = np.cos(ang.astype(np.float64)).astype(f32), np.sin(ang.astype(np.float64)).astype(f32)
        return np.tile(c, (repeat, 1)), np.tile(s, (repeat, 1))

    def swap(dim):
        m = np.zeros((P, P), f32)
        for o in range(P):
            half = dim // 2
            if o % dim < half:
                m[o + half, o] = -1.0
            else:
                m[o - half, o] = 1.0
        return m

    dist = 255 - np.arange(BAND)
    exact = BUCKETS // 2
    near = np.maximum(dist, 1).astype(f32) / f32(exact)
    ratio = np.log(near).astype(f32) / f32(math.log(MAX_DIST / exact))
    large = np.minimum(exact + (ratio * f32(BUCKETS - exact)).astype(np.int32), BUCKETS - 1)
    bucket = np.where(dist < exact, np.maximum(dist, 0), large)
    inside = (dist >= 0) & (dist < WINDOW)
    onehot = np.zeros((BUCKETS + 1, BAND), f32)
    onehot[:BUCKETS] = (np.arange(BUCKETS)[:, None] == bucket[None, :]) & inside[None, :]
    onehot[BUCKETS] = np.where(inside, 0.0, NEG)
    decay = []
    pos = np.arange(S)
    for h in range(RET_H):
        diff = pos[None, :] - pos[:, None]
        full_decay = np.where(diff >= 0, np.exp(math.log(1.0 - 2.0 ** (-5 - h)) * np.maximum(diff, 0)), 0.0)
        full_decay = (full_decay / 16.0).astype(f32)
        decay += [full_decay[:P, :], full_decay[P:, P:]]
    c1, s1 = rope(ROPE, 8)
    c2, s2 = rope(HD, 4)
    c3, s3 = rope(256, 1)
    return {
        "ident": np.eye(P, dtype=f32),
        "tab1": np.concatenate([mask, c1, s1, swap(ROPE)], 1),
        "onehot": onehot,
        "tab2": np.concatenate([mask, c2, s2, swap(HD), -(key >= query).astype(f32), -full, strict_neg], 1),
        "tab3": np.concatenate([c3, s3] + decay, 1),
    }


def lay_out(i):
    f32 = np.float32

    def chunks(w, width):
        k, n = w.shape
        a = w.reshape(k // P, P, n // width, width).transpose(2, 1, 0, 3)
        return np.ascontiguousarray(a).reshape(n // width * P, k // P * width)

    def blocks(w):
        k, n = w.shape
        a = w.reshape(k // P, P, n // 256, 2, P).transpose(2, 1, 3, 0, 4)
        return np.ascontiguousarray(a).reshape(n // 256 * P, k // P * 256)

    def mixed_chunks(name, w):
        return np.concatenate([(chunks(w[:, 256 * c:256 * c + 256], 256) if PH[name].row(c) else blocks(w[:, 256 * c:256 * c + 256]))
                               for c in range(w.shape[1] // 256)], 0)

    def pad(a, n):
        return np.concatenate([a, np.zeros(a.shape[:-1] + (n - a.shape[-1],), f32)], -1)

    def columns(v):
        return np.ascontiguousarray(v.reshape(-1, P).T)

    arrays = tables()
    arrays["cond"] = np.tile(i["c_2"][0], (P, 1))
    arrays["x"] = np.ascontiguousarray(i["x"][0].T.reshape(DT, P, S).transpose(1, 0, 2)).reshape(P, DT * S)
    order = np.concatenate([np.r_[j * HD:(j + 1) * HD, (4 + j) * HD:(5 + j) * HD] for j in range(4)])
    heads = np.array([n // 2 + 4 * (n % 2) for n in range(8)])
    w = i["w_in"][0]
    a, f, m = w[:, :768], w[:, 768:1540], w[:, 1540:]
    w_in = np.concatenate([m[:, :384], np.tile(m[:, 384:416], (1, 4)), a[:, order], f[:, :512], a[:, 512:640],
                           pad(f[:, 768:772], P), f[:, 512:768], pad(a[:, 640:768], 2 * P)], 1)
    last = chunks(w_in[:, -256:-128], P)
    arrays["w_in"] = np.concatenate([mixed_chunks("w_in", w_in[:, :-256]), pad(last, CHUNK)], 0)
    uq = i["w_uq"][0].reshape(256, 4, 96)
    uq = np.concatenate([uq[:, :, :64].reshape(256, 256), uq[:, :, 64:].reshape(256, 128)], 1)
    ukv = i["w_ukv"][0].reshape(128, 4, 2, 64).transpose(0, 2, 1, 3).reshape(128, 512)
    arrays["mla"] = np.concatenate([chunks(uq, 384), ukv], 1)
    mixed = np.concatenate([order, np.arange(512, 1024)])
    arrays["w_out"] = blocks(i["w_out"][0][mixed])

    def paired(w):
        k, n = w.shape
        return w.reshape(k, 2, FT, P).transpose(0, 2, 1, 3).reshape(k, n)

    def halves(w):
        a = w.reshape(2, HALF, P, DT, P).transpose(3, 0, 2, 1, 4)
        return np.ascontiguousarray(a).reshape(2 * DT * P, HALF * P)

    arrays["up"] = blocks(paired(i["w_up"][0]))
    arrays["down"] = halves(i["w_down"][0])
    at = [D * part + D // 2 * kind for kind in range(2) for part in range(2)]
    qkv = np.concatenate([i["att_w_qkv_2"][0][:, a:a + D // 2] for a in at] + [i["att_w_qkv_2"][0][:, 2 * D:]], 1)
    arrays["qkv"] = mixed_chunks("qkv", qkv)
    arrays["att_o"] = blocks(i["att_w_o_2"][0])
    arrays["ret_in"] = mixed_chunks("ret_in", i["ret_w_in_2"][0])
    arrays["ret_o"] = chunks(i["ret_w_o_2"][0], P)
    for n in range(2):
        arrays[f"gu{n}"] = blocks(paired(i["ffn_w_gate_up_2"][n]))
        arrays[f"dn{n}"] = halves(i["ffn_w_down_2"][n])
    arrays["ada"] = np.concatenate([np.ascontiguousarray(w.T).reshape(ADA_PIECES, 2, P, D).transpose(0, 2, 1, 3).reshape(-1, 2 * D)
                                    for w in i["ada_w_2"]], 0)

    def conv(v):
        return columns(paired(v[None, :])[0])

    def rows(v):
        return np.concatenate([v, np.zeros((P - v.shape[0], v.shape[1]), f32)], 0)

    rel = np.concatenate([i["rel_bias"][:, heads], np.ones((1, 8), f32)], 0)
    vectors = {
        "pre": columns(i["attn_pre_norm"][0]), "qlat": columns(i["q_latent_norm"][0]),
        "kvlat": columns(i["kv_latent_norm"][0]), "group": columns(i["group_norm"][0][mixed]),
        "post": columns(i["attn_post_norm"][0]), "ffnpre": columns(i["ffn_pre_norm"][0]),
        "conv_w": np.concatenate([conv(i["conv_w"][0, t]) for t in range(3)], 1), "conv_b": conv(i["conv_b"][0]),
        "ffnpost": columns(i["ffn_post_norm"][0]), "norms2": columns(i["norm_gains_2"]),
        "ada_b": columns(i["ada_b_2"]), "gn": columns(i["ret_gn_2"][0]), "final": columns(i["final_norm_2"]),
        "sinks": np.tile(i["swa_sinks"][0][heads], (P, 1)),
        "fbias": rows(i["forget_bias"][0][:, None]), "rel": rows(rel),
    }
    arrays["cols"] = np.concatenate([vectors[n].astype(f32) for n in COLS], 1)
    return {n: np.ascontiguousarray(a) for n, a in arrays.items()}


def program(nc, arrays):
    dram = {n: nc.dram_tensor(f"in_{n}", a.shape, F32, kind="ExternalInput").ap() for n, a in arrays.items()}
    dram["out"] = nc.dram_tensor("out_0", (P, DT * S), F32, kind="ExternalOutput").ap()
    band = nc.dram_tensor("band", (8, BAND), F32, kind="Internal")
    rows = nc.dram_tensor("band_rows", (P, 8 * BAND), F32, kind="Internal")
    dram["band"], dram["band_rows"] = band.ap(), rows.ap()
    dram["band_repeat"] = bass.AP(band, 0, [[0, P], [1, 8 * BAND]])
    dram["band_skew"] = bass.AP(rows, P - 1, [[8 * BAND - 1, P], [BAND, 8], [1, S]])
    build(nc, dram)


def kernel(**inputs):
    import concourse.bacc as bacc
    from concourse.bass_utils import run_bass_kernel_spmd

    arrays = lay_out({n: np.asarray(a) for n, a in inputs.items()})
    nc = bacc.Bacc("TRN2", target_bir_lowering=False, num_devices=1)
    program(nc, arrays)
    result = run_bass_kernel_spmd(nc, [{f"in_{n}": a for n, a in arrays.items()}], core_ids=[0]).results[0]["out_0"]
    return np.ascontiguousarray(result.reshape(P, DT, S).transpose(2, 1, 0)).reshape(1, S, D)
```
